# Optimizing a Trainium2 kernel written in Bass

```python
import functools
import jax, jax.numpy as jnp
from jax import lax
import numpy as np

D_MODEL = 1024
BATCH = 1
SEQ = 1024
DEPTH = 1
DEC_BATCH = 8
DEC_SEQ = 8
PAST_LEN = 8192
PAGE_SIZE = 128

HEAD_DIM = 64
N_HEADS_A = D_MODEL // 128
WIDTH_A = N_HEADS_A * HEAD_DIM
WIDTH_B = D_MODEL - WIDTH_A
MIX_WIDTH = WIDTH_A + WIDTH_B
DILATED_BRANCHES = ((128, 1), (512, 4), (2048, 16))
WIN_MAX = 2048
CONV_WIDTH = 31
D_FF = 2816
N_MEM = 256
N_HEADS_X = 4
HEAD_DIM_X = D_MODEL // N_HEADS_X
EPS = 1e-6

kernel_name = 'hybrid_dilated_conformer_decoder_step'

def rmsnorm(x, g):
    xf = x.astype(jnp.float32)
    y = xf * lax.rsqrt(jnp.mean(xf * xf, axis=-1, keepdims=True) + EPS)
    return (y * g.astype(jnp.float32)).astype(x.dtype)

def layernorm(x, g, b):
    xf = x.astype(jnp.float32)
    mu = jnp.mean(xf, axis=-1, keepdims=True)
    xc = xf - mu
    y = xc * lax.rsqrt(jnp.mean(xc * xc, axis=-1, keepdims=True) + EPS)
    return (y * g.astype(jnp.float32) + b.astype(jnp.float32)).astype(x.dtype)

def ffn_half_step(x, g, wg, wu, wd):
    h = rmsnorm(x, g)
    return x + 0.5 * ((jax.nn.silu(h @ wg) * (h @ wu)) @ wd)

def alibi_slopes(n):
    return 2.0 ** (-8.0 * jnp.arange(1, n + 1, dtype=jnp.float32) / n)

def project_in(h, w_in):
    B, T, _ = h.shape
    z = h @ w_in
    q, k, v, a, g = jnp.split(z, [WIDTH_A, 2 * WIDTH_A, 3 * WIDTH_A, 3 * WIDTH_A + WIDTH_B], axis=-1)
    heads = lambda t: t.reshape(B, T, N_HEADS_A, HEAD_DIM)
    return heads(q), heads(k), heads(v), a * jax.nn.sigmoid(g)

def conv_branch(u_ext, conv_w, conv_b, ln_g, ln_b):
    y = lax.conv_general_dilated(u_ext, conv_w[:, None, :], window_strides=(1,), padding='VALID',
                                 dimension_numbers=('NWC', 'WIO', 'NWC'),
                                 feature_group_count=u_ext.shape[-1])
    return jax.nn.silu(layernorm(y + conv_b, ln_g, ln_b))

def dilated_branch_prompt(q, k, v, slopes, window, dilation):
    B, S, H, Dh = q.shape
    w = window // dilation
    L = S // dilation
    nblk = -(-L // w)
    Lp = nblk * w
    split = lambda a: a.reshape(B, L, dilation, H, Dh)
    qb = jnp.pad(split(q), ((0, 0), (0, Lp - L), (0, 0), (0, 0), (0, 0))).reshape(B, nblk, w, dilation, H, Dh)
    kpad = ((0, 0), (w, Lp - L), (0, 0), (0, 0), (0, 0))
    ks = jnp.pad(split(k), kpad).reshape(B, nblk + 1, w, dilation, H, Dh)
    vs = jnp.pad(split(v), kpad).reshape(B, nblk + 1, w, dilation, H, Dh)
    kb = jnp.concatenate([ks[:, :-1], ks[:, 1:]], axis=2)
    vb = jnp.concatenate([vs[:, :-1], vs[:, 1:]], axis=2)
    s = jnp.einsum('bnqrhe,bnkrhe->bnrhqk', qb, kb).astype(jnp.float32) * (Dh ** -0.5)
    qi = jnp.arange(w)[:, None]
    kj = jnp.arange(2 * w)[None, :]
    dist = qi + w - kj
    blk = jnp.arange(nblk)[:, None, None]
    valid = (dist >= 0) & (dist <= w) & (blk * w + kj - w >= 0)
    bias = -slopes[:, None, None] * (dist * dilation).astype(jnp.float32)
    s = jnp.where(valid[None, :, None, None], s + bias, -jnp.inf)
    m = jnp.max(s, axis=-1)
    p = jnp.exp(s - m[..., None])
    den = jnp.sum(p, axis=-1)
    num = jnp.einsum('bnrhqk,bnkrhe->bnqrhe', p, vb.astype(jnp.float32))
    to_seq = lambda t: t.transpose(0, 1, 4, 2, 3).reshape(B, Lp, dilation, H)[:, :L].reshape(B, S, H)
    num = num.reshape(B, Lp, dilation, H, Dh)[:, :L].reshape(B, S, H, Dh)
    return to_seq(m), to_seq(den), num

def dilated_branch_sample(q, k_all, v_all, slopes, window, dilation):
    B, T, H, Dh = q.shape
    u0 = k_all.shape[1] - T
    w = window // dilation
    dist = jnp.arange(w + 1) * dilation
    u = u0 + jnp.arange(T)[:, None] - dist[None, :]
    valid = u >= 0
    uc = jnp.maximum(u, 0)
    kg = k_all[:, uc]
    vg = v_all[:, uc]
    s = jnp.einsum('bthe,btjhe->bthj', q, kg).astype(jnp.float32) * (Dh ** -0.5)
    s = s - slopes[:, None] * dist.astype(jnp.float32)[None, :]
    s = jnp.where(valid[None, :, None, :], s, -jnp.inf)
    m = jnp.max(s, axis=-1)
    p = jnp.exp(s - m[..., None])
    den = jnp.sum(p, axis=-1)
    num = jnp.einsum('bthj,btjhe->bthe', p, vg.astype(jnp.float32))
    return m, den, num

def merge_by_denominator(parts):
    m = functools.reduce(jnp.maximum, [pt[0] for pt in parts])
    scales = [jnp.exp(pt[0] - m) for pt in parts]
    den = functools.reduce(jnp.add, [sc * pt[1] for sc, pt in zip(scales, parts)])
    num = functools.reduce(jnp.add, [sc[..., None] * pt[2] for sc, pt in zip(scales, parts)])
    return num / den[..., None]

def mem_kv(mem, g, w_ck, w_cv):
    B = mem.shape[0]
    mn = rmsnorm(mem, g)
    return ((mn @ w_ck).reshape(B, N_MEM, N_HEADS_X, HEAD_DIM_X),
            (mn @ w_cv).reshape(B, N_MEM, N_HEADS_X, HEAD_DIM_X))

def cross_attend(h, mk, mv, w_cq, w_co):
    B, T, _ = h.shape
    q = (h @ w_cq).reshape(B, T, N_HEADS_X, HEAD_DIM_X)
    s = jnp.einsum('bthe,bmhe->bhtm', q, mk).astype(jnp.float32) * (HEAD_DIM_X ** -0.5)
    p = jax.nn.softmax(s, axis=-1)
    o = jnp.einsum('bhtm,bmhe->bthe', p, mv.astype(jnp.float32)).reshape(B, T, N_HEADS_X * HEAD_DIM_X)
    return o.astype(h.dtype) @ w_co

def setup_inputs(seed: int = 0) -> dict:
    key = jax.random.key(seed)
    ks = iter(jax.random.split(key, 48))
    nrm = lambda shape, scale: jax.random.normal(next(ks), shape, jnp.float32) * scale
    gain = lambda shape: 1.0 + nrm(shape, 0.02)
    w_buf = min(WIN_MAX, PAST_LEN)
    L = DEPTH
    return {
        'x_prompt': nrm((BATCH, SEQ, D_MODEL), 1.0),
        'x_sample': nrm((DEC_BATCH, DEC_SEQ, D_MODEL), 1.0),
        'mem_prompt': nrm((BATCH, N_MEM, D_MODEL), 1.0),
        'cache_win_k': nrm((L, DEC_BATCH, w_buf, N_HEADS_A, HEAD_DIM), 1.0),
        'cache_win_v': nrm((L, DEC_BATCH, w_buf, N_HEADS_A, HEAD_DIM), 1.0),
        'cache_conv': nrm((L, DEC_BATCH, CONV_WIDTH - 1, WIDTH_B), 0.5),
        'cache_mem_k': nrm((L, DEC_BATCH, N_MEM, N_HEADS_X, HEAD_DIM_X), 1.0),
        'cache_mem_v': nrm((L, DEC_BATCH, N_MEM, N_HEADS_X, HEAD_DIM_X), 1.0),
        'ffn1_norm': gain((L, D_MODEL)),
        'ffn1_gate': nrm((L, D_MODEL, D_FF), D_MODEL ** -0.5),
        'ffn1_up': nrm((L, D_MODEL, D_FF), D_MODEL ** -0.5),
        'ffn1_down': nrm((L, D_FF, D_MODEL), D_FF ** -0.5),
        'mix_norm': gain((L, D_MODEL)),
        'w_in': nrm((L, D_MODEL, 3 * WIDTH_A + 2 * WIDTH_B), D_MODEL ** -0.5),
        'conv_w': nrm((L, CONV_WIDTH, WIDTH_B), CONV_WIDTH ** -0.5),
        'conv_b': nrm((L, WIDTH_B), 0.02),
        'conv_ln_g': gain((L, WIDTH_B)),
        'conv_ln_b': nrm((L, WIDTH_B), 0.02),
        'w_out': nrm((L, MIX_WIDTH, D_MODEL), MIX_WIDTH ** -0.5),
        'xattn_norm': gain((L, D_MODEL)),
        'mem_norm': gain((L, D_MODEL)),
        'w_cq': nrm((L, D_MODEL, N_HEADS_X * HEAD_DIM_X), D_MODEL ** -0.5),
        'w_ck': nrm((L, D_MODEL, N_HEADS_X * HEAD_DIM_X), D_MODEL ** -0.5),
        'w_cv': nrm((L, D_MODEL, N_HEADS_X * HEAD_DIM_X), D_MODEL ** -0.5),
        'w_co': nrm((L, N_HEADS_X * HEAD_DIM_X, D_MODEL), (N_HEADS_X * HEAD_DIM_X) ** -0.5),
        'ffn2_norm': gain((L, D_MODEL)),
        'ffn2_gate': nrm((L, D_MODEL, D_FF), D_MODEL ** -0.5),
        'ffn2_up': nrm((L, D_MODEL, D_FF), D_MODEL ** -0.5),
        'ffn2_down': nrm((L, D_FF, D_MODEL), D_FF ** -0.5),
        'final_norm': gain((D_MODEL,)),
    }

def reference(x_prompt, x_sample, mem_prompt, cache_win_k, cache_win_v, cache_conv, cache_mem_k, cache_mem_v,
              ffn1_norm, ffn1_gate, ffn1_up, ffn1_down, mix_norm, w_in, conv_w, conv_b, conv_ln_g, conv_ln_b,
              w_out, xattn_norm, mem_norm, w_cq, w_ck, w_cv, w_co, ffn2_norm, ffn2_gate, ffn2_up, ffn2_down,
              final_norm):
    slopes = alibi_slopes(N_HEADS_A)
    yp, ys = x_prompt, x_sample
    Bp, S, _ = x_prompt.shape
    Bs, T, _ = x_sample.shape
    keep = min(WIN_MAX, S)
    pk, pv, pc, pmk, pmv, sk, sv, sc = [], [], [], [], [], [], [], []
    for l in range(DEPTH):
        yp = ffn_half_step(yp, ffn1_norm[l], ffn1_gate[l], ffn1_up[l], ffn1_down[l])
        q, k, v, u = project_in(rmsnorm(yp, mix_norm[l]), w_in[l])
        o_a = merge_by_denominator([dilated_branch_prompt(q, k, v, slopes, wdw, dil)
                                    for (wdw, dil) in DILATED_BRANCHES])
        u_ext = jnp.pad(u, ((0, 0), (CONV_WIDTH - 1, 0), (0, 0)))
        o_b = conv_branch(u_ext, conv_w[l], conv_b[l], conv_ln_g[l], conv_ln_b[l])
        yp = yp + jnp.concatenate([o_a.reshape(Bp, S, WIDTH_A).astype(yp.dtype), o_b], axis=-1) @ w_out[l]
        mk, mv = mem_kv(mem_prompt, mem_norm[l], w_ck[l], w_cv[l])
        yp = yp + cross_attend(rmsnorm(yp, xattn_norm[l]), mk, mv, w_cq[l], w_co[l])
        yp = ffn_half_step(yp, ffn2_norm[l], ffn2_gate[l], ffn2_up[l], ffn2_down[l])
        pk.append(k[:, S - keep:])
        pv.append(v[:, S - keep:])
        pc.append(u[:, S - (CONV_WIDTH - 1):])
        pmk.append(mk)
        pmv.append(mv)
        ys = ffn_half_step(ys, ffn1_norm[l], ffn1_gate[l], ffn1_up[l], ffn1_down[l])
        q, k, v, u = project_in(rmsnorm(ys, mix_norm[l]), w_in[l])
        k_all = jnp.concatenate([cache_win_k[l].astype(k.dtype), k], axis=1)
        v_all = jnp.concatenate([cache_win_v[l].astype(v.dtype), v], axis=1)
        o_a = merge_by_denominator([dilated_branch_sample(q, k_all, v_all, slopes, wdw, dil)
                                    for (wdw, dil) in DILATED_BRANCHES])
        u_ext = jnp.concatenate([cache_conv[l].astype(u.dtype), u], axis=1)
        o_b = conv_branch(u_ext, conv_w[l], conv_b[l], conv_ln_g[l], conv_ln_b[l])
        ys = ys + jnp.concatenate([o_a.reshape(Bs, T, WIDTH_A).astype(ys.dtype), o_b], axis=-1) @ w_out[l]
        ys = ys + cross_attend(rmsnorm(ys, xattn_norm[l]), cache_mem_k[l], cache_mem_v[l], w_cq[l], w_co[l])
        ys = ffn_half_step(ys, ffn2_norm[l], ffn2_gate[l], ffn2_up[l], ffn2_down[l])
        sk.append(k)
        sv.append(v)
        sc.append(u_ext[:, u_ext.shape[1] - (CONV_WIDTH - 1):])
    y_prompt = rmsnorm(yp, final_norm)
    y_sample = rmsnorm(ys, final_norm)
    return (y_prompt, y_sample, jnp.stack(pk), jnp.stack(pv), jnp.stack(pc), jnp.stack(pmk), jnp.stack(pmv),
            jnp.stack(sk), jnp.stack(sv), jnp.stack(sc))


_drawn_inputs = setup_inputs


def setup_inputs(seed=0):
    import zlib

    import numpy as np

    out = dict(_drawn_inputs(seed))
    spreads = {}
    factors = {'ffn1_norm': 6.81,
     'mix_norm': 2.694,
     'conv_b': 3.682,
     'conv_ln_g': 50.52,
     'conv_ln_b': 59.304,
     'xattn_norm': 23.089,
     'mem_norm': 8.644,
     'ffn2_norm': 26.368,
     'final_norm': 25.104,
     'cache_win_k': 2.756,
     'cache_win_v': 3.339}
    for name, (base, spread) in spreads.items():
        noise = np.random.default_rng([zlib.crc32(name.encode()), seed]).standard_normal(out[name].shape)
        drawn = base * np.exp(spread * noise) if base else spread * noise
        out[name] = __import__('jax').numpy.asarray(drawn.astype(out[name].dtype))
    for name, factor in factors.items():
        out[name] = (out[name] * factor).astype(out[name].dtype)
    return out
```

```python
from collections import defaultdict
from contextlib import ExitStack

import concourse.bass as bass
import numpy as np
from concourse import mybir

F32 = mybir.dt.float32
F32R = mybir.dt.float32r
ALU = mybir.AluOpType
ACT = mybir.ActivationFunctionType
AX = mybir.AxisListType

P = 128
D = 1024
KT = D // P
SEQ, NB, TS = 1024, 8, 8
TSAMP = NB * TS
T = SEQ + TSAMP
CHUNKS = [(0, 384), (384, 384), (768, T - 768)]
NC = len(CHUNKS)
DFF = 2816
FG = DFF // (2 * P)
H, HD = 8, 64
WA = H * HD
CT = WA // P
CONVW = 31
PAD = CONVW - 1
NMEM, HX, HDX = 256, 4, 256
EPS = 1e-6
WBUF = 2048
OLD = WBUF - 512
OG, ORS = OLD // 16, 8
RR = 4
NKEY = OG * ORS + 512 + TS
NEG = -1.0e30
QT = SEQ // P
SLOTS = 4


def log_multiplicity(d):
    c = ((d <= 128).astype(np.float64) + ((d <= 512) & (d % 4 == 0)) + ((d <= 2048) & (d % 16 == 0))) * (d >= 0)
    return np.where(c > 0, np.log(np.maximum(c, 1.0)), NEG)


def prompt_bias():
    d = np.arange(P)[:, None] + (SEQ - P) - np.arange(SEQ)[None, :]
    slopes = 2.0 ** -(np.arange(H) + 1.0)
    b = 8.0 * (log_multiplicity(d)[None] - slopes[:, None, None] * d[None])
    return np.where(d[None] < 0, NEG, np.maximum(b, NEG)).astype(np.float32)


def sample_bias():
    old = np.arange(OG)[None, :] * 16 + np.arange(ORS)[:, None]
    recent = OLD + np.arange(P)[None, :] * RR + np.arange(RR)[:, None]
    pos = np.concatenate([old.ravel(), recent.ravel(), WBUF + np.arange(TS)])
    d = WBUF + np.arange(TS)[:, None] - pos[None, :]
    slopes = 2.0 ** -(np.arange(H) + 1.0)
    b = 8.0 * (log_multiplicity(d)[None] - slopes[:, None, None] * d[None])
    b = np.where(d[None] < 0, NEG, np.maximum(b, NEG)).reshape(H * TS, NKEY)
    return np.concatenate([b, b]).astype(np.float32)


def decoder_layer(nc, I, O):
    ctx = ExitStack()

    def sem(name):
        return ctx.enter_context(nc.semaphore(name))

    def alloc(stack, name, shape, dt=F32):
        return stack.enter_context(nc.sbuf_tensor(name, shape, dt))

    z = nc.dram_tensor("z_scratch", (20 * P, T), F32).ap()
    zx = nc.dram_tensor("zx_scratch", (KT * P, T), F32).ap()
    mix = nc.dram_tensor("mix_scratch", (KT * P, T), F32).ap()
    mixx = nc.dram_tensor("mixx_scratch", (KT * P, T), F32).ap()
    mkT = nc.dram_tensor("mkT_scratch", (KT * P, NMEM), F32).ap()

    x = alloc(ctx, "x", [P, KT, T])
    raw = alloc(ctx, "raw", [P, 2, KT, P])
    wh = alloc(ctx, "wh", [P, SLOTS, KT, P], F32R)
    wl = alloc(ctx, "wl", [P, SLOTS, KT, P], F32R)
    ident = alloc(ctx, "ident", [P, P])
    ones = alloc(ctx, "ones", [P, P])
    vecs = alloc(ctx, "vecs", [P, 60])
    taps = alloc(ctx, "taps", [P, CT, CONVW])
    G_FFN1, G_MIX, G_X, G_MEM, G_FFN2, G_FIN = (8 * j for j in range(6))
    V_CB, V_LG, V_LB = 48, 52, 56

    with ExitStack() as g:
        hh = alloc(g, "hh", [P, KT, T], F32R)
        hl = alloc(g, "hl", [P, KT, T], F32R)
        sq = alloc(g, "sq", [P, 4, 384])
        tb = alloc(g, "tb", [P, 3, 384])
        rs = alloc(g, "rs", [P, NC, 384])
        bh = alloc(g, "bh", [P, 2, KT, P], F32R)
        bl = alloc(g, "bl", [P, 2, KT, P], F32R)
        with ExitStack() as f:
            hidh = alloc(f, "hidh", [P, 2, T], F32R)
            hidl = alloc(f, "hidl", [P, 2, T], F32R)
            sg = alloc(f, "sg", [P, 2, 384])
            ht = alloc(f, "ht", [P, 2, 384])
        with ExitStack() as f:
            xin = alloc(f, "xin", [P, 3, D])
            small = alloc(f, "small", [60, P])
            taps_in = alloc(f, "taps_in", [CONVW, WA])
        with ExitStack() as f:
            stage = alloc(f, "stage", [P, SLOTS, T])
        with ExitStack() as f:
            mixin = alloc(f, "mixin", [P, 3, T])
        with ExitStack() as f:
            ytok = alloc(f, "ytok", [P, 2, D])
    with ExitStack() as g:
        min_ = alloc(g, "min_", [P, 2, D])
        memT = alloc(g, "memT", [P, KT, NMEM])
        mh = alloc(g, "mh", [P, KT, NMEM], F32R)
        ml = alloc(g, "ml", [P, KT, NMEM], F32R)
        msq = alloc(g, "msq", [P, 4, 384])
        mtb = alloc(g, "mtb", [P, 3, 384])
        mrs = alloc(g, "mrs", [P, 1, 384])
        kvT = alloc(g, "kvT", [P, KT, NMEM])
        kvtok = alloc(g, "kvtok", [P, 2, D])
        az = alloc(g, "az", [P, T])
        gz = alloc(g, "gz", [P, T])
        U = alloc(g, "U", [P, CT, PAD + SEQ])
        Us = alloc(g, "Us", [P, CT, NB, PAD + TS])
        ya = alloc(g, "ya", [P, CT, T])
        cc_in = alloc(g, "cc_in", [4 * PAD, 2, WA])
        cct = alloc(g, "cct", [P, CT, 2, 4 * PAD])
        ucs = alloc(g, "ucs", [4 * PAD, 3, WA])
        mu = alloc(g, "mu", [P, 384])
    with ExitStack() as g:
        qT = alloc(g, "qT", [P, SEQ])
        kTp = alloc(g, "kTp", [P, SEQ])
        vT = alloc(g, "vT", [P, SEQ])
        pb = alloc(g, "pb", [P, 2, SEQ])
        Sb = alloc(g, "Sb", [P, 3, SEQ])
        PT = alloc(g, "PT", [P, 2, QT, P])
        vtok = alloc(g, "vtok", [P, QT, P])
        ktok = alloc(g, "ktok", [P, QT, P])
        oT = alloc(g, "oT", [P, SEQ])
        stat = alloc(g, "stat", [P, 4, 4])
        ks = alloc(g, "ks", [P, 2, CT, TSAMP])
        kvs = alloc(g, "kvs", [TSAMP, 2, WA])
    with ExitStack() as g:
        Ko = alloc(g, "Ko", [OG, 2, ORS, WA])
        Kr = alloc(g, "Kr", [P, 2, RR, WA])
        Vo = alloc(g, "Vo", [OG, 2, ORS, WA])
        Vr = alloc(g, "Vr", [P, 2, RR, WA])
        Vn = alloc(g, "Vn", [TS, 2, WA])
        Kc = alloc(g, "Kc", [P, CT, 512])
        Qc = alloc(g, "Qc", [P, 2, CT, H * TS])
        Qin = alloc(g, "Qin", [P, CT, 2 * TS])
        Knc = alloc(g, "Knc", [P, CT, 2 * TS])
        sbias = alloc(g, "sbias", [P, NKEY])
        Ss = alloc(g, "Ss", [P, NKEY])
        PTs = alloc(g, "PTs", [P, 13, P])
        sstat = alloc(g, "sstat", [P, 8])
        oS = alloc(g, "oS", [P, CT, NB, TS])
    with ExitStack() as g:
        xq = alloc(g, "xq", [P, 2, SEQ])
        xk = alloc(g, "xk", [P, 2, NMEM])
        xv = alloc(g, "xv", [P, 2, HDX])
        Xb = alloc(g, "Xb", [P, 3, NMEM])
        XT = alloc(g, "XT", [P, 2, 2, P])
        xo = alloc(g, "xo", [P, 2, SEQ])
        xstat = alloc(g, "xstat", [P, 4, 4])
        cq = alloc(g, "cq", [P, KT, TSAMP])
        cqc = alloc(g, "cqc", [P, 4, KT, HX * TS])
        cK = alloc(g, "cK", [P, 2, 2, D])
        cV = alloc(g, "cV", [P, 4, 2, D])
        cKT = alloc(g, "cKT", [P, KT, NMEM])
        cS = alloc(g, "cS", [P, NMEM])
        cPT = alloc(g, "cPT", [P, 2, P])
        cstat = alloc(g, "cstat", [P, 4])
        co = alloc(g, "co", [P, KT, NB, TS])

    ps = ctx.enter_context(nc.psum_tensor("ps", [P, 8, 512], F32))

    setup_done = sem("setup_done")
    raw_full = [sem("raw_full0"), sem("raw_full1")]
    w_hi = sem("w_hi")
    w_split = sem("w_split")
    unit_done = sem("unit_done")
    row_done = sem("row_done")
    met = sem("met")
    phase_end = sem("phase_end")

    OUT = O
    W = {n: I[n].rearrange("o (k p) n -> p (o k) n", p=P) for n in
         ("ffn1_gate", "ffn1_up", "ffn2_gate", "ffn2_up", "w_in", "w_out", "w_cq", "w_ck", "w_cv", "w_co")}
    DOWN = {n: I[n].rearrange("o f n -> (o f) n") for n in ("ffn1_down", "ffn2_down")}

    plan = [("ffn1", 6 * FG), ("w_in", 20), ("w_ck", 8), ("w_cv", 8), ("w_out", 8), ("w_cq", 8), ("w_co", 8),
            ("ffn2", 6 * FG)]
    UNIT, COL, ROW = {}, {}, {}
    u = c = r = 0
    for n, k in plan:
        UNIT[n], COL[n], ROW[n] = u, c, r
        u += k
        c += 4 * FG if n.startswith("ffn") else k
        r += 2 * FG if n.startswith("ffn") else 0

    class Sems:
        def __init__(self, tag, shared=None, base=None):
            self.tag, self.made, self.base = tag, {} if shared is None else shared, defaultdict(int, base or {})

        def __getitem__(self, n):
            if n not in self.made:
                self.made[n] = sem(f"{self.tag}_{n}")
            return self.made[n]

    S = {n: Sems(n) for n in ("mk", "conv", "pa", "sa", "xa", "xs")}

    def of_norm(nc_, split=True):
        return {"sqa": 4 * nc_, "sqd": 4 * nc_, "summed": KT * nc_, "var": nc_, "std": nc_, "rstd": nc_,
                "t": KT * nc_ * split, "hi": KT * nc_ * split, "h": KT * nc_}

    def of_proj(n, stored):
        return {"part": 2 * n, "free": 3 * n} | {f"st{w}": 16 * (n // 4) * stored for w in range(4)}

    of_split = {"hi": KT, "h": KT, "in0": 48, "in1": 48, "in2": 32}
    of_ffn = {"gate": 4 * FG, "up": 4 * FG, "prod": 6 * FG, "res": NC * KT * FG, "sg": 6 * FG, "hhi": 6 * FG,
              "hid": 6 * FG, "down": (NC * KT - 1) * FG}
    shared, base = {}, defaultdict(int)
    for n, adds in (("load", {"in0": 48, "in1": 48, "in2": 48, "xt": 2 * (QT + 1)}), ("n1", of_norm(NC) | of_ffn),
                    ("nm", of_norm(NC) | of_proj(20, 1)), ("mem", of_norm(1)), ("so", of_split | of_proj(8, 0)),
                    ("nx", of_norm(NC) | of_proj(8, 1)), ("sc", of_split | of_proj(8, 0)),
                    ("n2", of_norm(NC) | of_ffn), ("fin", of_norm(NC, False))):
        S[n] = Sems("g", shared, base)
        for name, v in adds.items():
            base[name] += v
    block = ctx.enter_context(nc.Block())
    x_tok = I["x_prompt"].rearrange("b t d -> (b t) d")
    xs_tok = I["x_sample"].rearrange("b t d -> (b t) d")
    mem_tok = I["mem_prompt"].rearrange("b (t p) d -> p (b t) d", p=P)
    rows = [("ffn1_norm", G_FFN1, 8), ("mix_norm", G_MIX, 8), ("xattn_norm", G_X, 8), ("mem_norm", G_MEM, 8),
            ("ffn2_norm", G_FFN2, 8), ("final_norm", G_FIN, 8), ("conv_b", V_CB, 4), ("conv_ln_g", V_LG, 4),
            ("conv_ln_b", V_LB, 4)]
    cache_conv = I["cache_conv"].rearrange("o (a b) t c -> (b t) (o a) c", b=4)
    new_conv_s = OUT["new_conv_sample"].rearrange("o (a b) t c -> (b t) (o a) c", b=4)
    new_conv_p = OUT["new_conv_prompt"].rearrange("o b t c -> (o b t) c")
    win_p = {n: OUT[f"new_win_{n}_prompt"].rearrange("o b (t p) h e -> p (o b t) (h e)", p=P) for n in "kv"}
    win_s = {n: OUT[f"new_win_{n}_sample"].rearrange("o b t h e -> (o b t) (h e)") for n in "kv"}
    mem_o = {n: OUT[f"new_mem_{n}_prompt"].rearrange("o b (t p) h e -> p (o b t) (h e)", p=P) for n in "kv"}
    win_c = {n: I[f"cache_win_{n}"].rearrange("o b w h e -> (o b) w (h e)") for n in "kv"}
    mem_c = {n: I[f"cache_mem_{n}"].rearrange("o b (p j) h e -> (o b) p j (h e)", j=2) for n in "kv"}

    def sq_slot(k):
        return 2 * (k % 2) + k // 2 % 2

    def barrier(eng, n):
        eng.drain().then_inc(phase_end, 1)
        eng.wait_ge(phase_end, 3 * n)

    @block.sync
    def _(sp):
        def load_unit(parity, split_needed, src, dst=None):
            sp.wait_ge(w_split, split_needed)
            sp.dma_start(raw[:, parity] if dst is None else dst, src).then_inc(raw_full[parity], 16)

        def ffn_loads(name):
            u0 = UNIT[name]
            gate, up, down = W[f"{name}_gate"], W[f"{name}_up"], DOWN[f"{name}_down"]
            with sp.Fori(0, FG) as i:
                for j in range(6):
                    if j < 4:
                        src = (gate, up)[j % 2][:, :, bass.ds(i * (2 * P) + (j // 2) * P, P)]
                        dst = None
                    else:
                        src = down[bass.ds(i * (2 * P) + (j - 4) * P, P), :]
                        dst = raw[:, j % 2].rearrange("p k n -> p (k n)")
                    load_unit(j % 2, i * 6 + (u0 + j + 1), src, dst)

        def col_loads(name):
            u0 = UNIT[name]
            n = (UNIT["ffn2"] if name == "w_co" else UNIT[plan[[p[0] for p in plan].index(name) + 1][0]]) - u0
            with sp.Fori(0, n // 4) as i:
                for j in range(4):
                    load_unit(j % 2, i * 4 + (u0 + j + 1), W[name][:, :, bass.ds(i * (4 * P) + j * P, P)])

        L = S["load"]
        for name, c0, n in rows:
            v = I[name]
            v = v.rearrange("(k p) -> k p", p=P) if name == "final_norm" else v.rearrange("o (k p) -> (o k) p", p=P)
            sp.dma_start(small[c0:c0 + n, :], v).then_inc(L["small"], 16)
        sp.dma_start(taps_in[:], I["conv_w"].rearrange("o t c -> (o t) c")).then_inc(L["small"], 16)
        for t in range(QT + 1):
            if t >= 3:
                sp.wait_ge(L["xin_free"], L.base["xin_free"] + 2 * (t - 2))
            n = P if t < QT else TSAMP
            src = x_tok[t * P:t * P + n, :] if t < QT else xs_tok
            sp.dma_start(xin[0:n, t % 3, :], src).then_inc(L[f"in{t % 3}"], 16)
        ffn_loads("ffn1")
        col_loads("w_in")
        C = S["conv"]
        sp.wait_ge(phase_end, 3 * 3)
        sp.dma_start(min_[:], mem_tok).then_inc(S["mem"]["in"], 16)
        sp.dma_start(cc_in[:], cache_conv).then_inc(C["cc_in"], 16)
        for k in range(CT):
            if k >= 1:
                sp.wait_ge(C["glu"], 2 * k)
            sp.dma_start(az[:], z[(12 + k) * P:(13 + k) * P, :]).then_inc(C["az"], 16)
            sp.dma_start(gz[:], z[(16 + k) * P:(17 + k) * P, :]).then_inc(C["gz"], 16)
        col_loads("w_ck")
        col_loads("w_cv")
        A = S["pa"]
        sp.wait_ge(phase_end, 3 * 4)
        for a in range(2):
            sp.dma_start(ks[:, a], z[(1 + a) * CT * P:(2 + a) * CT * P, SEQ:T].rearrange("(k p) t -> p k t", p=P)
                         ).then_inc(A["tok_in"], 16)
        with sp.Fori(0, H // 2) as i:
            sp.wait_ge(A["s_full"], i * (2 * QT) + 1)
            sp.dma_start(vT[:], z[bass.ds(i * P + 8 * P, P), 0:SEQ]).then_inc(A["in"], 16)
            sp.dma_start(kTp[:], z[bass.ds(i * P + 4 * P, P), 0:SEQ]).then_inc(A["in"], 16)
            sp.dma_start(qT[:], z[bass.ds(i * P, P), 0:SEQ]).then_inc(A["in"], 16)
            sp.wait_ge(A["s_free"], i * (2 * QT) + 2)
            sp.dma_start(pb[:], I["prompt_bias"][bass.ds(i * 2, 2), :, :].rearrange("h p n -> p h n")
                         ).then_inc(A["in"], 16)
        B = S["sa"]
        sp.wait_ge(phase_end, 3 * 5)
        sp.dma_start(sbias[:], I["sample_bias"]).then_inc(B["bias"], 16)

        def rows_of(n, b):
            c = win_c[n][bass.ds(b, 1), :, :].rearrange("b w e -> (b w) e")
            old = c[0:OLD, :].rearrange("(g s) e -> g s e", s=16)[:, 0:ORS, :]
            return old, c[OLD:WBUF, :].rearrange("(p r) e -> p r e", r=RR)

        with sp.Fori(0, NB // 2) as i:
            for b in range(2):
                old, recent = rows_of("k", i * 2 + b)
                sp.wait_ge(B["s_full"], i * 2 + (b + 1))
                sp.dma_start(Ko[:, b], old).then_inc(B[f"k{b}"], 16)
                sp.dma_start(Kr[:, b], recent).then_inc(B[f"k{b}"], 16)
            sp.wait_ge(B["s_full"], i * 2 + 2)
            for dst, r0 in ((Qin, 0), (Knc, CT)):
                sp.dma_start(dst[:], z[r0 * P:(r0 + CT) * P, bass.ds(i * (2 * TS) + SEQ, 2 * TS)
                                       ].rearrange("(k p) t -> p k t", p=P)).then_inc(B["qk_in"], 16)
            for b in range(2):
                old, recent = rows_of("v", i * 2 + b)
                sp.wait_ge(B["v_used"], i * 2 + (b + 1))
                sp.dma_start(Vo[:, b], old).then_inc(B[f"v{b}"], 16)
                sp.dma_start(Vr[:, b], recent).then_inc(B[f"v{b}"], 16)
            sp.dma_start(Vn[:], win_s["v"][bass.ds(i * (2 * TS), 2 * TS), :].rearrange("(b t) e -> t b e", b=2)
                         ).then_inc(B["vn"], 16)
        M = S["so"]
        sp.wait_ge(phase_end, 3 * 6)
        for k in range(KT):
            if k >= 3:
                sp.wait_ge(M["h"], M.base["h"] + k - 2)
            sp.dma_start(mixin[:, k % 3], mix[k * P:(k + 1) * P, :]).then_inc(M[f"in{k % 3}"], 16)
        col_loads("w_out")
        col_loads("w_cq")
        X = S["xa"]
        sp.wait_ge(phase_end, 3 * 8)
        with sp.Fori(0, HX) as i:
            sp.wait_ge(X["o_full"], i * QT + 1)
            sp.dma_start(xq[:], zx[bass.ds(i * HDX, HDX), 0:SEQ].rearrange("(k p) t -> p k t", p=P)
                         ).then_inc(X["in"], 16)
            sp.dma_start(xk[:], mkT[bass.ds(i * HDX, HDX), :].rearrange("(k p) t -> p k t", p=P)
                         ).then_inc(X["in"], 16)
            sp.dma_start(xv[:], mem_o["v"][:, :, bass.ds(i * HDX, HDX)]).then_inc(X["in"], 16)
        Y = S["xs"]
        sp.dma_start(cq[:], zx[:, SEQ:T].rearrange("(k p) t -> p k t", p=P)).then_inc(Y["q_in"], 16)
        with sp.Fori(0, 2) as i:
            for b in range(4):
                sp.wait_ge(Y["s_full"], i * 4 + (b + 1))
                sp.dma_start(cK[:, b % 2], mem_c["k"][bass.ds(i * 4 + b, 1)].rearrange("b p j e -> p (b j) e")
                             ).then_inc(Y[f"k{b % 2}"], 16)
            sp.wait_ge(Y["o_full"], i + 1)
            sp.dma_start(cV[:].rearrange("p b j e -> p b (j e)"),
                         mem_c["v"][bass.ds(i * 4, 4)].rearrange("b p j e -> p b (j e)")).then_inc(Y["v"], 16)
        M = S["sc"]
        sp.wait_ge(phase_end, 3 * 9)
        for k in range(KT):
            if k >= 3:
                sp.wait_ge(M["h"], M.base["h"] + k - 2)
            sp.dma_start(mixin[:, k % 3], mixx[k * P:(k + 1) * P, :]).then_inc(M[f"in{k % 3}"], 16)
        col_loads("w_co")
        ffn_loads("ffn2")
        F = S["fin"]
        yp = OUT["y_prompt"].rearrange("b t d -> (b t) d")
        for t in range(QT + 1):
            n = P if t < QT else TSAMP
            sp.wait_ge(F["tok"], F.base["tok"] + 2 * (t + 1))
            dst = yp[t * P:t * P + n, :] if t < QT else OUT["y_sample"].rearrange("b t d -> (b t) d")
            sp.dma_start(dst, ytok[0:n, t % 2, :]).then_inc(F[f"out{t % 2}"], 16)
        sp.wait_ge(F["out0"], F.base["out0"] + 16 * ((QT + 2) // 2))
        sp.wait_ge(F["out1"], F.base["out1"] + 16 * ((QT + 1) // 2))

    @block.gpsimd
    def _(pool):
        pool.memset(ident[:], 0.0).then_inc(setup_done, 1)
        pool.memset(ones[:], 1.0).then_inc(setup_done, 1)
        pool.wait_ge(setup_done, 1)
        pool.affine_select(out=ident[:], in_=ident[:], compare_op=ALU.not_equal, fill=1.0, base=0,
                           pattern=[[-1, P]], channel_multiplier=1).then_inc(setup_done, 1)
        pool.sem_inc(w_split, 2)

        def split(parity, full, m, hi, lo, slot_sem, slot_need):
            pool.wait_ge(raw_full[parity], full)
            pool.wait_ge(slot_sem, slot_need)
            pool.sem_inc(met, 1)
            pool.tensor_copy(hi, raw[:, parity]).then_inc(w_hi, 1)
            pool.wait_ge(w_hi, m + 1)
            pool.tensor_tensor(lo, raw[:, parity], hi.bitcast(F32), ALU.subtract).then_inc(w_split, 1)

        def ffn_split(name):
            u0, c0, r0 = UNIT[name], COL[name], ROW[name]
            with pool.Fori(0, FG) as i:
                for j in range(6):
                    full = i * 48 + 16 * ((u0 + j) // 2 + 1)
                    if j < 4:
                        split(j % 2, full, i * 6 + (u0 + j), wh[:, j], wl[:, j], unit_done, i * 4 + (c0 + j + 1))
                    else:
                        split(j % 2, full, i * 6 + (u0 + j), bh[:, j - 4], bl[:, j - 4], row_done,
                              i * 2 + (r0 + j - 4 + 1))

        def col_split(name, n):
            u0, c0 = UNIT[name], COL[name]
            with pool.Fori(0, n // 4) as i:
                for j in range(4):
                    split(j % 2, i * 32 + 16 * ((u0 + j) // 2 + 1), i * 4 + (u0 + j), wh[:, j], wl[:, j],
                          unit_done, i * 4 + (c0 + j + 1))

        for name, n in plan:
            if name.startswith("ffn"):
                if name == "ffn2":
                    pool.wait_ge(phase_end, 3 * 9)
                ffn_split(name)
            else:
                col_split(name, n)

    @block.tensor
    def _(pe):
        pe.sem_inc(unit_done, SLOTS)
        pe.sem_inc(row_done, 2)
        pe.wait_ge(setup_done, 3)

        def three(out, w_hi_, w_lo_, a_hi, a_lo, first, last):
            pe.matmul(out, w_hi_, a_hi, start=first, stop=False)
            pe.matmul(out, w_lo_, a_hi, start=False, stop=False)
            return pe.matmul(out, w_hi_, a_lo, start=False, stop=last)

        def norm(s, chunks, sqt):
            for c, (c0, n) in enumerate(chunks):
                for k in range(KT):
                    pe.wait_ge(s[("sqa", "sqd")[k % 2]], s.base[("sqa", "sqd")[k % 2]] + c * (KT // 2) + k // 2 + 1)
                    pe.matmul(ps[:, 5 + c, 0:n], ones[:], sqt[:, sq_slot(k), 0:n], start=(k == 0),
                              stop=(k == KT - 1)).then_inc(s["summed"], 1)

        def ffn(name, s):
            u0, c0_, r0 = UNIT[name], COL[name], ROW[name]
            with pe.Fori(0, FG) as i:
                for f in range(2):
                    for c, (c0, n) in enumerate(CHUNKS):
                        j = NC * f + c
                        if f == 0:
                            pe.wait_ge(s["h"], s.base["h"] + KT * (c + 1))
                        pe.wait_ge(s["prod"], s.base["prod"] + i * 6 + (j + 1))
                        for gu in range(2):
                            if c == 0:
                                pe.wait_ge(w_split, i * 6 + (u0 + 2 * f + gu + 3))
                            out = ps[:, 2 * (j % 2) + gu, 0:n]
                            w = 2 * f + gu
                            for k in range(KT):
                                mm = three(out, wh[:, w, k], wl[:, w, k], hh[:, k, c0:c0 + n], hl[:, k, c0:c0 + n],
                                           k == 0, k == KT - 1)
                            if c < NC - 1:
                                mm.then_inc(s[("gate", "up")[gu]], 1)
                            else:
                                mm.then_inc(unit_done, 1)
                pe.wait_ge(w_split, i * 6 + (u0 + 8))
                for c, (c0, n) in enumerate(CHUNKS):
                    pe.wait_ge(s["hid"], s.base["hid"] + i * 6 + (NC + c + 2))
                    for d in range(KT):
                        j = c * KT + d
                        pe.wait_ge(s["res"], s.base["res"] + i * (NC * KT) + (j + 1))
                        out = ps[:, 4 + j % 4, 0:n]
                        for f in range(2):
                            mm = three(out, bh[:, f, d], bl[:, f, d], hidh[:, f, c0:c0 + n], hidl[:, f, c0:c0 + n],
                                       f == 0, f == 1)
                        if j < NC * KT - 1:
                            mm.then_inc(s["down"], 1)
                        else:
                            mm.then_inc(row_done, 2)

        def proj(name, s, nunits, chunks, ah, al, h_need):
            u0 = UNIT[name]
            nc_ = len(chunks)
            with pe.Fori(0, nunits // 4) as i:
                for w in range(4):
                    pe.wait_ge(w_split, i * 4 + (u0 + w + 3))
                    for c, (c0, n) in enumerate(chunks):
                        j = w * nc_ + c
                        if w == 0:
                            pe.wait_ge(s["h"], s.base["h"] + h_need(c))
                        pe.wait_ge(s["free"], s.base["free"] + i * (4 * nc_) + (j + 1))
                        out = ps[:, j % 4, 0:n]
                        for k in range(KT):
                            mm = three(out, wh[:, w, k], wl[:, w, k], ah[:, k, c0:c0 + n], al[:, k, c0:c0 + n],
                                       k == 0, k == KT - 1)
                        mm.then_inc(s["part"] if c < nc_ - 1 else unit_done, 1)

        L = S["load"]
        pe.wait_ge(L["small"], L.base["small"] + 16 * 10)
        pe.transpose(ps[:, 0, 0:60], small[:], ident[0:60, 0:60])
        for k in range(CT):
            mm = pe.transpose(ps[:, 1, k * CONVW:(k + 1) * CONVW], taps_in[:, k * P:(k + 1) * P],
                              ident[0:CONVW, 0:CONVW])
        mm.then_inc(L["vecs_t"], 1)
        for t in range(QT + 1):
            n = P if t < QT else TSAMP
            pe.wait_ge(L[f"in{t % 3}"], L.base[f"in{t % 3}"] + 16 * (t // 3 + 1))
            for h in range(2):
                j = 2 * t + h
                if j >= 4:
                    pe.wait_ge(L["xin_free"], L.base["xin_free"] + j - 3)
                for k in range(4):
                    kk = 4 * h + k
                    mm = pe.transpose(ps[:, 2 + j % 4, k * P:k * P + n], xin[0:n, t % 3, kk * P:(kk + 1) * P],
                                      ident[0:n, 0:n])
                mm.then_inc(L["xt"], 1)
        barrier(pe, 1)
        norm(S["n1"], CHUNKS, sq)
        ffn("ffn1", S["n1"])
        barrier(pe, 2)
        norm(S["nm"], CHUNKS, sq)
        proj("w_in", S["nm"], 20, CHUNKS, hh, hl, lambda c: KT * (c + 1))
        barrier(pe, 3)
        M, C = S["mem"], S["conv"]
        pe.wait_ge(M["in"], M.base["in"] + 16)
        for t in range(2):
            for h in range(2):
                for k in range(4):
                    kk = 4 * h + k
                    mm = pe.transpose(ps[:, 2 * t + h, k * P:(k + 1) * P], min_[:, t, kk * P:(kk + 1) * P], ident[:])
                mm.then_inc(M["xt"], 1)
        pe.wait_ge(C["cc_in"], 16)
        for k in range(CT):
            for a in range(2):
                mm = pe.transpose(ps[:, 6 + k // 2, ((k % 2) * 2 + a) * 120:((k % 2) * 2 + a) * 120 + 120],
                                  cc_in[:, a, k * P:(k + 1) * P], ident[0:120, 0:120])
        mm.then_inc(C["cct"], 1)
        norm(M, [(0, NMEM)], msq)
        for name, n in (("w_ck", "mk"), ("w_cv", "mv")):
            s = S["mk"]
            u0 = UNIT[name]
            with pe.Fori(0, 2) as i:
                for w in range(4):
                    pe.wait_ge(w_split, i * 4 + (u0 + w + 3))
                    pe.wait_ge(M["h"], M.base["h"] + KT)
                    pe.wait_ge(s[n + "_free"], s.base[n + "_free"] + i * 4 + (w + 1))
                    for k in range(KT):
                        mm = three(ps[:, w, 0:NMEM], wh[:, w, k], wl[:, w, k], mh[:, k], ml[:, k], k == 0, k == KT - 1)
                    mm.then_inc(unit_done, 1)
            for t in range(2):
                for h in range(2):
                    j = 2 * t + h
                    pe.wait_ge(s[n + "_free"], s.base[n + "_free"] + 12)
                    for k in range(4):
                        kk = 4 * h + k
                        mm = pe.transpose(ps[:, j, k * P:(k + 1) * P], kvT[:, kk, t * P:(t + 1) * P], ident[:])
                    mm.then_inc(s[n + "_t"], 1)
            pe.wait_ge(s[n + "_tok"], s.base[n + "_tok"] + 4)
        for k in range(CT):
            pe.wait_ge(C["ug"], k + 1)
            if k >= 1:
                pe.wait_ge(C["ucs"], 2 * k)
            pe.transpose(ps[0:PAD, 4, 0:P], U[:, k, SEQ:SEQ + PAD], ident[:])
            for a in range(2):
                mm = pe.transpose(ps[0:120, 4, (a + 1) * P:(a + 2) * P], cct[:, k, a, :], ident[:])
            mm.then_inc(C["ut"], 1)
        for c, (c0, n) in enumerate(CHUNKS):
            pe.wait_ge(C["tap"], 2 * CONVW * CT)
            for k in range(CT):
                mm = pe.matmul(ps[:, 5, 0:n], ones[:], ya[:, k, c0:c0 + n], start=(k == 0), stop=(k == CT - 1))
            mm.then_inc(C["mean"], 1)
            for k in range(CT):
                pe.wait_ge(C["sq"], c * CT + k + 1)
                mm = pe.matmul(ps[:, 6, 0:n], ones[:], msq[:, k % 2, 0:n], start=(k == 0),
                               stop=(k == CT - 1)).then_inc(C["summed"], 1)
        barrier(pe, 4)
        A = S["pa"]
        pe.sem_inc(A["s_full"], 1)
        pe.wait_ge(A["tok_in"], 32)
        for a in range(2):
            for k in range(CT):
                mm = pe.transpose(ps[0:TSAMP, 6 + a, k * P:(k + 1) * P], ks[:, a, k, :], ident[:])
            mm.then_inc(A["tok_t"], 1)
        pe.wait_ge(A["tok_e"], 2)
        steps = [(h, t) for h in range(2) for t in range(QT)]
        NS = len(steps)
        TF = 4 + sum(1 + (t >= 4) for _, t in steps)
        with pe.Fori(0, H // 2) as i:
            pe.wait_ge(A["in"], i * 64 + 64)
            tf = [0]

            def tbank():
                b = 4 + tf[0] % 2
                pe.wait_ge(A["t_free"], i * TF + (tf[0] + 1))
                tf[0] += 1
                return b

            for src in (vT, kTp):
                for h in range(2):
                    b = tbank()
                    for k in range(4):
                        mm = pe.transpose(ps[:, b, k * P:(k + 1) * P], src[:, (4 * h + k) * P:(4 * h + k + 1) * P],
                                          ident[:])
                    mm.then_inc(A["t_full"], 1)

            def scores(n):
                h, t = steps[n]
                pe.wait_ge(A["s_free"], i * NS + (n + 1))
                for c in range(1 + (t >= 4)):
                    w = min(512, P * (t + 1) - 512 * c)
                    mm = pe.matmul(ps[:, 2 * (n % 2) + c, 0:w], qT[64 * h:64 * h + 64, t * P:(t + 1) * P],
                                   kTp[64 * h:64 * h + 64, 512 * c:512 * c + w], start=True, stop=True)
                mm.then_inc(A["s_full"], 1)

            def turn(n):
                h, t = steps[n]
                pe.wait_ge(A["p"], i * NS + (n + 1))
                for c in range(1 + (t >= 4)):
                    b = tbank()
                    for k in range(4 * c, min(4 * c + 4, t + 1)):
                        mm = pe.transpose(ps[:, b, (k % 4) * P:(k % 4 + 1) * P], Sb[:, n % 3, k * P:(k + 1) * P],
                                          ident[:])
                    mm.then_inc(A["t_full"], 1)

            def values(n, tf_n):
                h, t = steps[n]
                pe.wait_ge(A["t_free"], i * TF + (tf_n + 2))
                pe.wait_ge(A["o_free"], i * NS + (n + 1))
                for k in range(t + 1):
                    mm = pe.matmul(ps[64 * h:64 * h + 64, 6 + n % 2, 0:P], vtok[:, k, 64 * h:64 * h + 64],
                                   PT[:, n % 2, k, :], start=(k == 0), stop=(k == t))
                mm.then_inc(A["o_full"], 1)

            scores(0)
            scores(1)
            for n in range(NS):
                turn(n)
                upto = tf[0]
                if n + 2 < NS:
                    scores(n + 2)
                values(n, upto)
        barrier(pe, 5)
        B = S["sa"]
        pe.sem_inc(B["s_full"], 2)
        pe.sem_inc(B["v_used"], 2)
        pe.sem_inc(B["s_part"], 1)
        with pe.Fori(0, NB // 2) as i:
            pe.wait_ge(B["q"], i * 16 + 16)
            for b, c in [(b, c) for b in range(2) for c in range(3)]:
                if c == 0:
                    pe.wait_ge(B[f"k{b}"], i * 32 + 32)
                j = b * 3 + c
                for k in range(CT):
                    pe.wait_ge(B[("t_freea", "t_freed")[k % 2]], i * 12 + (2 * j + k // 2 + 1))
                    for r in range(4):
                        if c < 2:
                            src, w = Ko[:, b, 4 * c + r, k * P:(k + 1) * P], OG
                        else:
                            src, w = Kr[:, b, r, k * P:(k + 1) * P], P
                        mm = pe.transpose(ps[:, k % 2, r * w:(r + 1) * w], src, ident[0:w, 0:w])
                    mm.then_inc(B["t_full"], 1)
                if j == 0:
                    pe.wait_ge(B["s_free"], i + 1)
                pe.wait_ge(B["t_freea"], i * 12 + (2 * j + 3))
                pe.wait_ge(B["t_freed"], i * 12 + (2 * j + 3))
                w = 4 * (OG if c < 2 else P)
                for k in range(CT):
                    mm = pe.matmul(ps[64 * b:64 * b + 64, 2 + c, 0:w], Qc[:, b, k, :], Kc[:, k, 0:w],
                                   start=(k == 0), stop=(k == CT - 1))
                mm.then_inc(B["s_part"], 1)
                if c == 2:
                    for k in range(CT):
                        mm = pe.matmul(ps[64 * b:64 * b + 64, 5, 0:TS], Qc[:, b, k, :],
                                       Knc[:, k, b * TS:(b + 1) * TS], start=(k == 0), stop=(k == CT - 1))
                    mm.then_inc(B["s_full"], 1)
            pe.wait_ge(B["p"], i + 1)
            for g_ in range(4):
                if g_ >= 2:
                    pe.wait_ge(B[("pt_a", "pt_d")[g_ % 2]], i * 2 + 1)
                for r in range(4 if g_ < 3 else 1):
                    blk = 4 * g_ + r
                    w = OG if blk < ORS else (P if blk < 12 else TS)
                    off = blk * OG if blk < ORS else ORS * OG + (blk - ORS) * P
                    mm = pe.transpose(ps[0:w, g_ % 2, r * P:(r + 1) * P], Ss[:, off:off + w], ident[:])
                mm.then_inc(B["pt_full"], 1)
            pe.wait_ge(B["pt_a"], i * 2 + 2)
            pe.wait_ge(B["pt_d"], i * 2 + 2)
            pe.wait_ge(B["vn"], i * 16 + 16)
            pe.wait_ge(B["o_free"], i * 2 + 1)
            for b in range(2):
                pe.wait_ge(B[f"v{b}"], i * 32 + 32)
                for k in range(CT):
                    for blk in range(13):
                        if blk < ORS:
                            v, w = Vo[:, b, blk, k * P:(k + 1) * P], OG
                        elif blk < 12:
                            v, w = Vr[:, b, blk - ORS, k * P:(k + 1) * P], P
                        else:
                            v, w = Vn[:, b, k * P:(k + 1) * P], TS
                        mm = pe.matmul(ps[:, 6, (b * CT + k) * 16:(b * CT + k) * 16 + 16], v,
                                       PTs[0:w, blk, b * 64 + k * 16:b * 64 + k * 16 + 16],
                                       start=(blk == 0), stop=(blk == 12))
                mm.then_inc(B["v_used"], 1)
        barrier(pe, 6)
        proj("w_out", S["so"], 8, CHUNKS, hh, hl, lambda c: KT)
        barrier(pe, 7)
        norm(S["nx"], CHUNKS, sq)
        proj("w_cq", S["nx"], 8, CHUNKS, hh, hl, lambda c: KT * (c + 1))
        barrier(pe, 8)
        X = S["xa"]
        pe.sem_inc(X["o_full"], 1)
        with pe.Fori(0, HX) as i:
            pe.wait_ge(X["in"], i * 48 + 48)

            def xscores(t):
                pe.wait_ge(X["e"], i * QT + (t + 1))
                for k in range(2):
                    mm = pe.matmul(ps[:, t % 2, 0:NMEM], xq[:, k, t * P:(t + 1) * P], xk[:, k, :], start=(k == 0),
                                   stop=(k == 1))
                mm.then_inc(X["s_full"], 1)

            xscores(0)
            xscores(1)
            for t in range(QT):
                pe.wait_ge(X["p"], i * QT + (t + 1))
                pe.wait_ge(X["t_free"], i * QT + (t + 1))
                for k in range(2):
                    mm = pe.transpose(ps[:, 2 + t % 2, k * P:(k + 1) * P], Xb[:, t % 3, k * P:(k + 1) * P], ident[:])
                mm.then_inc(X["t_full"], 1)
                if t + 2 < QT:
                    xscores(t + 2)
                pe.wait_ge(X["t_free"], i * QT + (t + 3))
                pe.wait_ge(X["o_free"], i * QT + (t + 1))
                for d in range(2):
                    for k in range(2):
                        mm = pe.matmul(ps[:, 4 + t % 2, d * P:(d + 1) * P], xv[:, k, d * P:(d + 1) * P],
                                       XT[:, t % 2, k, :], start=(k == 0), stop=(k == 1))
                mm.then_inc(X["o_full"], 1)
        Y = S["xs"]
        pe.sem_inc(Y["s_full"], 2)
        pe.sem_inc(Y["o_full"], 1)
        with pe.Fori(0, 2) as i:
            for b in range(4):
                pe.wait_ge(Y[f"k{b % 2}"], i * 32 + 16 * (b // 2 + 1))
                for m in range(4):
                    pe.wait_ge(Y[("t_freea", "t_freed")[m % 2]], i * 8 + (b * 2 + m // 2 + 1))
                    for k in range(2):
                        for j in range(2):
                            mm = pe.transpose(ps[:, m % 2, k * 256 + j * P:k * 256 + (j + 1) * P],
                                              cK[:, b % 2, j, (2 * m + k) * P:(2 * m + k + 1) * P], ident[:])
                    mm.then_inc(Y["t_full"], 1)
                pe.wait_ge(Y["t_freea"], i * 8 + (b * 2 + 3))
                pe.wait_ge(Y["t_freed"], i * 8 + (b * 2 + 3))
                if b == 0:
                    pe.wait_ge(Y["qc"], i * 4 + 4)
                    pe.wait_ge(Y["e"], i + 1)
                for k in range(KT):
                    mm = pe.matmul(ps[32 * b:32 * b + 32, 2, 0:NMEM], cqc[:, b, k, :], cKT[:, k, :], start=(k == 0),
                                   stop=(k == KT - 1))
                mm.then_inc(Y["s_full"], 1)
            pe.wait_ge(Y["p"], i + 1)
            for j in range(2):
                mm = pe.transpose(ps[:, 3, j * P:(j + 1) * P], cS[:, j * P:(j + 1) * P], ident[:])
            mm.then_inc(Y["pt_full"], 1)
            pe.wait_ge(Y["pt"], i + 1)
            pe.wait_ge(Y["v"], i * 16 + 16)
            pe.wait_ge(Y["oe"], i + 1)
            for b in range(4):
                for k in range(KT):
                    for j in range(2):
                        mm = pe.matmul(ps[:, 4, (k * 4 + b) * TS:(k * 4 + b + 1) * TS],
                                       cV[:, b, j, k * P:(k + 1) * P],
                                       cPT[:, j, b * 32 + (k // 2) * TS:b * 32 + (k // 2) * TS + TS],
                                       start=(j == 0), stop=(j == 1))
            mm.then_inc(Y["o_full"], 1)
        barrier(pe, 9)
        proj("w_co", S["sc"], 8, CHUNKS, hh, hl, lambda c: KT)
        barrier(pe, 10)
        norm(S["n2"], CHUNKS, sq)
        ffn("ffn2", S["n2"])
        barrier(pe, 11)
        F = S["fin"]
        norm(F, CHUNKS, sq)
        for t in range(QT + 1):
            n = P if t < QT else TSAMP
            pe.wait_ge(F["h"], F.base["h"] + KT * ([c for c, (c0, w) in enumerate(CHUNKS) if t * P < c0 + w][0] + 1))
            for h in range(2):
                j = 2 * t + h
                if j >= 4:
                    pe.wait_ge(F["tok"], F.base["tok"] + j - 3)
                for k in range(4):
                    mm = pe.transpose(ps[0:n, j % 4, k * P:(k + 1) * P], x[:, 4 * h + k, t * P:t * P + n], ident[:])
                mm.then_inc(F["yt"], 1)

    @block.scalar
    def _(act):
        def squares(s, chunks, src, sqt):
            for c, (c0, n) in enumerate(chunks):
                for k in range(0, KT, 2):
                    j = c * KT + k
                    if j >= 4:
                        act.wait_ge(s["summed"], s.base["summed"] + j - 3)
                    act.activation(sqt[:, sq_slot(k), 0:n], src[:, k, c0:c0 + n], ACT.Square).then_inc(s["sqa"], 1)

        def roots(s, chunks, rst):
            for c, (c0, n) in enumerate(chunks):
                act.wait_ge(s["var"], s.base["var"] + c + 1)
                act.activation(rst[:, c, 0:n], rst[:, c, 0:n], ACT.Sqrt).then_inc(s["std"], 1)

        def norm(s, chunks, src, sqt, rst, tbt, hit):
            squares(s, chunks, src, sqt)
            roots(s, chunks, rst)
            for c, (c0, n) in enumerate(chunks):
                for k in range(KT):
                    j = c * KT + k
                    act.wait_ge(s["t"], s.base["t"] + j + 1)
                    act.copy(hit[:, k, c0:c0 + n], tbt[:, j % 3, 0:n]).then_inc(s["hi"], 1)

        def ffn(name, s):
            c0_ = COL[name]
            with act.Fori(0, FG) as i:
                def silu(j):
                    f, c = divmod(j, NC)
                    n = CHUNKS[c][1]
                    if c < NC - 1:
                        act.wait_ge(s["gate"], s.base["gate"] + i * 4 + (2 * f + c + 1))
                    else:
                        act.wait_ge(unit_done, i * 4 + (SLOTS + c0_ + 2 * f + 1))
                    act.wait_ge(s["prod"], s.base["prod"] + i * 6 + (j + 1))
                    act.activation(sg[:, j % 2, 0:n], ps[:, 2 * (j % 2), 0:n], ACT.Silu).then_inc(s["sg"], 1)

                def hi(j):
                    f, c = divmod(j, NC)
                    c0, n = CHUNKS[c]
                    act.wait_ge(s["prod"], s.base["prod"] + i * 6 + (j + 3))
                    act.copy(hidh[:, f, c0:c0 + n], ht[:, j % 2, 0:n]).then_inc(s["hhi"], 1)

                for j in range(2 * NC):
                    silu(j)
                    if j >= 1:
                        hi(j - 1)
                hi(2 * NC - 1)

        def store_proj(name, s, nunits, dst):
            with act.Fori(0, nunits // 4) as i:
                for w in range(4):
                    act.wait_ge(s[f"st{w}"], s.base[f"st{w}"] + i * 16 + 16)
                    for c, (c0, n) in enumerate(CHUNKS):
                        j = w * NC + c
                        if c < NC - 1:
                            act.wait_ge(s["part"], s.base["part"] + i * 8 + (2 * w + c + 1))
                        else:
                            act.wait_ge(unit_done, i * 4 + (SLOTS + COL[name] + w + 1))
                        act.copy(stage[:, w, c0:c0 + n], ps[:, j % 4, 0:n]).then_inc(s["free"], 1)
                    act.wait_ge(s["free"], s.base["free"] + i * 12 + (4 + NC * (w + 1)))
                    act.dma_start(dst[bass.ds(i * (4 * P) + w * P, P), :], stage[:, w, :]).then_inc(s[f"st{w}"], 16)
            for w in range(4):
                act.wait_ge(s[f"st{w}"], s.base[f"st{w}"] + 16 * (nunits // 4) + 16)

        def split_input(s):
            for k in range(KT):
                act.wait_ge(s[f"in{k % 3}"], s.base[f"in{k % 3}"] + 16 * (k // 3 + 1))
                act.copy(hh[:, k, :], mixin[:, k % 3, :]).then_inc(s["hi"], 1)

        for w in range(4):
            act.sem_inc(S["nm"][f"st{w}"], 16)
        barrier(act, 1)
        norm(S["n1"], CHUNKS, x, sq, rs, tb, hh)
        ffn("ffn1", S["n1"])
        barrier(act, 2)
        norm(S["nm"], CHUNKS, x, sq, rs, tb, hh)
        store_proj("w_in", S["nm"], 20, z)
        barrier(act, 3)
        M, C, s = S["mem"], S["conv"], S["mk"]
        act.sem_inc(s["mk_free"], 4)
        act.sem_inc(s["mv_free"], 4)
        act.wait_ge(M["ev"], M.base["ev"] + 4)
        norm(M, [(0, NMEM)], memT, msq, mrs, mtb, mh)
        for k in range(CT):
            act.wait_ge(C["gz"], 16 * (k + 1))
            act.activation(gz[:], gz[:], ACT.Sigmoid).then_inc(C["sig"], 1)
        for name, n in (("w_ck", "mk"), ("w_cv", "mv")):
            if n == "mv":
                act.wait_ge(s["mkst"], s.base["mkst"] + 16)
            with act.Fori(0, 2) as i:
                for w in range(4):
                    act.wait_ge(unit_done, i * 4 + (SLOTS + COL[name] + w + 1))
                    act.copy(kvT[:, bass.ds(i * 4 + w, 1), :], ps[:, w:w + 1, 0:NMEM]).then_inc(s[n + "_free"], 1)
            if n == "mk":
                act.wait_ge(s["mk_free"], s.base["mk_free"] + 12)
                act.dma_start(mkT.rearrange("(k p) t -> p k t", p=P), kvT[:]).then_inc(s["mkst"], 16)
            for t in range(2):
                for h in range(2):
                    j = 2 * t + h
                    act.wait_ge(s[n + "_t"], s.base[n + "_t"] + j + 1)
                    if n == "mv" and j == 0:
                        act.wait_ge(s["kvst"], s.base["kvst"] + 16)
                    act.copy(kvtok[:, t, 512 * h:512 * h + 512], ps[:, j, :]).then_inc(s[n + "_tok"], 1)
            act.wait_ge(s[n + "_tok"], s.base[n + "_tok"] + 4)
            act.dma_start(mem_o[n[1]], kvtok[:]).then_inc(s["kvst"], 16)
        for k in range(CT):
            act.wait_ge(C["ut"], k + 1)
            act.copy(ucs[0:PAD, 0, k * P:(k + 1) * P], ps[0:PAD, 4, 0:P]).then_inc(C["ucs"], 1)
            act.copy(ucs[:, 1:3, k * P:(k + 1) * P], ps[0:4 * PAD, 4, P:3 * P].rearrange("p (a c) -> p a c", a=2)
                     ).then_inc(C["ucs"], 1)
        act.wait_ge(C["ucs"], 2 * CT)
        act.dma_start(new_conv_p, ucs[0:PAD, 0, :]).then_inc(C["ucst"], 16)
        act.dma_start(new_conv_s, ucs[:, 1:3, :]).then_inc(C["ucst"], 16)
        for c, (c0, n) in enumerate(CHUNKS):
            for k in range(CT):
                j = c * CT + k
                act.wait_ge(C["xc"], j + 1)
                if j >= 2:
                    act.wait_ge(C["summed"], j - 1)
                act.activation(msq[:, k % 2, 0:n], ya[:, k, c0:c0 + n], ACT.Square).then_inc(C["sq"], 1)
            act.wait_ge(C["var"], c + 1)
            act.activation(mrs[:, 0, 0:n], mrs[:, 0, 0:n], ACT.Sqrt).then_inc(C["std"], 1)
        for k in range(CT):
            act.wait_ge(C["ln"], CT * NC)
            act.activation(ya[:, k, :], ya[:, k, :], ACT.Silu, bias=vecs[:, V_LB + k:V_LB + k + 1]
                           ).then_inc(C["ob"], 1)
        act.wait_ge(C["ob"], CT)
        act.dma_start(mix[CT * P:KT * P, :].rearrange("(k p) t -> p k t", p=P), ya[:]).then_inc(C["obst"], 16)
        act.wait_ge(C["obst"], 16)
        act.wait_ge(C["ucst"], 32)
        act.wait_ge(s["kvst"], s.base["kvst"] + 32)
        act.wait_ge(s["mkst"], s.base["mkst"] + 16)
        barrier(act, 4)
        A = S["pa"]
        act.sem_inc(A["t_free"], 2)
        act.sem_inc(A["kst"], 32)
        for a in range(2):
            act.wait_ge(A["tok_t"], a + 1)
            act.copy(kvs[:, a, :], ps[0:TSAMP, 6 + a, :]).then_inc(A["tok_e"], 1)
        act.wait_ge(A["tok_e"], 2)
        act.dma_start(win_s["k"], kvs[:, 0, :]).then_inc(A["tokst"], 16)
        act.dma_start(win_s["v"], kvs[:, 1, :]).then_inc(A["tokst"], 16)
        steps = [(h, t) for h in range(2) for t in range(QT)]
        NS = len(steps)
        TF = 4 + sum(1 + (t >= 4) for _, t in steps)
        with act.Fori(0, H // 2) as i:
            tf = [0]

            def evac(dst):
                act.wait_ge(A["t_full"], i * TF + (tf[0] + 1))
                nb = dst.shape[1]
                act.copy(dst, ps[:, 4 + tf[0] % 2, 0:nb * P].rearrange("p (k c) -> p k c", c=P)
                         ).then_inc(A["t_free"], 1)
                tf[0] += 1

            act.wait_ge(A["kst"], i * 32 + 32)
            for dst in (vtok, ktok):
                for h in range(2):
                    evac(dst[:, 4 * h:4 * h + 4, :])
            act.wait_ge(A["t_free"], i * TF + 6)
            act.dma_start(win_p["v"][:, :, bass.ds(i * P, P)], vtok[:]).then_inc(A["kst"], 16)
            act.dma_start(win_p["k"][:, :, bass.ds(i * P, P)], ktok[:]).then_inc(A["kst"], 16)

            def exp(n):
                h, t = steps[n]
                act.wait_ge(A["m"], i * NS + (n + 1))
                w = P * (t + 1)
                act.activation(Sb[:, n % 3, 0:w], Sb[:, n % 3, 0:w], ACT.Exp, bias=stat[:, n % 4, 1:2], scale=0.125,
                               accum_out=stat[:, n % 4, 2:3]).then_inc(A["e"], 1)

            exp(0)
            exp(1)
            for n in range(NS):
                h, t = steps[n]
                if n >= 2:
                    act.wait_ge(A["o_full"], i * NS + (n - 1))
                for c in range(1 + (t >= 4)):
                    evac(PT[:, n % 2, 4 * c:min(4 * c + 4, t + 1), :])
                if n + 2 < NS:
                    exp(n + 2)
            act.wait_ge(A["o_free"], i * NS + (2 + NS))
            act.dma_start(mix[bass.ds(i * P, P), 0:SEQ], oT[:]).then_inc(A["ost"], 16)
        act.wait_ge(A["kst"], 32 * (H // 2) + 32)
        act.wait_ge(A["ost"], 16 * (H // 2) + 16)
        act.wait_ge(A["tokst"], 32)
        barrier(act, 5)
        B = S["sa"]
        act.sem_inc(B["t_freea"], 1)
        with act.Fori(0, NB // 2) as i:
            for b, c in [(b, c) for b in range(2) for c in range(3)]:
                j = 3 * b + c
                w = 4 * (OG if c < 2 else P)
                for k in range(0, CT, 2):
                    act.wait_ge(B["t_full"], i * 24 + (j * CT + k + 1))
                    act.wait_ge(B["s_part"], i * 6 + (j + 1))
                    act.copy(Kc[:, k, 0:w], ps[:, 0, 0:w]).then_inc(B["t_freea"], 1)
            act.wait_ge(B["m"], i + 1)
            act.activation(Ss[:], Ss[:], ACT.Exp, bias=sstat[:, 5:6], scale=0.125, accum_out=sstat[:, 6:7]
                           ).then_inc(B["e"], 1)
            for g_ in (0, 2):
                act.wait_ge(B["pt_full"], i * 4 + (g_ + 1))
                w = OG if g_ == 0 else P
                act.copy(PTs[0:w, 4 * g_:4 * g_ + 4, :], ps[0:w, 0, :].rearrange("p (k c) -> p k c", c=P)
                         ).then_inc(B["pt_a"], 1)
        act.wait_ge(B["o_free"], 1 + NB)
        act.dma_start(mix[0:CT * P, SEQ:T].rearrange("(k p) t -> p k t", p=P),
                      oS[:].rearrange("p k b t -> p k (b t)")).then_inc(B["ost"], 16)
        act.wait_ge(B["ost"], 16)
        barrier(act, 6)
        split_input(S["so"])
        barrier(act, 7)
        norm(S["nx"], CHUNKS, x, sq, rs, tb, hh)
        store_proj("w_cq", S["nx"], 8, zx)
        barrier(act, 8)
        X = S["xa"]
        act.sem_inc(X["t_free"], 2)
        act.sem_inc(X["e"], 2)
        with act.Fori(0, HX) as i:
            def xexp(t):
                act.wait_ge(X["m"], i * QT + (t + 1))
                act.activation(Xb[:, t % 3, :], ps[:, t % 2, 0:NMEM], ACT.Exp, bias=xstat[:, t % 4, 1:2],
                               scale=HDX ** -0.5, accum_out=xstat[:, t % 4, 2:3]).then_inc(X["e"], 1)

            xexp(0)
            xexp(1)
            for t in range(QT):
                act.wait_ge(X["t_full"], i * QT + (t + 1))
                if t >= 2:
                    act.wait_ge(X["o_full"], i * QT + t)
                act.copy(XT[:, t % 2], ps[:, 2 + t % 2, 0:2 * P].rearrange("p (k c) -> p k c", c=P)
                         ).then_inc(X["t_free"], 1)
                if t + 2 < QT:
                    xexp(t + 2)
            act.wait_ge(X["o_free"], i * QT + (2 + QT))
            act.dma_start(mixx[bass.ds(i * HDX, HDX), 0:SEQ].rearrange("(k p) t -> p k t", p=P), xo[:]
                          ).then_inc(X["ost"], 16)
        Y = S["xs"]
        act.sem_inc(Y["t_freea"], 1)
        act.sem_inc(Y["e"], 1)
        with act.Fori(0, 2) as i:
            for b in range(4):
                for m in (0, 2):
                    act.wait_ge(Y["t_full"], i * 16 + (b * 4 + m + 1))
                    act.wait_ge(Y["s_full"], i * 4 + (b + 2))
                    act.copy(cKT[:, 2 * m:2 * m + 2, :], ps[:, 0, :].rearrange("p (k c) -> p k c", k=2)
                             ).then_inc(Y["t_freea"], 1)
            act.wait_ge(Y["m"], i + 1)
            act.activation(cS[:], ps[:, 2, 0:NMEM], ACT.Exp, bias=cstat[:, 1:2], scale=HDX ** -0.5,
                           accum_out=cstat[:, 2:3]).then_inc(Y["e"], 1)
            act.wait_ge(Y["pt_full"], i + 1)
            act.copy(cPT[:], ps[:, 3, 0:2 * P].rearrange("p (k c) -> p k c", c=P)).then_inc(Y["pt"], 1)
        act.wait_ge(Y["oe"], 3)
        act.dma_start(mixx[:, SEQ:T].rearrange("(k p) t -> p k t", p=P), co[:].rearrange("p k b t -> p k (b t)")
                      ).then_inc(Y["ost"], 16)
        act.wait_ge(X["ost"], 16 * HX + 16)
        act.wait_ge(Y["ost"], 16)
        barrier(act, 9)
        split_input(S["sc"])
        barrier(act, 10)
        norm(S["n2"], CHUNKS, x, sq, rs, tb, hh)
        ffn("ffn2", S["n2"])
        barrier(act, 11)
        F = S["fin"]
        squares(F, CHUNKS, x, sq)
        roots(F, CHUNKS, rs)
        for t in range(QT + 1):
            n = P if t < QT else TSAMP
            for h in range(2):
                act.wait_ge(F["yt"], F.base["yt"] + 2 * t + h + 1)
                if t >= 2:
                    act.wait_ge(F[f"out{t % 2}"], F.base[f"out{t % 2}"] + 16 * (t // 2))
                act.copy(ytok[0:n, t % 2, 512 * h:512 * h + 512], ps[0:n, (2 * t + h) % 4, :]).then_inc(F["tok"], 1)

    @block.vector
    def _(dve):
        def squares(s, chunks, src, sqt):
            for c, (c0, n) in enumerate(chunks):
                for k in range(1, KT, 2):
                    j = c * KT + k
                    if j >= 4:
                        dve.wait_ge(s["summed"], s.base["summed"] + j - 3)
                    dve.tensor_tensor(sqt[:, sq_slot(k), 0:n], src[:, k, c0:c0 + n], src[:, k, c0:c0 + n], ALU.mult
                                      ).then_inc(s["sqd"], 1)

        def inverse_rms(s, chunks, rst):
            for c, (c0, n) in enumerate(chunks):
                dve.wait_ge(s["summed"], s.base["summed"] + KT * (c + 1))
                dve.tensor_scalar(rst[:, c, 0:n], ps[:, 5 + c, 0:n], 1.0 / D, EPS, ALU.mult, ALU.add
                                  ).then_inc(s["var"], 1)
            for c, (c0, n) in enumerate(chunks):
                dve.wait_ge(s["std"], s.base["std"] + c + 1)
                dve.reciprocal(rst[:, c, 0:n], rst[:, c, 0:n]).then_inc(s["rstd"], 1)

        def norm(s, chunks, src, sqt, rst, tbt, gain, hit, lot):
            squares(s, chunks, src, sqt)
            inverse_rms(s, chunks, rst)
            jobs = [(c, k) for c in range(len(chunks)) for k in range(KT)]

            def lo(j):
                c, k = jobs[j]
                c0, n = chunks[c]
                dve.wait_ge(s["hi"], s.base["hi"] + j + 1)
                dve.tensor_tensor(lot[:, k, c0:c0 + n], tbt[:, j % 3, 0:n], hit[:, k, c0:c0 + n].bitcast(F32),
                                  ALU.subtract).then_inc(s["h"], 1)

            for j, (c, k) in enumerate(jobs):
                c0, n = chunks[c]
                dve.wait_ge(s["rstd"], s.base["rstd"] + c + 1)
                if j >= 3:
                    dve.wait_ge(s["h"], s.base["h"] + j - 2)
                dve.scalar_tensor_tensor(out=tbt[:, j % 3, 0:n], in0=src[:, k, c0:c0 + n],
                                         scalar=vecs[:, gain + k:gain + k + 1], in1=rst[:, c, 0:n], op0=ALU.mult,
                                         op1=ALU.mult).then_inc(s["t"], 1)
                if j >= 1:
                    lo(j - 1)
            lo(len(jobs) - 1)

        def ffn(name, s):
            c0_, r0_ = COL[name], ROW[name]
            with dve.Fori(0, FG) as i:
                def lo(j):
                    f, c = divmod(j, NC)
                    c0, n = CHUNKS[c]
                    dve.wait_ge(s["hhi"], s.base["hhi"] + i * 6 + (j + 1))
                    dve.tensor_tensor(hidl[:, f, c0:c0 + n], ht[:, j % 2, 0:n], hidh[:, f, c0:c0 + n].bitcast(F32),
                                      ALU.subtract).then_inc(s["hid"], 1)

                for j in range(2 * NC):
                    f, c = divmod(j, NC)
                    n = CHUNKS[c][1]
                    if c < NC - 1:
                        dve.wait_ge(s["up"], s.base["up"] + i * 4 + (2 * f + c + 1))
                    else:
                        dve.wait_ge(unit_done, i * 4 + (SLOTS + c0_ + 2 * f + 2))
                    dve.wait_ge(s["sg"], s.base["sg"] + i * 6 + (j + 1))
                    dve.wait_ge(s["hid"], s.base["hid"] + i * 6 + max(j, 1))
                    dve.tensor_tensor(ht[:, j % 2, 0:n], ps[:, 2 * (j % 2) + 1, 0:n], sg[:, j % 2, 0:n], ALU.mult
                                      ).then_inc(s["prod"], 1)
                    if j >= 1:
                        lo(j - 1)
                lo(2 * NC - 1)
                for j in range(NC * KT):
                    c, d = divmod(j, KT)
                    c0, n = CHUNKS[c]
                    if j < NC * KT - 1:
                        dve.wait_ge(s["down"], s.base["down"] + i * (NC * KT - 1) + (j + 1))
                    else:
                        dve.wait_ge(row_done, i * 2 + (2 + r0_ + 2))
                    dve.scalar_tensor_tensor(out=x[:, d, c0:c0 + n], in0=ps[:, 4 + j % 4, 0:n], scalar=0.5,
                                             in1=x[:, d, c0:c0 + n], op0=ALU.mult, op1=ALU.add
                                             ).then_inc(s["res"], 1)

        def split_input(s):
            for k in range(KT):
                dve.wait_ge(s["hi"], s.base["hi"] + k + 1)
                dve.tensor_tensor(hl[:, k, :], mixin[:, k % 3, :], hh[:, k, :].bitcast(F32), ALU.subtract
                                  ).then_inc(s["h"], 1)

        def add_proj(name, s):
            split_input(s)
            with dve.Fori(0, 2) as i:
                for w in range(4):
                    for c, (c0, n) in enumerate(CHUNKS):
                        j = w * NC + c
                        if c < NC - 1:
                            dve.wait_ge(s["part"], s.base["part"] + i * 8 + (2 * w + c + 1))
                        else:
                            dve.wait_ge(unit_done, i * 4 + (SLOTS + COL[name] + w + 1))
                        xt = x[:, bass.ds(i * 4 + w, 1), c0:c0 + n]
                        dve.tensor_tensor(xt, ps[:, j % 4:j % 4 + 1, 0:n], xt, ALU.add).then_inc(s["free"], 1)

        dve.sem_inc(S["n1"]["prod"], 2)
        dve.sem_inc(S["n1"]["res"], 4)
        dve.sem_inc(S["n1"]["free"], 4)
        dve.sem_inc(S["n1"]["hid"], 1)
        L = S["load"]
        dve.wait_ge(L["vecs_t"], L.base["vecs_t"] + 1)
        dve.tensor_copy(vecs[:], ps[:, 0, 0:60]).then_inc(L["vecs"], 1)
        dve.tensor_copy(taps[:], ps[:, 1, 0:CT * CONVW].rearrange("p (k t) -> p k t", t=CONVW)
                        ).then_inc(L["vecs"], 1)
        for t in range(QT + 1):
            n = P if t < QT else TSAMP
            for h in range(2):
                j = 2 * t + h
                dve.wait_ge(L["xt"], L.base["xt"] + j + 1)
                dve.tensor_copy(x[:, 4 * h:4 * h + 4, t * P:t * P + n],
                                ps[:, 2 + j % 4, :].rearrange("p (k c) -> p k c", c=P)[:, :, 0:n]
                                ).then_inc(L["xin_free"], 1)
        barrier(dve, 1)
        norm(S["n1"], CHUNKS, x, sq, rs, tb, G_FFN1, hh, hl)
        ffn("ffn1", S["n1"])
        barrier(dve, 2)
        norm(S["nm"], CHUNKS, x, sq, rs, tb, G_MIX, hh, hl)
        barrier(dve, 3)
        M, C = S["mem"], S["conv"]
        for t in range(2):
            for h in range(2):
                dve.wait_ge(M["xt"], M.base["xt"] + 2 * t + h + 1)
                dve.tensor_copy(memT[:, 4 * h:4 * h + 4, t * P:(t + 1) * P],
                                ps[:, 2 * t + h, :].rearrange("p (k c) -> p k c", c=P)).then_inc(M["ev"], 1)
        dve.wait_ge(C["cct"], 1)
        for k in range(CT):
            dve.tensor_copy(Us[:, k, :, 0:PAD], ps[:, 6 + k // 2, (k % 2) * 240:(k % 2) * 240 + 240]
                            .rearrange("p (b t) -> p b t", t=PAD)).then_inc(C["us"], 1)
        dve.memset(U[:, :, 0:PAD], 0.0).then_inc(C["us"], 1)
        dve.wait_ge(M["ev"], M.base["ev"] + 4)
        norm(M, [(0, NMEM)], memT, msq, mrs, mtb, G_MEM, mh, ml)
        dve.wait_ge(C["us"], CT + 1)
        for k in range(CT):
            dve.wait_ge(C["az"], 16 * (k + 1))
            dve.wait_ge(C["sig"], k + 1)
            dve.tensor_tensor(U[:, k, PAD:PAD + SEQ], az[:, 0:SEQ], gz[:, 0:SEQ], ALU.mult).then_inc(C["glu"], 1)
            dve.tensor_tensor(Us[:, k, :, PAD:PAD + TS], az[:, SEQ:T].rearrange("p (b t) -> p b t", t=TS),
                              gz[:, SEQ:T].rearrange("p (b t) -> p b t", t=TS), ALU.mult).then_inc(C["glu"], 1)
            dve.wait_ge(C["glu"], 2 * k + 2)
            dve.tensor_copy(cct[:, k].rearrange("p a (b t) -> p (a b) t", t=PAD), Us[:, k, :, TS:PAD + TS]
                            ).then_inc(C["ug"], 1)
        with dve.Fori(0, CT) as i:
            for t in range(CONVW):
                up = U[:, bass.ds(i, 1), t:t + SEQ].rearrange("p o t -> p (o t)")
                us = Us[:, bass.ds(i, 1), :, t:t + TS].rearrange("p o b t -> p (o b) t")
                yp = ya[:, bass.ds(i, 1), 0:SEQ].rearrange("p o t -> p (o t)")
                ys = ya[:, bass.ds(i, 1), SEQ:T].rearrange("p o (b t) -> p (o b) t", t=TS)
                w = taps[:, bass.ds(i, 1), t:t + 1].rearrange("p o t -> p (o t)")
                for q, (src, dst) in enumerate(((up, yp), (us, ys))):
                    if t == 0:
                        dve.tensor_scalar(dst, src, w, vecs[:, bass.ds(i + V_CB, 1)], ALU.mult, ALU.add
                                          ).then_inc(C["tap"], 1)
                    else:
                        dve.wait_ge(C["tap"], i * (2 * CONVW) + (2 * t - 1 + q))
                        dve.scalar_tensor_tensor(out=dst, in0=src, scalar=w, in1=dst, op0=ALU.mult, op1=ALU.add
                                                 ).then_inc(C["tap"], 1)
        dve.wait_ge(C["tap"], 2 * CONVW * CT)
        for c, (c0, n) in enumerate(CHUNKS):
            dve.wait_ge(C["mean"], c + 1)
            dve.wait_ge(C["xc"], CT * c)
            dve.tensor_scalar(mu[:, 0:n], ps[:, 5, 0:n], 1.0 / WA, None, ALU.mult).then_inc(C["mu"], 1)
            dve.wait_ge(C["mu"], c + 1)
            for k in range(CT):
                dve.tensor_tensor(ya[:, k, c0:c0 + n], ya[:, k, c0:c0 + n], mu[:, 0:n], ALU.subtract
                                  ).then_inc(C["xc"], 1)
            dve.wait_ge(C["summed"], CT * (c + 1))
            dve.wait_ge(C["ln"], CT * c)
            dve.tensor_scalar(mrs[:, 0, 0:n], ps[:, 6, 0:n], 1.0 / WA, EPS, ALU.mult, ALU.add).then_inc(C["var"], 1)
            dve.wait_ge(C["std"], c + 1)
            dve.reciprocal(mrs[:, 0, 0:n], mrs[:, 0, 0:n]).then_inc(C["rstd"], 1)
            dve.wait_ge(C["rstd"], c + 1)
            for k in range(CT):
                dve.scalar_tensor_tensor(out=ya[:, k, c0:c0 + n], in0=ya[:, k, c0:c0 + n],
                                         scalar=vecs[:, V_LG + k:V_LG + k + 1], in1=mrs[:, 0, 0:n], op0=ALU.mult,
                                         op1=ALU.mult).then_inc(C["ln"], 1)
        barrier(dve, 4)
        A = S["pa"]
        steps = [(h, t) for h in range(2) for t in range(QT)]
        NS = len(steps)
        dve.sem_inc(A["s_free"], 2)
        dve.sem_inc(A["ost"], 16)
        dve.sem_inc(A["o_free"], 2)
        with dve.Fori(0, H // 2) as i:
            dve.wait_ge(A["in"], i * 64 + 64)

            def mask(n):
                h, t = steps[n]
                w = P * (t + 1)
                dve.wait_ge(A["s_full"], i * NS + (n + 2))
                b = 2 * (n % 2)
                dve.sem_inc(met, 1)
                dve.tensor_tensor_reduce(out=Sb[:, n % 3, 0:w], in0=ps[:, b:b + 2, :].rearrange("p b n -> p (b n)")
                                         [:, 0:w], in1=pb[:, h, SEQ - w:SEQ], scale=1.0, scalar=-3.0e38, op0=ALU.add,
                                         op1=ALU.max, accum_out=stat[:, n % 4, 0:1]).then_inc(A["s_free"], 1)
                dve.wait_ge(A["s_free"], i * NS + (n + 3))
                dve.tensor_scalar(stat[:, n % 4, 1:2], stat[:, n % 4, 0:1], -0.125, None, ALU.mult
                                  ).then_inc(A["m"], 1)

            def normalise(n):
                h, t = steps[n]
                w = P * (t + 1)
                dve.wait_ge(A["e"], i * NS + (n + 1))
                dve.reciprocal(stat[:, n % 4, 3:4], stat[:, n % 4, 2:3]).then_inc(A["r"], 1)
                dve.wait_ge(A["r"], i * NS + (n + 1))
                dve.tensor_scalar(Sb[:, n % 3, 0:w], Sb[:, n % 3, 0:w], stat[:, n % 4, 3:4], None, ALU.mult
                                  ).then_inc(A["p"], 1)

            def output(n):
                h, t = steps[n]
                if n == 0:
                    dve.wait_ge(A["ost"], i * 16 + 16)
                dve.wait_ge(A["o_full"], i * NS + (n + 1))
                dve.tensor_copy(oT[64 * h:64 * h + 64, t * P:(t + 1) * P], ps[64 * h:64 * h + 64, 6 + n % 2, 0:P]
                                ).then_inc(A["o_free"], 1)

            mask(0)
            mask(1)
            for n in range(NS):
                normalise(n)
                if n >= 1:
                    output(n - 1)
                if n + 2 < NS:
                    mask(n + 2)
            output(NS - 1)
        barrier(dve, 5)
        B = S["sa"]
        dve.sem_inc(B["t_freed"], 1)
        dve.sem_inc(B["s_free"], 1)
        dve.sem_inc(B["o_free"], 1)
        dve.memset(Qc[:], 0.0).then_inc(B["qz"], 1)
        dve.wait_ge(B["qz"], 1)
        dve.wait_ge(B["bias"], 16)
        with dve.Fori(0, NB // 2) as i:
            dve.wait_ge(B["qk_in"], i * 32 + 32)
            dve.wait_ge(B["s_full"], i * 2 + 2)
            for b in range(2):
                for k in range(CT):
                    for hf in range(2):
                        h = 2 * k + hf
                        dve.tensor_copy(Qc[64 * hf:64 * hf + 64, b, k, h * TS:(h + 1) * TS],
                                        Qin[64 * hf:64 * hf + 64, k, b * TS:(b + 1) * TS]).then_inc(B["q"], 1)
            for b, c in [(b, c) for b in range(2) for c in range(3)]:
                j = 3 * b + c
                w = 4 * (OG if c < 2 else P)
                for k in range(1, CT, 2):
                    dve.wait_ge(B["t_full"], i * 24 + (j * CT + k + 1))
                    dve.wait_ge(B["s_part"], i * 6 + (j + 1))
                    dve.tensor_copy(Kc[:, k, 0:w], ps[:, 1, 0:w]).then_inc(B["t_freed"], 1)
            dve.wait_ge(B["s_full"], i * 2 + 4)
            dve.sem_inc(met, 1)
            off = 0
            for c, w in enumerate((4 * OG, 4 * OG, 512, TS)):
                ttr = dve.tensor_tensor_reduce(out=Ss[:, off:off + w], in0=ps[:, 2 + c, 0:w], in1=sbias[:, off:off + w],
                                               scale=1.0, scalar=-3.0e38, op0=ALU.add, op1=ALU.max,
                                               accum_out=sstat[:, c:c + 1])
                off += w
            ttr.then_inc(B["s_free"], 1)
            dve.wait_ge(B["s_free"], i + 2)
            dve.tensor_reduce(sstat[:, 4:5], sstat[:, 0:4], AX.X, ALU.max).then_inc(B["mx"], 1)
            dve.wait_ge(B["mx"], i + 1)
            dve.tensor_scalar(sstat[:, 5:6], sstat[:, 4:5], -0.125, None, ALU.mult).then_inc(B["m"], 1)
            dve.wait_ge(B["e"], i + 1)
            dve.reciprocal(sstat[:, 7:8], sstat[:, 6:7]).then_inc(B["r"], 1)
            dve.wait_ge(B["r"], i + 1)
            dve.tensor_scalar(Ss[:], Ss[:], sstat[:, 7:8], None, ALU.mult).then_inc(B["p"], 1)
            dve.wait_ge(B["pt_full"], i * 4 + 2)
            dve.tensor_copy(PTs[0:OG, 4:8, :], ps[0:OG, 1, :].rearrange("p (k c) -> p k c", c=P)
                            ).then_inc(B["pt_d"], 1)
            dve.wait_ge(B["pt_full"], i * 4 + 4)
            dve.tensor_copy(PTs[0:TS, 12, :], ps[0:TS, 1, 0:P]).then_inc(B["pt_d"], 1)
            dve.wait_ge(B["v_used"], i * 2 + 4)
            for hf in range(2):
                src = ps[64 * hf:64 * hf + 64, 6, 0:P].rearrange("p (b k c) -> p k b c", b=2, k=CT)
                dve.tensor_copy(oS[64 * hf:64 * hf + 64, :, bass.ds(i * 2, 2), :], src[:, :, :, hf * TS:(hf + 1) * TS]
                                ).then_inc(B["o_free"], 1)
        barrier(dve, 6)
        add_proj("w_out", S["so"])
        barrier(dve, 7)
        norm(S["nx"], CHUNKS, x, sq, rs, tb, G_X, hh, hl)
        barrier(dve, 8)
        X = S["xa"]
        dve.sem_inc(X["o_free"], 2)
        dve.sem_inc(X["ost"], 16)
        with dve.Fori(0, HX) as i:
            def xmax(t):
                dve.wait_ge(X["s_full"], i * QT + (t + 1))
                dve.tensor_reduce(xstat[:, t % 4, 0:1], ps[:, t % 2, 0:NMEM], AX.X, ALU.max).then_inc(X["mx"], 1)
                dve.wait_ge(X["mx"], i * QT + (t + 1))
                dve.tensor_scalar(xstat[:, t % 4, 1:2], xstat[:, t % 4, 0:1], -(HDX ** -0.5), None, ALU.mult
                                  ).then_inc(X["m"], 1)

            def xnorm(t):
                dve.wait_ge(X["e"], i * QT + (t + 3))
                dve.reciprocal(xstat[:, t % 4, 3:4], xstat[:, t % 4, 2:3]).then_inc(X["r"], 1)
                dve.wait_ge(X["r"], i * QT + (t + 1))
                dve.tensor_scalar(Xb[:, t % 3, :], Xb[:, t % 3, :], xstat[:, t % 4, 3:4], None, ALU.mult
                                  ).then_inc(X["p"], 1)

            def xout(t):
                if t == 0:
                    dve.wait_ge(X["ost"], i * 16 + 16)
                dve.wait_ge(X["o_full"], i * QT + (t + 2))
                dve.tensor_copy(xo[:, :, t * P:(t + 1) * P], ps[:, 4 + t % 2, 0:2 * P]
                                .rearrange("p (k c) -> p k c", c=P)).then_inc(X["o_free"], 1)

            xmax(0)
            xmax(1)
            for t in range(QT):
                xnorm(t)
                if t >= 1:
                    xout(t - 1)
                if t + 2 < QT:
                    xmax(t + 2)
            xout(QT - 1)
        Y = S["xs"]
        dve.sem_inc(Y["t_freed"], 1)
        dve.sem_inc(Y["oe"], 1)
        dve.memset(cqc[:], 0.0).then_inc(Y["qz"], 1)
        dve.wait_ge(Y["qz"], 1)
        dve.wait_ge(Y["q_in"], 16)
        with dve.Fori(0, 2) as i:
            dve.wait_ge(Y["s_full"], i * 4 + 2)
            for h in range(HX):
                dve.tensor_copy(cqc[:, :, 2 * h:2 * h + 2, h * TS:(h + 1) * TS],
                                cq[:, 2 * h:2 * h + 2, bass.ds(i * 32, 32)].rearrange("p k (b t) -> p b k t", b=4)
                                ).then_inc(Y["qc"], 1)
            for b in range(4):
                for m in (1, 3):
                    dve.wait_ge(Y["t_full"], i * 16 + (b * 4 + m + 1))
                    dve.wait_ge(Y["s_full"], i * 4 + (b + 2))
                    dve.tensor_copy(cKT[:, 2 * m:2 * m + 2, :], ps[:, 1, :].rearrange("p (k c) -> p k c", k=2)
                                    ).then_inc(Y["t_freed"], 1)
            dve.wait_ge(Y["s_full"], i * 4 + 6)
            dve.tensor_reduce(cstat[:, 0:1], ps[:, 2, 0:NMEM], AX.X, ALU.max).then_inc(Y["mx"], 1)
            dve.wait_ge(Y["mx"], i + 1)
            dve.tensor_scalar(cstat[:, 1:2], cstat[:, 0:1], -(HDX ** -0.5), None, ALU.mult).then_inc(Y["m"], 1)
            dve.wait_ge(Y["e"], i + 2)
            dve.reciprocal(cstat[:, 3:4], cstat[:, 2:3]).then_inc(Y["r"], 1)
            dve.wait_ge(Y["r"], i + 1)
            dve.tensor_scalar(cS[:], cS[:], cstat[:, 3:4], None, ALU.mult).then_inc(Y["p"], 1)
            dve.wait_ge(Y["o_full"], i + 2)
            dve.tensor_copy(co[:, :, bass.ds(i * 4, 4), :], ps[:, 4, 0:KT * 32]
                            .rearrange("p (k b t) -> p k b t", b=4, t=TS)).then_inc(Y["oe"], 1)
        barrier(dve, 9)
        add_proj("w_co", S["sc"])
        barrier(dve, 10)
        norm(S["n2"], CHUNKS, x, sq, rs, tb, G_FFN2, hh, hl)
        ffn("ffn2", S["n2"])
        barrier(dve, 11)
        F = S["fin"]
        squares(F, CHUNKS, x, sq)
        inverse_rms(F, CHUNKS, rs)
        for c, (c0, n) in enumerate(CHUNKS):
            dve.wait_ge(F["rstd"], F.base["rstd"] + c + 1)
            for k in range(KT):
                dve.scalar_tensor_tensor(out=x[:, k, c0:c0 + n], in0=x[:, k, c0:c0 + n],
                                         scalar=vecs[:, G_FIN + k:G_FIN + k + 1], in1=rs[:, c, 0:n], op0=ALU.mult,
                                         op1=ALU.mult).then_inc(F["h"], 1)

    ctx.close()


_INS = ["x_prompt", "x_sample", "mem_prompt", "cache_win_k", "cache_win_v", "cache_conv", "cache_mem_k",
        "cache_mem_v", "ffn1_norm", "ffn1_gate", "ffn1_up", "ffn1_down", "mix_norm", "w_in", "conv_w", "conv_b",
        "conv_ln_g", "conv_ln_b", "w_out", "xattn_norm", "mem_norm", "w_cq", "w_ck", "w_cv", "w_co", "ffn2_norm",
        "ffn2_gate", "ffn2_up", "ffn2_down", "final_norm"]
_OUTS = [("y_prompt", (1, SEQ, D)), ("y_sample", (NB, TS, D)),
         ("new_win_k_prompt", (1, 1, SEQ, H, HD)), ("new_win_v_prompt", (1, 1, SEQ, H, HD)),
         ("new_conv_prompt", (1, 1, PAD, WA)),
         ("new_mem_k_prompt", (1, 1, NMEM, HX, HDX)), ("new_mem_v_prompt", (1, 1, NMEM, HX, HDX)),
         ("new_win_k_sample", (1, NB, TS, H, HD)), ("new_win_v_sample", (1, NB, TS, H, HD)),
         ("new_conv_sample", (1, NB, PAD, WA))]


def kernel(**inputs):
    import concourse.bacc as _bacc
    from concourse.bass_utils import run_bass_kernel_spmd as _run

    nc = _bacc.Bacc("TRN2", target_bir_lowering=False, num_devices=1)
    given = {n: np.ascontiguousarray(inputs[n]) for n in _INS}
    given["prompt_bias"] = prompt_bias()
    given["sample_bias"] = sample_bias()
    arrays, ins = {}, {}
    for name, a in given.items():
        arrays[f"in_{name}"] = a
        ins[name] = nc.dram_tensor(f"in_{name}", a.shape, mybir.dt.from_np(a.dtype), kind="ExternalInput").ap()
    outs = {name: nc.dram_tensor(f"out_{name}", shape, F32, kind="ExternalOutput").ap() for name, shape in _OUTS}
    decoder_layer(nc, ins, outs)
    r = _run(nc, [arrays], core_ids=[0])
    return tuple(r.results[0][f"out_{name}"] for name, _ in _OUTS)
```

```python
from collections import defaultdict
from contextlib import ExitStack

import concourse.bass as bass
import numpy as np
from concourse import mybir

F32 = mybir.dt.float32
F32R = mybir.dt.float32r
ALU = mybir.AluOpType
ACT = mybir.ActivationFunctionType
AX = mybir.AxisListType

P = 128
D = 1024
KT = D // P
SEQ, NB, TS = 1024, 8, 8
TSAMP = NB * TS
T = SEQ + TSAMP
CHUNKS = [(0, 384), (384, 384), (768, T - 768)]
NC = len(CHUNKS)
DFF = 2816
FG = DFF // (2 * P)
H, HD = 8, 64
WA = H * HD
CT = WA // P
CONVW = 31
PAD = CONVW - 1
NMEM, HX, HDX = 256, 4, 256
EPS = 1e-6
WBUF = 2048
OLD = WBUF - 512
OG, ORS = OLD // 16, 8
RR = 4
NKEY = OG * ORS + 512 + TS
NEG = -1.0e30
QT = SEQ // P
SLOTS = 4
LNB = (4, 6, 7)


def log_multiplicity(d):
    c = ((d <= 128).astype(np.float64) + ((d <= 512) & (d % 4 == 0)) + ((d <= 2048) & (d % 16 == 0))) * (d >= 0)
    return np.where(c > 0, np.log(np.maximum(c, 1.0)), NEG)


def prompt_bias():
    d = np.arange(P)[:, None] + (SEQ - P) - np.arange(SEQ)[None, :]
    slopes = 2.0 ** -(np.arange(H) + 1.0)
    b = 8.0 * (log_multiplicity(d)[None] - slopes[:, None, None] * d[None])
    return np.where(d[None] < 0, NEG, np.maximum(b, NEG)).astype(np.float32)


def sample_bias():
    old = np.arange(OG)[None, :] * 16 + np.arange(ORS)[:, None]
    recent = OLD + np.arange(P)[None, :] * RR + np.arange(RR)[:, None]
    pos = np.concatenate([old.ravel(), recent.ravel(), WBUF + np.arange(TS)])
    d = WBUF + np.arange(TS)[:, None] - pos[None, :]
    slopes = 2.0 ** -(np.arange(H) + 1.0)
    b = 8.0 * (log_multiplicity(d)[None] - slopes[:, None, None] * d[None])
    b = np.where(d[None] < 0, NEG, np.maximum(b, NEG)).reshape(H * TS, NKEY)
    return np.concatenate([b, b]).astype(np.float32)


def decoder_layer(nc, I, O):
    ctx = ExitStack()

    def sem(name):
        return ctx.enter_context(nc.semaphore(name))

    def alloc(stack, name, shape, dt=F32):
        return stack.enter_context(nc.sbuf_tensor(name, shape, dt))

    z = nc.dram_tensor("z_scratch", (20 * P, T), F32).ap()
    zx = nc.dram_tensor("zx_scratch", (KT * P, T), F32).ap()
    mix = nc.dram_tensor("mix_scratch", (KT * P, T), F32).ap()
    mixx = nc.dram_tensor("mixx_scratch", (KT * P, T), F32).ap()
    mkT = nc.dram_tensor("mkT_scratch", (KT * P, NMEM), F32).ap()

    x = alloc(ctx, "x", [P, KT, T])
    raw = alloc(ctx, "raw", [P, 2, KT, P])
    wh = alloc(ctx, "wh", [P, SLOTS, KT, P], F32R)
    wl = alloc(ctx, "wl", [P, SLOTS, KT, P], F32R)
    ident = alloc(ctx, "ident", [P, P])
    ones = alloc(ctx, "ones", [P, P])
    vecs = alloc(ctx, "vecs", [P, 60])
    taps = alloc(ctx, "taps", [P, CT, CONVW])
    G_FFN1, G_MIX, G_X, G_MEM, G_FFN2, G_FIN = (8 * j for j in range(6))
    V_CB, V_LG, V_LB = 48, 52, 56

    early = ExitStack()
    Us = alloc(early, "Us", [P, CT, NB, PAD + TS])
    with ExitStack() as g:
        hh = alloc(g, "hh", [P, KT, T], F32R)
        hl = alloc(g, "hl", [P, KT, T], F32R)
        sq = alloc(g, "sq", [P, 4, 384])
        tb = alloc(g, "tb", [P, 3, 384])
        rs = alloc(g, "rs", [P, NC, 384])
        with ExitStack() as f:
            bh = alloc(f, "bh", [P, 2, KT, P], F32R)
            bl = alloc(f, "bl", [P, 2, KT, P], F32R)
            hidh = alloc(f, "hidh", [P, 2, T], F32R)
            hidl = alloc(f, "hidl", [P, 2, T], F32R)
            sg = alloc(f, "sg", [P, 2, 384])
            ht = alloc(f, "ht", [P, 2, 384])
        with ExitStack() as f:
            xin = alloc(f, "xin", [P, 3, D])
            small = alloc(f, "small", [60, P])
            taps_in = alloc(f, "taps_in", [CONVW, WA])
            cc_in = alloc(f, "cc_in", [4 * PAD, 2, WA])
        with ExitStack() as f:
            stage = alloc(f, "stage", [P, 2, T])
        with ExitStack() as f:
            mixin = alloc(f, "mixin", [P, 3, T])
        with ExitStack() as f:
            ytok = alloc(f, "ytok", [P, 2, D])
    with ExitStack() as e:
        U = alloc(e, "U", [P, CT, T])
        ya = alloc(e, "ya", [P, CT, T])
        with ExitStack() as g:
            h3h = alloc(g, "h3h", [P, KT, T], F32R)
            h3l = alloc(g, "h3l", [P, KT, T], F32R)
            sq3 = alloc(g, "sq3", [P, 4, 384])
            tb3 = alloc(g, "tb3", [P, 3, 384])
            rs3 = alloc(g, "rs3", [P, NC, 384])
            stage3 = alloc(g, "stage3", [P, 2, T])
        with ExitStack() as g:
            min_ = alloc(g, "min_", [P, 2, D])
            memT = alloc(g, "memT", [P, KT, NMEM])
            mh = alloc(g, "mh", [P, KT, NMEM], F32R)
            ml = alloc(g, "ml", [P, KT, NMEM], F32R)
            msq = alloc(g, "msq", [P, 4, 384])
            mtb = alloc(g, "mtb", [P, 3, 384])
            mrs = alloc(g, "mrs", [P, NC, 384])
            kvT = alloc(g, "kvT", [P, KT, NMEM])
            kvtok = alloc(g, "kvtok", [P, 2, D])
            cct = alloc(g, "cct", [P, CT, 2, 4 * PAD])
            ucs = alloc(g, "ucs", [4 * PAD, 3, WA])
            mu = alloc(g, "mu", [P, NC, 384])
    early.close()
    with ExitStack() as g:
        qT = alloc(g, "qT", [P, 2, SEQ])
        kTp = alloc(g, "kTp", [P, 2, SEQ])
        vT = alloc(g, "vT", [P, 2, SEQ])
        pb = alloc(g, "pb", [P, 2, 2, SEQ])
        Sb = alloc(g, "Sb", [P, 3, SEQ])
        PT = alloc(g, "PT", [P, 2, QT, P])
        vtok = alloc(g, "vtok", [P, 2, QT, P])
        ktok = alloc(g, "ktok", [P, 2, QT, P])
        oT = alloc(g, "oT", [P, 2, SEQ])
        stat = alloc(g, "stat", [P, 4, 4])
        ks = alloc(g, "ks", [P, 2, CT, TSAMP])
        kvs = alloc(g, "kvs", [TSAMP, 2, WA])
    with ExitStack() as g:
        Ko = alloc(g, "Ko", [OG, 2, ORS, WA])
        Kr = alloc(g, "Kr", [P, 2, RR, WA])
        Vo = alloc(g, "Vo", [OG, 2, ORS, WA])
        Vr = alloc(g, "Vr", [P, 2, RR, WA])
        Vn = alloc(g, "Vn", [TS, 2, WA])
        Kc = alloc(g, "Kc", [P, CT, 512])
        Qc = alloc(g, "Qc", [P, 2, CT, H * TS])
        Qin = alloc(g, "Qin", [P, CT, 2 * TS])
        Knc = alloc(g, "Knc", [P, CT, 2 * TS])
        sbias = alloc(g, "sbias", [P, NKEY])
        Ss = alloc(g, "Ss", [P, NKEY])
        PTs = alloc(g, "PTs", [P, 13, P])
        sstat = alloc(g, "sstat", [P, 8])
        oS = alloc(g, "oS", [P, CT, NB, TS])
    with ExitStack() as g:
        xq = alloc(g, "xq", [P, 2, 2, SEQ])
        xk = alloc(g, "xk", [P, 2, 2, NMEM])
        xv = alloc(g, "xv", [P, 2, 2, HDX])
        Xb = alloc(g, "Xb", [P, 3, NMEM])
        XT = alloc(g, "XT", [P, 2, 2, P])
        xo = alloc(g, "xo", [P, 2, 2, SEQ])
        xstat = alloc(g, "xstat", [P, 4, 4])
        cq = alloc(g, "cq", [P, KT, TSAMP])
        cqc = alloc(g, "cqc", [P, 4, KT, HX * TS])
        cK = alloc(g, "cK", [P, 2, 2, D])
        cV = alloc(g, "cV", [P, 4, 2, D])
        cKT = alloc(g, "cKT", [P, KT, NMEM])
        cS = alloc(g, "cS", [P, NMEM])
        cPT = alloc(g, "cPT", [P, 2, P])
        cstat = alloc(g, "cstat", [P, 4])
        co = alloc(g, "co", [P, KT, NB, TS])

    ps = ctx.enter_context(nc.psum_tensor("ps", [P, 8, 512], F32))

    setup_done = sem("setup_done")
    raw_full = [sem("raw_full0"), sem("raw_full1")]
    w_hi = sem("w_hi")
    w_split = sem("w_split")
    unit_done = sem("unit_done")
    row_done = sem("row_done")
    met = sem("met")
    phase_end = sem("phase_end")

    OUT = O
    W = {n: I[n].rearrange("o (k p) n -> p (o k) n", p=P) for n in
         ("ffn1_gate", "ffn1_up", "ffn2_gate", "ffn2_up", "w_in", "w_out", "w_cq", "w_ck", "w_cv", "w_co")}
    DOWN = {n: I[n].rearrange("o f n -> (o f) n") for n in ("ffn1_down", "ffn2_down")}

    plan = [("ffn1", 6 * FG), ("w_in", 20), ("w_ck", 8), ("w_cv", 8), ("w_out", 8), ("w_cq", 8), ("w_co", 8),
            ("ffn2", 6 * FG)]
    UNIT, COL, ROW = {}, {}, {}
    u = c = r = 0
    for n, k in plan:
        UNIT[n], COL[n], ROW[n] = u, c, r
        u += k
        c += 4 * FG if n.startswith("ffn") else k
        r += 2 * FG if n.startswith("ffn") else 0

    class Sems:
        def __init__(self, tag, shared=None, base=None):
            self.tag, self.made, self.base = tag, {} if shared is None else shared, defaultdict(int, base or {})

        def __getitem__(self, n):
            if n not in self.made:
                self.made[n] = sem(f"{self.tag}_{n}")
            return self.made[n]

    S = {n: Sems(n) for n in ("mk", "conv", "pa", "sa", "xa", "xs")}

    def of_norm(nc_, split=True):
        return {"sqa": 4 * nc_, "sqd": 4 * nc_, "summed": KT * nc_, "var": nc_, "std": nc_, "rstd": nc_,
                "t": KT * nc_ * split, "hi": KT * nc_ * split, "h": KT * nc_}

    def of_proj(n, stored):
        return {"part": 2 * n, "free": 3 * n} | {f"st{w}": 8 * stored for w in range(2)}

    of_split = {"hi": KT, "h": KT, "in0": 48, "in1": 48, "in2": 32}
    of_ffn = {"gate": 4 * FG, "up": 4 * FG, "prod": 6 * FG, "res": NC * KT * FG, "sg": 6 * FG, "hhi": 6 * FG,
              "hid": 6 * FG, "down": (NC * KT - 1) * FG}
    shared, base = {}, defaultdict(int)
    for n, adds in (("load", {"in0": 48, "in1": 48, "in2": 48, "xt": 2 * (QT + 1)}), ("n1", of_norm(NC) | of_ffn),
                    ("nm", of_norm(NC) | of_proj(20, 12)), ("mem", of_norm(1)), ("so", of_split | of_proj(8, 0)),
                    ("nx", of_norm(NC) | of_proj(8, 8)), ("sc", of_split | of_proj(8, 0)),
                    ("n2", of_norm(NC) | of_ffn), ("fin", of_norm(NC, False))):
        S[n] = Sems("g", shared, base)
        for name, v in adds.items():
            base[name] += v
    block = ctx.enter_context(nc.Block())
    x_tok = I["x_prompt"].rearrange("b t d -> (b t) d")
    xs_tok = I["x_sample"].rearrange("b t d -> (b t) d")
    mem_tok = I["mem_prompt"].rearrange("b (t p) d -> p (b t) d", p=P)
    rows = [("ffn1_norm", G_FFN1, 8), ("mix_norm", G_MIX, 8), ("xattn_norm", G_X, 8), ("mem_norm", G_MEM, 8),
            ("ffn2_norm", G_FFN2, 8), ("final_norm", G_FIN, 8), ("conv_b", V_CB, 4), ("conv_ln_g", V_LG, 4),
            ("conv_ln_b", V_LB, 4)]
    cache_conv = I["cache_conv"].rearrange("o (a b) t c -> (b t) (o a) c", b=4)
    new_conv_s = OUT["new_conv_sample"].rearrange("o (a b) t c -> (b t) (o a) c", b=4)
    new_conv_p = OUT["new_conv_prompt"].rearrange("o b t c -> (o b t) c")
    win_p = {n: OUT[f"new_win_{n}_prompt"].rearrange("o b (t p) h e -> p (o b t) (h e)", p=P) for n in "kv"}
    win_s = {n: OUT[f"new_win_{n}_sample"].rearrange("o b t h e -> (o b t) (h e)") for n in "kv"}
    mem_o = {n: OUT[f"new_mem_{n}_prompt"].rearrange("o b (t p) h e -> p (o b t) (h e)", p=P) for n in "kv"}
    win_c = {n: I[f"cache_win_{n}"].rearrange("o b w h e -> (o b) w (h e)") for n in "kv"}
    mem_c = {n: I[f"cache_mem_{n}"].rearrange("o b (p j) h e -> (o b) p j (h e)", j=2) for n in "kv"}

    wsteps = [(p, h, t) for p in range(2) for h in range(2) for t in range(QT)]
    WN, WP = len(wsteps), len(wsteps) // 2
    xsteps = [(p, t) for p in range(2) for t in range(QT)]
    XN = len(xsteps)

    def turns(n):
        p, h, t = wsteps[n]
        own = [("p", c) for c in range(1 + (t >= 4))]
        early = {WP - 2: [("v", 0), ("v", 1)], WP - 1: [("k", 0), ("k", 1)]}
        return early.get(n, []) + own

    WT = 4 + sum(len(turns(n)) for n in range(WN))

    def sq_slot(k):
        return 2 * (k % 2) + k // 2 % 2

    def barrier(eng, n):
        eng.drain().then_inc(phase_end, 1)
        eng.wait_ge(phase_end, 3 * n)

    @block.sync
    def _(sp):
        def load_unit(parity, split_needed, src, dst=None):
            sp.wait_ge(w_split, split_needed)
            sp.dma_start(raw[:, parity] if dst is None else dst, src).then_inc(raw_full[parity], 16)

        def ffn_loads(name):
            u0 = UNIT[name]
            gate, up, down = W[f"{name}_gate"], W[f"{name}_up"], DOWN[f"{name}_down"]
            with sp.Fori(0, FG) as i:
                for j in range(6):
                    if j < 4:
                        src = (gate, up)[j % 2][:, :, bass.ds(i * (2 * P) + (j // 2) * P, P)]
                        dst = None
                    else:
                        src = down[bass.ds(i * (2 * P) + (j - 4) * P, P), :]
                        dst = raw[:, j % 2].rearrange("p k n -> p (k n)")
                    load_unit(j % 2, i * 6 + (u0 + j + 1), src, dst)

        def col_loads(name):
            u0 = UNIT[name]
            n = dict(plan)[name]
            with sp.Fori(0, n // 4) as i:
                for j in range(4):
                    load_unit(j % 2, i * 4 + (u0 + j + 1), W[name][:, :, bass.ds(i * (4 * P) + j * P, P)])

        def in_loads():
            u0 = UNIT["w_in"]
            with sp.Fori(0, CT // 2) as i:
                for j in range(4):
                    load_unit(j % 2, i * 4 + (u0 + j + 1),
                              W["w_in"][:, :, bass.ds(i * (2 * P) + (3 * CT + j // 2 + CT * (j % 2)) * P, P)])
            with sp.Fori(0, 3 * CT // 4) as i:
                for j in range(4):
                    load_unit(j % 2, i * 4 + (u0 + 2 * CT + j + 1), W["w_in"][:, :, bass.ds(i * (4 * P) + j * P, P)])

        L = S["load"]
        for name, c0, n in rows:
            v = I[name]
            v = v.rearrange("(k p) -> k p", p=P) if name == "final_norm" else v.rearrange("o (k p) -> (o k) p", p=P)
            sp.dma_start(small[c0:c0 + n, :], v).then_inc(L["small"], 16)
        sp.dma_start(taps_in[:], I["conv_w"].rearrange("o t c -> (o t) c")).then_inc(L["small"], 16)
        for t in range(QT + 1):
            if t >= 3:
                sp.wait_ge(L["xin_free"], L.base["xin_free"] + 2 * (t - 2))
            n = P if t < QT else TSAMP
            src = x_tok[t * P:t * P + n, :] if t < QT else xs_tok
            sp.dma_start(xin[0:n, t % 3, :], src).then_inc(L[f"in{t % 3}"], 16)
        sp.dma_start(cc_in[:], cache_conv).then_inc(S["conv"]["cc_in"], 16)
        ffn_loads("ffn1")
        in_loads()
        sp.wait_ge(phase_end, 3 * 3)
        sp.dma_start(min_[:], mem_tok).then_inc(S["mem"]["in"], 16)
        col_loads("w_ck")
        col_loads("w_cv")
        A = S["pa"]
        sp.wait_ge(phase_end, 3 * 4)
        for a in range(2):
            sp.dma_start(ks[:, a], z[(1 + a) * CT * P:(2 + a) * CT * P, SEQ:T].rearrange("(k p) t -> p k t", p=P)
                         ).then_inc(A["tok_in"], 16)
        with sp.Fori(0, H // 4) as i:
            for p in range(2):
                sp.wait_ge(A["s_full"], i * WN + WP * (p + 1))
                for dst, r0 in ((vT, 2 * CT), (kTp, CT), (qT, 0)):
                    sp.dma_start(dst[:, p], z[bass.ds(i * (2 * P) + (r0 + p) * P, P), 0:SEQ]).then_inc(A[f"in{p}"], 16)
                sp.wait_ge(A["s_free"], i * WN + WP * (p + 1))
                sp.dma_start(pb[:, p], I["prompt_bias"][bass.ds(i * 4 + 2 * p, 2), :, :].rearrange("h p n -> p h n")
                             ).then_inc(A[f"in{p}"], 16)
        B = S["sa"]
        sp.wait_ge(phase_end, 3 * 5)
        sp.dma_start(sbias[:], I["sample_bias"]).then_inc(B["bias"], 16)

        def rows_of(n, b):
            c = win_c[n][bass.ds(b, 1), :, :].rearrange("b w e -> (b w) e")
            old = c[0:OLD, :].rearrange("(g s) e -> g s e", s=16)[:, 0:ORS, :]
            return old, c[OLD:WBUF, :].rearrange("(p r) e -> p r e", r=RR)

        with sp.Fori(0, NB // 2) as i:
            for b in range(2):
                old, recent = rows_of("k", i * 2 + b)
                sp.wait_ge(B["s_full"], i * 2 + (b + 1))
                sp.dma_start(Ko[:, b], old).then_inc(B[f"k{b}"], 16)
                sp.dma_start(Kr[:, b], recent).then_inc(B[f"k{b}"], 16)
            sp.wait_ge(B["s_full"], i * 2 + 2)
            for dst, r0 in ((Qin, 0), (Knc, CT)):
                sp.dma_start(dst[:], z[r0 * P:(r0 + CT) * P, bass.ds(i * (2 * TS) + SEQ, 2 * TS)
                                       ].rearrange("(k p) t -> p k t", p=P)).then_inc(B["qk_in"], 16)
            for b in range(2):
                old, recent = rows_of("v", i * 2 + b)
                sp.wait_ge(B["v_used"], i * 2 + (b + 1))
                sp.dma_start(Vo[:, b], old).then_inc(B[f"v{b}"], 16)
                sp.dma_start(Vr[:, b], recent).then_inc(B[f"v{b}"], 16)
            sp.dma_start(Vn[:], win_s["v"][bass.ds(i * (2 * TS), 2 * TS), :].rearrange("(b t) e -> t b e", b=2)
                         ).then_inc(B["vn"], 16)
        M = S["so"]
        sp.wait_ge(phase_end, 3 * 6)
        for k in range(KT):
            if k >= 3:
                sp.wait_ge(M["h"], M.base["h"] + k - 2)
            sp.dma_start(mixin[:, k % 3], mix[k * P:(k + 1) * P, :]).then_inc(M[f"in{k % 3}"], 16)
        col_loads("w_out")
        col_loads("w_cq")
        X = S["xa"]
        sp.wait_ge(phase_end, 3 * 8)
        with sp.Fori(0, HX // 2) as i:
            for p in range(2):
                sp.wait_ge(X["o_full"], i * XN + QT * (p + 1))
                sp.dma_start(xq[:, p], zx[bass.ds(i * (2 * HDX) + p * HDX, HDX), 0:SEQ]
                             .rearrange("(k p) t -> p k t", p=P)).then_inc(X[f"in{p}"], 16)
                sp.dma_start(xk[:, p], mkT[bass.ds(i * (2 * HDX) + p * HDX, HDX), :]
                             .rearrange("(k p) t -> p k t", p=P)).then_inc(X[f"in{p}"], 16)
                sp.dma_start(xv[:, p], mem_o["v"][:, :, bass.ds(i * (2 * HDX) + p * HDX, HDX)]
                             ).then_inc(X[f"in{p}"], 16)
        Y = S["xs"]
        sp.dma_start(cq[:], zx[:, SEQ:T].rearrange("(k p) t -> p k t", p=P)).then_inc(Y["q_in"], 16)
        with sp.Fori(0, 2) as i:
            for b in range(4):
                sp.wait_ge(Y["s_full"], i * 4 + (b + 1))
                sp.dma_start(cK[:, b % 2], mem_c["k"][bass.ds(i * 4 + b, 1)].rearrange("b p j e -> p (b j) e")
                             ).then_inc(Y[f"k{b % 2}"], 16)
            sp.wait_ge(Y["o_full"], i + 1)
            sp.dma_start(cV[:].rearrange("p b j e -> p b (j e)"),
                         mem_c["v"][bass.ds(i * 4, 4)].rearrange("b p j e -> p b (j e)")).then_inc(Y["v"], 16)
        M = S["sc"]
        sp.wait_ge(phase_end, 3 * 9)
        for k in range(KT):
            if k >= 3:
                sp.wait_ge(M["h"], M.base["h"] + k - 2)
            sp.dma_start(mixin[:, k % 3], mixx[k * P:(k + 1) * P, :]).then_inc(M[f"in{k % 3}"], 16)
        col_loads("w_co")
        ffn_loads("ffn2")
        F = S["fin"]
        yp = OUT["y_prompt"].rearrange("b t d -> (b t) d")
        for t in range(QT + 1):
            n = P if t < QT else TSAMP
            sp.wait_ge(F["tok"], F.base["tok"] + 2 * (t + 1))
            dst = yp[t * P:t * P + n, :] if t < QT else OUT["y_sample"].rearrange("b t d -> (b t) d")
            sp.dma_start(dst, ytok[0:n, t % 2, :]).then_inc(F[f"out{t % 2}"], 16)
        sp.wait_ge(F["out0"], F.base["out0"] + 16 * ((QT + 2) // 2))
        sp.wait_ge(F["out1"], F.base["out1"] + 16 * ((QT + 1) // 2))

    @block.gpsimd
    def _(pool):
        pool.memset(ident[:], 0.0).then_inc(setup_done, 1)
        pool.memset(ones[:], 1.0).then_inc(setup_done, 1)
        pool.wait_ge(setup_done, 1)
        pool.affine_select(out=ident[:], in_=ident[:], compare_op=ALU.not_equal, fill=1.0, base=0,
                           pattern=[[-1, P]], channel_multiplier=1).then_inc(setup_done, 1)
        pool.sem_inc(w_split, 2)

        def split(parity, full, m, hi, lo, slot_sem, slot_need):
            pool.wait_ge(raw_full[parity], full)
            pool.wait_ge(slot_sem, slot_need)
            pool.sem_inc(met, 1)
            pool.tensor_copy(hi, raw[:, parity]).then_inc(w_hi, 1)
            pool.wait_ge(w_hi, m + 1)
            pool.tensor_tensor(lo, raw[:, parity], hi.bitcast(F32), ALU.subtract).then_inc(w_split, 1)

        def ffn_split(name, phase):
            u0, c0, r0 = UNIT[name], COL[name], ROW[name]
            with pool.Fori(0, FG) as i:
                for j in range(6):
                    full = i * 48 + 16 * ((u0 + j) // 2 + 1)
                    if j < 4:
                        split(j % 2, full, i * 6 + (u0 + j), wh[:, j], wl[:, j], unit_done, i * 4 + (c0 + j + 1))
                    else:
                        pool.wait_ge(phase_end, 3 * phase)
                        split(j % 2, full, i * 6 + (u0 + j), bh[:, j - 4], bl[:, j - 4], row_done,
                              i * 2 + (r0 + j - 4 + 1))

        def col_split(name, n):
            u0, c0 = UNIT[name], COL[name]
            with pool.Fori(0, n // 4) as i:
                for j in range(4):
                    split(j % 2, i * 32 + 16 * ((u0 + j) // 2 + 1), i * 4 + (u0 + j), wh[:, j], wl[:, j],
                          unit_done, i * 4 + (c0 + j + 1))

        for name, n in plan:
            if name.startswith("ffn"):
                ffn_split(name, {"ffn1": 1, "ffn2": 10}[name])
            else:
                col_split(name, n)

    @block.tensor
    def _(pe):
        pe.sem_inc(unit_done, SLOTS)
        pe.sem_inc(row_done, 2)
        pe.wait_ge(setup_done, 3)

        def three(out, w_hi_, w_lo_, a_hi, a_lo, first, last):
            pe.matmul(out, w_hi_, a_hi, start=first, stop=False)
            pe.matmul(out, w_lo_, a_hi, start=False, stop=False)
            return pe.matmul(out, w_hi_, a_lo, start=False, stop=last)

        def norm(s, chunks, sqt):
            for c, (c0, n) in enumerate(chunks):
                for k in range(KT):
                    pe.wait_ge(s[("sqa", "sqd")[k % 2]], s.base[("sqa", "sqd")[k % 2]] + c * (KT // 2) + k // 2 + 1)
                    pe.matmul(ps[:, 5 + c, 0:n], ones[:], sqt[:, sq_slot(k), 0:n], start=(k == 0),
                              stop=(k == KT - 1)).then_inc(s["summed"], 1)

        def ffn(name, s):
            u0, c0_, r0 = UNIT[name], COL[name], ROW[name]
            with pe.Fori(0, FG) as i:
                for f in range(2):
                    for c, (c0, n) in enumerate(CHUNKS):
                        j = NC * f + c
                        if f == 0:
                            pe.wait_ge(s["h"], s.base["h"] + KT * (c + 1))
                        pe.wait_ge(s["prod"], s.base["prod"] + i * 6 + (j + 1))
                        for gu in range(2):
                            if c == 0:
                                pe.wait_ge(w_split, i * 6 + (u0 + 2 * f + gu + 3))
                            out = ps[:, 2 * (j % 2) + gu, 0:n]
                            w = 2 * f + gu
                            for k in range(KT):
                                mm = three(out, wh[:, w, k], wl[:, w, k], hh[:, k, c0:c0 + n], hl[:, k, c0:c0 + n],
                                           k == 0, k == KT - 1)
                            if c < NC - 1:
                                mm.then_inc(s[("gate", "up")[gu]], 1)
                            else:
                                mm.then_inc(unit_done, 1)
                pe.wait_ge(w_split, i * 6 + (u0 + 8))
                for c, (c0, n) in enumerate(CHUNKS):
                    pe.wait_ge(s["hid"], s.base["hid"] + i * 6 + (NC + c + 2))
                    for d in range(KT):
                        j = c * KT + d
                        pe.wait_ge(s["res"], s.base["res"] + i * (NC * KT) + (j + 1))
                        out = ps[:, 4 + j % 4, 0:n]
                        for f in range(2):
                            mm = three(out, bh[:, f, d], bl[:, f, d], hidh[:, f, c0:c0 + n], hidl[:, f, c0:c0 + n],
                                       f == 0, f == 1)
                        if j < NC * KT - 1:
                            mm.then_inc(s["down"], 1)
                        else:
                            mm.then_inc(row_done, 2)

        def proj(name, s, nunits, chunks, ah, al, h_need):
            u0 = UNIT[name]
            nc_ = len(chunks)
            with pe.Fori(0, nunits // 4) as i:
                for w in range(4):
                    pe.wait_ge(w_split, i * 4 + (u0 + w + 3))
                    for c, (c0, n) in enumerate(chunks):
                        j = w * nc_ + c
                        if w == 0:
                            pe.wait_ge(s["h"], s.base["h"] + h_need(c))
                        pe.wait_ge(s["free"], s.base["free"] + i * (4 * nc_) + (j + 1))
                        out = ps[:, j % 4, 0:n]
                        for k in range(KT):
                            mm = three(out, wh[:, w, k], wl[:, w, k], ah[:, k, c0:c0 + n], al[:, k, c0:c0 + n],
                                       k == 0, k == KT - 1)
                        mm.then_inc(s["part"] if c < nc_ - 1 else unit_done, 1)

        L = S["load"]
        pe.wait_ge(L["small"], L.base["small"] + 16 * 10)
        pe.transpose(ps[:, 0, 0:60], small[:], ident[0:60, 0:60])
        for k in range(CT):
            mm = pe.transpose(ps[:, 1, k * CONVW:(k + 1) * CONVW], taps_in[:, k * P:(k + 1) * P],
                              ident[0:CONVW, 0:CONVW])
        mm.then_inc(L["vecs_t"], 1)
        for t in range(QT + 1):
            n = P if t < QT else TSAMP
            pe.wait_ge(L[f"in{t % 3}"], L.base[f"in{t % 3}"] + 16 * (t // 3 + 1))
            for h in range(2):
                j = 2 * t + h
                if j >= 4:
                    pe.wait_ge(L["xin_free"], L.base["xin_free"] + j - 3)
                for k in range(4):
                    kk = 4 * h + k
                    mm = pe.transpose(ps[:, 2 + j % 4, k * P:k * P + n], xin[0:n, t % 3, kk * P:(kk + 1) * P],
                                      ident[0:n, 0:n])
                mm.then_inc(L["xt"], 1)
        C = S["conv"]
        pe.wait_ge(C["cc_in"], 16)
        for k in range(CT):
            for a in range(2):
                mm = pe.transpose(ps[:, 6 + k // 2, ((k % 2) * 2 + a) * 120:((k % 2) * 2 + a) * 120 + 120],
                                  cc_in[:, a, k * P:(k + 1) * P], ident[0:120, 0:120])
        mm.then_inc(C["cct"], 1)
        barrier(pe, 1)
        norm(S["n1"], CHUNKS, sq)
        ffn("ffn1", S["n1"])
        barrier(pe, 2)
        norm(S["nm"], CHUNKS, sq3)
        proj("w_in", S["nm"], 20, CHUNKS, h3h, h3l, lambda c: KT * (c + 1))
        barrier(pe, 3)
        M, C = S["mem"], S["conv"]
        pe.wait_ge(M["in"], M.base["in"] + 16)
        for t in range(2):
            for h in range(2):
                for k in range(4):
                    kk = 4 * h + k
                    mm = pe.transpose(ps[:, 2 * t + h, k * P:(k + 1) * P], min_[:, t, kk * P:(kk + 1) * P], ident[:])
                mm.then_inc(M["xt"], 1)
        for k in range(CT):
            pe.wait_ge(C["ug"], k + 1)
            if k >= 1:
                pe.wait_ge(C["ucs"], 2 * k)
            pe.transpose(ps[0:PAD, 4, 0:P], U[:, k, SEQ:SEQ + PAD], ident[:])
            for a in range(2):
                mm = pe.transpose(ps[0:120, 4, (a + 1) * P:(a + 2) * P], cct[:, k, a, :], ident[:])
            mm.then_inc(C["ut"], 1)
        norm(M, [(0, NMEM)], msq)
        pe.wait_ge(C["ucs"], 2 * CT)
        for c, (c0, n) in enumerate(CHUNKS):
            for k in range(CT):
                mm = pe.matmul(ps[:, LNB[c], 0:n], ones[:], ya[:, k, c0:c0 + n], start=(k == 0), stop=(k == CT - 1))
            mm.then_inc(C["mean"], 1)
        for name, n in (("w_ck", "mk"), ("w_cv", "mv")):
            s = S["mk"]
            u0 = UNIT[name]
            with pe.Fori(0, 2) as i:
                for w in range(4):
                    pe.wait_ge(w_split, i * 4 + (u0 + w + 3))
                    pe.wait_ge(M["h"], M.base["h"] + KT)
                    pe.wait_ge(s[n + "_free"], s.base[n + "_free"] + i * 4 + (w + 1))
                    for k in range(KT):
                        mm = three(ps[:, w, 0:NMEM], wh[:, w, k], wl[:, w, k], mh[:, k], ml[:, k], k == 0, k == KT - 1)
                    mm.then_inc(unit_done, 1)
            for t in range(2):
                for h in range(2):
                    j = 2 * t + h
                    pe.wait_ge(s[n + "_free"], s.base[n + "_free"] + 12)
                    for k in range(4):
                        kk = 4 * h + k
                        mm = pe.transpose(ps[:, j, k * P:(k + 1) * P], kvT[:, kk, t * P:(t + 1) * P], ident[:])
                    mm.then_inc(s[n + "_t"], 1)
            if n == "mk":
                for c, (c0, w) in enumerate(CHUNKS):
                    for k in range(CT):
                        pe.wait_ge(C["sq"], c * CT + k + 1)
                        mm = pe.matmul(ps[:, LNB[c], 0:w], ones[:], U[:, k, c0:c0 + w], start=(k == 0),
                                       stop=(k == CT - 1))
                    mm.then_inc(C["summed"], 1)
            pe.wait_ge(s[n + "_tok"], s.base[n + "_tok"] + 4)
        barrier(pe, 4)
        A = S["pa"]
        pe.sem_inc(A["s_full"], WN)
        pe.wait_ge(A["tok_in"], 32)
        for a in range(2):
            for k in range(CT):
                mm = pe.transpose(ps[0:TSAMP, 6 + a, k * P:(k + 1) * P], ks[:, a, k, :], ident[:])
            mm.then_inc(A["tok_t"], 1)
        pe.wait_ge(A["tok_e"], 2)
        with pe.Fori(0, H // 4) as i:
            tf = [0]
            upto = {}

            def tbank():
                b = 4 + tf[0] % 2
                pe.wait_ge(A["t_free"], i * WT + (tf[0] + 1))
                tf[0] += 1
                return b

            def tokens(src, p, half):
                b = tbank()
                for k in range(4):
                    mm = pe.transpose(ps[:, b, k * P:(k + 1) * P], src[:, p, (4 * half + k) * P:(4 * half + k + 1) * P],
                                      ident[:])
                mm.then_inc(A["t_full"], 1)

            def scores(n):
                p, h, t = wsteps[n]
                if n % WP == 0:
                    pe.wait_ge(A[f"in{p}"], i * 64 + 64)
                pe.wait_ge(A["s_free"], i * WN + (WN + n - 1))
                for c in range(1 + (t >= 4)):
                    w = min(512, P * (t + 1) - 512 * c)
                    mm = pe.matmul(ps[:, 2 * (n % 2) + c, 0:w], qT[64 * h:64 * h + 64, p, t * P:(t + 1) * P],
                                   kTp[64 * h:64 * h + 64, p, 512 * c:512 * c + w], start=True, stop=True)
                mm.then_inc(A["s_full"], 1)

            def turn(n):
                p, h, t = wsteps[n]
                for kind, c in turns(n):
                    if kind != "p":
                        tokens(vT if kind == "v" else kTp, 1, c)
                        continue
                    if c == 0:
                        pe.wait_ge(A["p"], i * WN + (n + 1))
                    b = tbank()
                    for k in range(4 * c, min(4 * c + 4, t + 1)):
                        mm = pe.transpose(ps[:, b, (k % 4) * P:(k % 4 + 1) * P], Sb[:, n % 3, k * P:(k + 1) * P],
                                          ident[:])
                    mm.then_inc(A["t_full"], 1)
                upto[n] = tf[0]

            def values(n):
                p, h, t = wsteps[n]
                pe.wait_ge(A["t_free"], i * WT + (upto[n] + 2))
                pe.wait_ge(A["o_free"], i * WN + (n + 1))
                for k in range(t + 1):
                    mm = pe.matmul(ps[64 * h:64 * h + 64, 6 + n % 2, 0:P], vtok[:, p, k, 64 * h:64 * h + 64],
                                   PT[:, n % 2, k, :], start=(k == 0), stop=(k == t))
                mm.then_inc(A["o_full"], 1)

            scores(0)
            scores(1)
            for src in (vT, kTp):
                for half in range(2):
                    tokens(src, 0, half)
            for n in range(WN):
                if n + 2 < WN:
                    scores(n + 2)
                turn(n)
                if n >= 1:
                    values(n - 1)
            values(WN - 1)
        barrier(pe, 5)
        B = S["sa"]
        pe.sem_inc(B["s_full"], 2)
        pe.sem_inc(B["v_used"], 2)
        pe.sem_inc(B["s_part"], 1)
        with pe.Fori(0, NB // 2) as i:
            pe.wait_ge(B["q"], i * 16 + 16)
            for b, c in [(b, c) for b in range(2) for c in range(3)]:
                if c == 0:
                    pe.wait_ge(B[f"k{b}"], i * 32 + 32)
                j = b * 3 + c
                for k in range(CT):
                    pe.wait_ge(B[("t_freea", "t_freed")[k % 2]], i * 12 + (2 * j + k // 2 + 1))
                    for r in range(4):
                        if c < 2:
                            src, w = Ko[:, b, 4 * c + r, k * P:(k + 1) * P], OG
                        else:
                            src, w = Kr[:, b, r, k * P:(k + 1) * P], P
                        mm = pe.transpose(ps[:, k % 2, r * w:(r + 1) * w], src, ident[0:w, 0:w])
                    mm.then_inc(B["t_full"], 1)
                if j == 0:
                    pe.wait_ge(B["s_free"], i + 1)
                pe.wait_ge(B["t_freea"], i * 12 + (2 * j + 3))
                pe.wait_ge(B["t_freed"], i * 12 + (2 * j + 3))
                w = 4 * (OG if c < 2 else P)
                for k in range(CT):
                    mm = pe.matmul(ps[64 * b:64 * b + 64, 2 + c, 0:w], Qc[:, b, k, :], Kc[:, k, 0:w],
                                   start=(k == 0), stop=(k == CT - 1))
                mm.then_inc(B["s_part"], 1)
                if c == 2:
                    for k in range(CT):
                        mm = pe.matmul(ps[64 * b:64 * b + 64, 5, 0:TS], Qc[:, b, k, :],
                                       Knc[:, k, b * TS:(b + 1) * TS], start=(k == 0), stop=(k == CT - 1))
                    mm.then_inc(B["s_full"], 1)
            pe.wait_ge(B["p"], i + 1)
            for g_ in range(4):
                if g_ >= 2:
                    pe.wait_ge(B[("pt_a", "pt_d")[g_ % 2]], i * 2 + 1)
                for r in range(4 if g_ < 3 else 1):
                    blk = 4 * g_ + r
                    w = OG if blk < ORS else (P if blk < 12 else TS)
                    off = blk * OG if blk < ORS else ORS * OG + (blk - ORS) * P
                    mm = pe.transpose(ps[0:w, g_ % 2, r * P:(r + 1) * P], Ss[:, off:off + w], ident[:])
                mm.then_inc(B["pt_full"], 1)
            pe.wait_ge(B["pt_a"], i * 2 + 2)
            pe.wait_ge(B["pt_d"], i * 2 + 2)
            pe.wait_ge(B["vn"], i * 16 + 16)
            pe.wait_ge(B["o_free"], i * 2 + 1)
            for b in range(2):
                pe.wait_ge(B[f"v{b}"], i * 32 + 32)
                for k in range(CT):
                    for blk in range(13):
                        if blk < ORS:
                            v, w = Vo[:, b, blk, k * P:(k + 1) * P], OG
                        elif blk < 12:
                            v, w = Vr[:, b, blk - ORS, k * P:(k + 1) * P], P
                        else:
                            v, w = Vn[:, b, k * P:(k + 1) * P], TS
                        mm = pe.matmul(ps[:, 6, (b * CT + k) * 16:(b * CT + k) * 16 + 16], v,
                                       PTs[0:w, blk, b * 64 + k * 16:b * 64 + k * 16 + 16],
                                       start=(blk == 0), stop=(blk == 12))
                mm.then_inc(B["v_used"], 1)
        barrier(pe, 6)
        proj("w_out", S["so"], 8, CHUNKS, hh, hl, lambda c: KT)
        barrier(pe, 7)
        norm(S["nx"], CHUNKS, sq)
        proj("w_cq", S["nx"], 8, CHUNKS, hh, hl, lambda c: KT * (c + 1))
        barrier(pe, 8)
        X = S["xa"]
        pe.sem_inc(X["o_full"], XN)
        with pe.Fori(0, HX // 2) as i:
            def xscores(n):
                p, t = xsteps[n]
                if t == 0:
                    pe.wait_ge(X[f"in{p}"], i * 48 + 48)
                pe.wait_ge(X["e"], i * XN + (n + 1))
                for k in range(2):
                    mm = pe.matmul(ps[:, n % 2, 0:NMEM], xq[:, p, k, t * P:(t + 1) * P], xk[:, p, k, :],
                                   start=(k == 0), stop=(k == 1))
                mm.then_inc(X["s_full"], 1)

            def xturn(n):
                pe.wait_ge(X["p"], i * XN + (n + 1))
                pe.wait_ge(X["t_free"], i * XN + (n + 1))
                for k in range(2):
                    mm = pe.transpose(ps[:, 2 + n % 2, k * P:(k + 1) * P], Xb[:, n % 3, k * P:(k + 1) * P], ident[:])
                mm.then_inc(X["t_full"], 1)

            def xvalues(n):
                p, t = xsteps[n]
                pe.wait_ge(X["t_free"], i * XN + (n + 3))
                pe.wait_ge(X["o_free"], i * XN + (n + 1))
                for d in range(2):
                    for k in range(2):
                        mm = pe.matmul(ps[:, 4 + n % 2, d * P:(d + 1) * P], xv[:, p, k, d * P:(d + 1) * P],
                                       XT[:, n % 2, k, :], start=(k == 0), stop=(k == 1))
                mm.then_inc(X["o_full"], 1)

            xscores(0)
            xscores(1)
            for n in range(XN):
                if n + 2 < XN:
                    xscores(n + 2)
                xturn(n)
                if n >= 1:
                    xvalues(n - 1)
            xvalues(XN - 1)
        Y = S["xs"]
        pe.sem_inc(Y["s_full"], 2)
        pe.sem_inc(Y["o_full"], 1)
        with pe.Fori(0, 2) as i:
            for b in range(4):
                pe.wait_ge(Y[f"k{b % 2}"], i * 32 + 16 * (b // 2 + 1))
                for m in range(4):
                    pe.wait_ge(Y[("t_freea", "t_freed")[m % 2]], i * 8 + (b * 2 + m // 2 + 1))
                    for k in range(2):
                        for j in range(2):
                            mm = pe.transpose(ps[:, m % 2, k * 256 + j * P:k * 256 + (j + 1) * P],
                                              cK[:, b % 2, j, (2 * m + k) * P:(2 * m + k + 1) * P], ident[:])
                    mm.then_inc(Y["t_full"], 1)
                pe.wait_ge(Y["t_freea"], i * 8 + (b * 2 + 3))
                pe.wait_ge(Y["t_freed"], i * 8 + (b * 2 + 3))
                if b == 0:
                    pe.wait_ge(Y["qc"], i * 4 + 4)
                    pe.wait_ge(Y["e"], i + 1)
                for k in range(KT):
                    mm = pe.matmul(ps[32 * b:32 * b + 32, 2, 0:NMEM], cqc[:, b, k, :], cKT[:, k, :], start=(k == 0),
                                   stop=(k == KT - 1))
                mm.then_inc(Y["s_full"], 1)
            pe.wait_ge(Y["p"], i + 1)
            for j in range(2):
                mm = pe.transpose(ps[:, 3, j * P:(j + 1) * P], cS[:, j * P:(j + 1) * P], ident[:])
            mm.then_inc(Y["pt_full"], 1)
            pe.wait_ge(Y["pt"], i + 1)
            pe.wait_ge(Y["v"], i * 16 + 16)
            pe.wait_ge(Y["oe"], i + 1)
            for b in range(4):
                for k in range(KT):
                    for j in range(2):
                        mm = pe.matmul(ps[:, 4, (k * 4 + b) * TS:(k * 4 + b + 1) * TS],
                                       cV[:, b, j, k * P:(k + 1) * P],
                                       cPT[:, j, b * 32 + (k // 2) * TS:b * 32 + (k // 2) * TS + TS],
                                       start=(j == 0), stop=(j == 1))
            mm.then_inc(Y["o_full"], 1)
        barrier(pe, 9)
        proj("w_co", S["sc"], 8, CHUNKS, hh, hl, lambda c: KT)
        barrier(pe, 10)
        norm(S["n2"], CHUNKS, sq)
        ffn("ffn2", S["n2"])
        barrier(pe, 11)
        F = S["fin"]
        norm(F, CHUNKS, sq)
        for t in range(QT + 1):
            n = P if t < QT else TSAMP
            pe.wait_ge(F["h"], F.base["h"] + KT * ([c for c, (c0, w) in enumerate(CHUNKS) if t * P < c0 + w][0] + 1))
            for h in range(2):
                j = 2 * t + h
                if j >= 4:
                    pe.wait_ge(F["tok"], F.base["tok"] + j - 3)
                for k in range(4):
                    mm = pe.transpose(ps[0:n, j % 4, k * P:(k + 1) * P], x[:, 4 * h + k, t * P:t * P + n], ident[:])
                mm.then_inc(F["yt"], 1)

    @block.scalar
    def _(act):
        def squares(s, chunks, src, sqt):
            for c, (c0, n) in enumerate(chunks):
                for k in range(0, KT, 2):
                    j = c * KT + k
                    if j >= 4:
                        act.wait_ge(s["summed"], s.base["summed"] + j - 3)
                    act.activation(sqt[:, sq_slot(k), 0:n], src[:, k, c0:c0 + n], ACT.Square).then_inc(s["sqa"], 1)

        def roots(s, chunks, rst):
            for c, (c0, n) in enumerate(chunks):
                act.wait_ge(s["var"], s.base["var"] + c + 1)
                act.activation(rst[:, c, 0:n], rst[:, c, 0:n], ACT.Sqrt).then_inc(s["std"], 1)

        def norm(s, chunks, src, sqt, rst, tbt, hit):
            squares(s, chunks, src, sqt)
            roots(s, chunks, rst)
            for c, (c0, n) in enumerate(chunks):
                for k in range(KT):
                    j = c * KT + k
                    act.wait_ge(s["t"], s.base["t"] + j + 1)
                    act.copy(hit[:, k, c0:c0 + n], tbt[:, j % 3, 0:n]).then_inc(s["hi"], 1)

        def ffn(name, s):
            c0_ = COL[name]
            with act.Fori(0, FG) as i:
                def silu(j):
                    f, c = divmod(j, NC)
                    n = CHUNKS[c][1]
                    if c < NC - 1:
                        act.wait_ge(s["gate"], s.base["gate"] + i * 4 + (2 * f + c + 1))
                    else:
                        act.wait_ge(unit_done, i * 4 + (SLOTS + c0_ + 2 * f + 1))
                    act.wait_ge(s["prod"], s.base["prod"] + i * 6 + (j + 1))
                    act.activation(sg[:, j % 2, 0:n], ps[:, 2 * (j % 2), 0:n], ACT.Silu).then_inc(s["sg"], 1)

                def hi(j):
                    f, c = divmod(j, NC)
                    c0, n = CHUNKS[c]
                    act.wait_ge(s["prod"], s.base["prod"] + i * 6 + (j + 3))
                    act.copy(hidh[:, f, c0:c0 + n], ht[:, j % 2, 0:n]).then_inc(s["hhi"], 1)

                for j in range(2 * NC):
                    silu(j)
                    if j >= 1:
                        hi(j - 1)
                hi(2 * NC - 1)

        def store_proj(name, s, stg, nunits, first, dst):
            with act.Fori(0, nunits // 4) as i:
                for w in range(4):
                    act.wait_ge(s[f"st{w % 2}"], s.base[f"st{w % 2}"] + i * 32 + 16 * (w // 2 + 1))
                    for c, (c0, n) in enumerate(CHUNKS):
                        j = w * NC + c
                        if c < NC - 1:
                            act.wait_ge(s["part"], s.base["part"] + i * 8 + (2 * (first + w) + c + 1))
                        else:
                            act.wait_ge(unit_done, i * 4 + (SLOTS + COL[name] + first + w + 1))
                        act.copy(stg[:, w % 2, c0:c0 + n], ps[:, j % 4, 0:n]).then_inc(s["free"], 1)
                    act.wait_ge(s["free"], s.base["free"] + i * 12 + (4 + NC * (first + w + 1)))
                    act.dma_start(dst[bass.ds(i * (4 * P) + w * P, P), :], stg[:, w % 2, :]
                                  ).then_inc(s[f"st{w % 2}"], 16)
            for w in range(2):
                act.wait_ge(s[f"st{w}"], s.base[f"st{w}"] + 8 * nunits + 16)

        def gate_units(s):
            C = S["conv"]
            with act.Fori(0, CT // 2) as i:
                for w in range(4):
                    k = bass.ds(i * 2 + w // 2, 1)
                    for c, (c0, n) in enumerate(CHUNKS):
                        bank = (w * NC + c) % 4
                        if c < NC - 1:
                            act.wait_ge(s["part"], s.base["part"] + i * 8 + (2 * w + c + 1))
                        else:
                            act.wait_ge(unit_done, i * 4 + (SLOTS + COL["w_in"] + w + 1))
                        if w % 2:
                            act.activation(ya[:, k, c0:c0 + n], ps[:, bank:bank + 1, 0:n], ACT.Sigmoid
                                           ).then_inc(s["free"], 1)
                            continue
                        np_ = min(n, SEQ - c0)
                        cp = act.copy(U[:, k, PAD + c0:PAD + c0 + np_], ps[:, bank:bank + 1, 0:np_])
                        if np_ < n:
                            cp = act.copy(Us[:, k, :, PAD:PAD + TS],
                                          ps[:, bank:bank + 1, np_:n].rearrange("p o (b t) -> p o b t", t=TS))
                        cp.then_inc(s["free"], 1)

        def split_input(s):
            for k in range(KT):
                act.wait_ge(s[f"in{k % 3}"], s.base[f"in{k % 3}"] + 16 * (k // 3 + 1))
                act.copy(hh[:, k, :], mixin[:, k % 3, :]).then_inc(s["hi"], 1)

        for w in range(2):
            act.sem_inc(S["nm"][f"st{w}"], 16)
        barrier(act, 1)
        norm(S["n1"], CHUNKS, x, sq, rs, tb, hh)
        ffn("ffn1", S["n1"])
        barrier(act, 2)
        norm(S["nm"], CHUNKS, x, sq3, rs3, tb3, h3h)
        gate_units(S["nm"])
        store_proj("w_in", S["nm"], stage3, 3 * CT, 2 * CT, z)
        barrier(act, 3)
        M, C, s = S["mem"], S["conv"], S["mk"]
        act.sem_inc(s["mk_free"], 4)
        act.sem_inc(s["mv_free"], 4)
        for k in range(CT):
            act.wait_ge(C["ut"], k + 1)
            act.copy(ucs[0:PAD, 0, k * P:(k + 1) * P], ps[0:PAD, 4, 0:P]).then_inc(C["ucs"], 1)
            act.copy(ucs[:, 1:3, k * P:(k + 1) * P], ps[0:4 * PAD, 4, P:3 * P].rearrange("p (a c) -> p a c", a=2)
                     ).then_inc(C["ucs"], 1)
        act.wait_ge(C["ucs"], 2 * CT)
        act.dma_start(new_conv_p, ucs[0:PAD, 0, :]).then_inc(C["ucst"], 16)
        act.dma_start(new_conv_s, ucs[:, 1:3, :]).then_inc(C["ucst"], 16)
        act.wait_ge(M["ev"], M.base["ev"] + 4)
        norm(M, [(0, NMEM)], memT, msq, mrs, mtb, mh)
        for c, (c0, n) in enumerate(CHUNKS):
            for k in range(CT):
                act.wait_ge(C["xc"], c * CT + k + 1)
                act.activation(U[:, k, c0:c0 + n], ya[:, k, c0:c0 + n], ACT.Square).then_inc(C["sq"], 1)
        for name, n in (("w_ck", "mk"), ("w_cv", "mv")):
            if n == "mv":
                act.wait_ge(s["mkst"], s.base["mkst"] + 16)
            with act.Fori(0, 2) as i:
                for w in range(4):
                    act.wait_ge(unit_done, i * 4 + (SLOTS + COL[name] + w + 1))
                    act.copy(kvT[:, bass.ds(i * 4 + w, 1), :], ps[:, w:w + 1, 0:NMEM]).then_inc(s[n + "_free"], 1)
            if n == "mk":
                act.wait_ge(s["mk_free"], s.base["mk_free"] + 12)
                act.dma_start(mkT.rearrange("(k p) t -> p k t", p=P), kvT[:]).then_inc(s["mkst"], 16)
            for t in range(2):
                for h in range(2):
                    j = 2 * t + h
                    act.wait_ge(s[n + "_t"], s.base[n + "_t"] + j + 1)
                    if n == "mv" and j == 0:
                        act.wait_ge(s["kvst"], s.base["kvst"] + 16)
                    act.copy(kvtok[:, t, 512 * h:512 * h + 512], ps[:, j, :]).then_inc(s[n + "_tok"], 1)
            act.wait_ge(s[n + "_tok"], s.base[n + "_tok"] + 4)
            act.dma_start(mem_o[n[1]], kvtok[:]).then_inc(s["kvst"], 16)
            if n == "mk":
                for c, (c0, w) in enumerate(CHUNKS):
                    act.wait_ge(C["var"], c + 1)
                    act.activation(mrs[:, c, 0:w], mrs[:, c, 0:w], ACT.Sqrt).then_inc(C["std"], 1)
                for k in range(CT):
                    act.wait_ge(C["ln"], CT * (NC - 1) + k + 1)
                    act.activation(ya[:, k, :], ya[:, k, :], ACT.Silu, bias=vecs[:, V_LB + k:V_LB + k + 1]
                                   ).then_inc(C["ob"], 1)
                act.wait_ge(C["ob"], CT)
                act.dma_start(mix[CT * P:KT * P, :].rearrange("(k p) t -> p k t", p=P), ya[:]).then_inc(C["obst"], 16)
        act.wait_ge(C["obst"], 16)
        act.wait_ge(C["ucst"], 32)
        act.wait_ge(s["kvst"], s.base["kvst"] + 32)
        act.wait_ge(s["mkst"], s.base["mkst"] + 16)
        barrier(act, 4)
        A = S["pa"]
        act.sem_inc(A["t_free"], 2)
        act.sem_inc(A["kst"], 32)
        for a in range(2):
            act.wait_ge(A["tok_t"], a + 1)
            act.copy(kvs[:, a, :], ps[0:TSAMP, 6 + a, :]).then_inc(A["tok_e"], 1)
        act.wait_ge(A["tok_e"], 2)
        act.dma_start(win_s["k"], kvs[:, 0, :]).then_inc(A["tokst"], 16)
        act.dma_start(win_s["v"], kvs[:, 1, :]).then_inc(A["tokst"], 16)
        with act.Fori(0, H // 4) as i:
            tf = [0]

            def evac(dst):
                act.wait_ge(A["t_full"], i * WT + (tf[0] + 1))
                nb = dst.shape[1]
                act.copy(dst, ps[:, 4 + tf[0] % 2, 0:nb * P].rearrange("p (k c) -> p k c", c=P)
                         ).then_inc(A["t_free"], 1)
                tf[0] += 1

            def tokens(kind, p, half):
                if kind == "v" and half == 0:
                    act.wait_ge(A["kst"], i * 64 + (32 + 32 * p))
                dst = vtok if kind == "v" else ktok
                evac(dst[:, p, 4 * half:4 * half + 4, :])
                if half == 1:
                    act.wait_ge(A["t_free"], i * WT + (tf[0] + 2))
                    act.dma_start(win_p[kind][:, :, bass.ds(i * (2 * P) + p * P, P)], dst[:, p]).then_inc(A["kst"], 16)

            def exp(n):
                p, h, t = wsteps[n]
                act.wait_ge(A["m"], i * WN + (n + 1))
                w = P * (t + 1)
                act.activation(Sb[:, n % 3, 0:w], Sb[:, n % 3, 0:w], ACT.Exp, bias=stat[:, n % 4, 1:2], scale=0.125,
                               accum_out=stat[:, n % 4, 2:3]).then_inc(A["e"], 1)

            def store(p):
                act.wait_ge(A["o_free"], i * WN + (2 + WP * (p + 1)))
                act.dma_start(mix[bass.ds(i * (2 * P) + p * P, P), 0:SEQ], oT[:, p]).then_inc(A[f"ost{p}"], 16)

            exp(0)
            exp(1)
            for kind in "vk":
                for half in range(2):
                    tokens(kind, 0, half)
            for n in range(WN):
                p, h, t = wsteps[n]
                for kind, c in turns(n):
                    if kind != "p":
                        tokens(kind, 1, c)
                        continue
                    if n >= 2 and c == 0:
                        act.wait_ge(A["o_full"], i * WN + (n - 1))
                    evac(PT[:, n % 2, 4 * c:min(4 * c + 4, t + 1), :])
                if n + 2 < WN:
                    exp(n + 2)
                if n == WP + 3:
                    store(0)
            store(1)
        act.wait_ge(A["kst"], 32 * (H // 2) + 32)
        for p in range(2):
            act.wait_ge(A[f"ost{p}"], 16 * (H // 4) + 16)
        act.wait_ge(A["tokst"], 32)
        barrier(act, 5)
        B = S["sa"]
        act.sem_inc(B["t_freea"], 1)
        with act.Fori(0, NB // 2) as i:
            for b, c in [(b, c) for b in range(2) for c in range(3)]:
                j = 3 * b + c
                w = 4 * (OG if c < 2 else P)
                for k in range(0, CT, 2):
                    act.wait_ge(B["t_full"], i * 24 + (j * CT + k + 1))
                    act.wait_ge(B["s_part"], i * 6 + (j + 1))
                    act.copy(Kc[:, k, 0:w], ps[:, 0, 0:w]).then_inc(B["t_freea"], 1)
            act.wait_ge(B["m"], i + 1)
            act.activation(Ss[:], Ss[:], ACT.Exp, bias=sstat[:, 5:6], scale=0.125, accum_out=sstat[:, 6:7]
                           ).then_inc(B["e"], 1)
            for g_ in (0, 2):
                act.wait_ge(B["pt_full"], i * 4 + (g_ + 1))
                w = OG if g_ == 0 else P
                act.copy(PTs[0:w, 4 * g_:4 * g_ + 4, :], ps[0:w, 0, :].rearrange("p (k c) -> p k c", c=P)
                         ).then_inc(B["pt_a"], 1)
        act.wait_ge(B["o_free"], 1 + NB)
        act.dma_start(mix[0:CT * P, SEQ:T].rearrange("(k p) t -> p k t", p=P),
                      oS[:].rearrange("p k b t -> p k (b t)")).then_inc(B["ost"], 16)
        act.wait_ge(B["ost"], 16)
        barrier(act, 6)
        split_input(S["so"])
        barrier(act, 7)
        norm(S["nx"], CHUNKS, x, sq, rs, tb, hh)
        store_proj("w_cq", S["nx"], stage, KT, 0, zx)
        barrier(act, 8)
        X = S["xa"]
        act.sem_inc(X["t_free"], 2)
        act.sem_inc(X["e"], 2)
        with act.Fori(0, HX // 2) as i:
            def xexp(n):
                act.wait_ge(X["m"], i * XN + (n + 1))
                act.activation(Xb[:, n % 3, :], ps[:, n % 2, 0:NMEM], ACT.Exp, bias=xstat[:, n % 4, 1:2],
                               scale=HDX ** -0.5, accum_out=xstat[:, n % 4, 2:3]).then_inc(X["e"], 1)

            def xstore(p):
                act.wait_ge(X["o_free"], i * XN + (2 + QT * (p + 1)))
                act.dma_start(mixx[bass.ds(i * (2 * HDX) + p * HDX, HDX), 0:SEQ].rearrange("(k p) t -> p k t", p=P),
                              xo[:, p]).then_inc(X[f"ost{p}"], 16)

            xexp(0)
            xexp(1)
            for n in range(XN):
                act.wait_ge(X["t_full"], i * XN + (n + 1))
                if n >= 2:
                    act.wait_ge(X["o_full"], i * XN + (XN + n - 1))
                act.copy(XT[:, n % 2], ps[:, 2 + n % 2, 0:2 * P].rearrange("p (k c) -> p k c", c=P)
                         ).then_inc(X["t_free"], 1)
                if n + 2 < XN:
                    xexp(n + 2)
                if n == QT + 3:
                    xstore(0)
            xstore(1)
        Y = S["xs"]
        act.sem_inc(Y["t_freea"], 1)
        act.sem_inc(Y["e"], 1)
        with act.Fori(0, 2) as i:
            for b in range(4):
                for m in (0, 2):
                    act.wait_ge(Y["t_full"], i * 16 + (b * 4 + m + 1))
                    act.wait_ge(Y["s_full"], i * 4 + (b + 2))
                    act.copy(cKT[:, 2 * m:2 * m + 2, :], ps[:, 0, :].rearrange("p (k c) -> p k c", k=2)
                             ).then_inc(Y["t_freea"], 1)
            act.wait_ge(Y["m"], i + 1)
            act.activation(cS[:], ps[:, 2, 0:NMEM], ACT.Exp, bias=cstat[:, 1:2], scale=HDX ** -0.5,
                           accum_out=cstat[:, 2:3]).then_inc(Y["e"], 1)
            act.wait_ge(Y["pt_full"], i + 1)
            act.copy(cPT[:], ps[:, 3, 0:2 * P].rearrange("p (k c) -> p k c", c=P)).then_inc(Y["pt"], 1)
        act.wait_ge(Y["oe"], 3)
        act.dma_start(mixx[:, SEQ:T].rearrange("(k p) t -> p k t", p=P), co[:].rearrange("p k b t -> p k (b t)")
                      ).then_inc(Y["ost"], 16)
        for p in range(2):
            act.wait_ge(X[f"ost{p}"], 16 * (HX // 2) + 16)
        act.wait_ge(Y["ost"], 16)
        barrier(act, 9)
        split_input(S["sc"])
        barrier(act, 10)
        norm(S["n2"], CHUNKS, x, sq, rs, tb, hh)
        ffn("ffn2", S["n2"])
        barrier(act, 11)
        F = S["fin"]
        squares(F, CHUNKS, x, sq)
        roots(F, CHUNKS, rs)
        for t in range(QT + 1):
            n = P if t < QT else TSAMP
            for h in range(2):
                act.wait_ge(F["yt"], F.base["yt"] + 2 * t + h + 1)
                if t >= 2:
                    act.wait_ge(F[f"out{t % 2}"], F.base[f"out{t % 2}"] + 16 * (t // 2))
                act.copy(ytok[0:n, t % 2, 512 * h:512 * h + 512], ps[0:n, (2 * t + h) % 4, :]).then_inc(F["tok"], 1)

    @block.vector
    def _(dve):
        def squares(s, chunks, src, sqt):
            for c, (c0, n) in enumerate(chunks):
                for k in range(1, KT, 2):
                    j = c * KT + k
                    if j >= 4:
                        dve.wait_ge(s["summed"], s.base["summed"] + j - 3)
                    dve.tensor_tensor(sqt[:, sq_slot(k), 0:n], src[:, k, c0:c0 + n], src[:, k, c0:c0 + n], ALU.mult
                                      ).then_inc(s["sqd"], 1)

        def inverse_rms(s, chunks, rst):
            for c, (c0, n) in enumerate(chunks):
                dve.wait_ge(s["summed"], s.base["summed"] + KT * (c + 1))
                dve.tensor_scalar(rst[:, c, 0:n], ps[:, 5 + c, 0:n], 1.0 / D, EPS, ALU.mult, ALU.add
                                  ).then_inc(s["var"], 1)
            for c, (c0, n) in enumerate(chunks):
                dve.wait_ge(s["std"], s.base["std"] + c + 1)
                dve.reciprocal(rst[:, c, 0:n], rst[:, c, 0:n]).then_inc(s["rstd"], 1)

        def norm(s, chunks, src, sqt, rst, tbt, gain, hit, lot):
            squares(s, chunks, src, sqt)
            inverse_rms(s, chunks, rst)
            jobs = [(c, k) for c in range(len(chunks)) for k in range(KT)]

            def lo(j):
                c, k = jobs[j]
                c0, n = chunks[c]
                dve.wait_ge(s["hi"], s.base["hi"] + j + 1)
                dve.tensor_tensor(lot[:, k, c0:c0 + n], tbt[:, j % 3, 0:n], hit[:, k, c0:c0 + n].bitcast(F32),
                                  ALU.subtract).then_inc(s["h"], 1)

            for j, (c, k) in enumerate(jobs):
                c0, n = chunks[c]
                dve.wait_ge(s["rstd"], s.base["rstd"] + c + 1)
                if j >= 3:
                    dve.wait_ge(s["h"], s.base["h"] + j - 2)
                dve.scalar_tensor_tensor(out=tbt[:, j % 3, 0:n], in0=src[:, k, c0:c0 + n],
                                         scalar=vecs[:, gain + k:gain + k + 1], in1=rst[:, c, 0:n], op0=ALU.mult,
                                         op1=ALU.mult).then_inc(s["t"], 1)
                if j >= 1:
                    lo(j - 1)
            lo(len(jobs) - 1)

        def ffn(name, s):
            c0_, r0_ = COL[name], ROW[name]
            with dve.Fori(0, FG) as i:
                def lo(j):
                    f, c = divmod(j, NC)
                    c0, n = CHUNKS[c]
                    dve.wait_ge(s["hhi"], s.base["hhi"] + i * 6 + (j + 1))
                    dve.tensor_tensor(hidl[:, f, c0:c0 + n], ht[:, j % 2, 0:n], hidh[:, f, c0:c0 + n].bitcast(F32),
                                      ALU.subtract).then_inc(s["hid"], 1)

                for j in range(2 * NC):
                    f, c = divmod(j, NC)
                    n = CHUNKS[c][1]
                    if c < NC - 1:
                        dve.wait_ge(s["up"], s.base["up"] + i * 4 + (2 * f + c + 1))
                    else:
                        dve.wait_ge(unit_done, i * 4 + (SLOTS + c0_ + 2 * f + 2))
                    dve.wait_ge(s["sg"], s.base["sg"] + i * 6 + (j + 1))
                    dve.wait_ge(s["hid"], s.base["hid"] + i * 6 + max(j, 1))
                    dve.tensor_tensor(ht[:, j % 2, 0:n], ps[:, 2 * (j % 2) + 1, 0:n], sg[:, j % 2, 0:n], ALU.mult
                                      ).then_inc(s["prod"], 1)
                    if j >= 1:
                        lo(j - 1)
                lo(2 * NC - 1)
                for j in range(NC * KT):
                    c, d = divmod(j, KT)
                    c0, n = CHUNKS[c]
                    if j < NC * KT - 1:
                        dve.wait_ge(s["down"], s.base["down"] + i * (NC * KT - 1) + (j + 1))
                    else:
                        dve.wait_ge(row_done, i * 2 + (2 + r0_ + 2))
                    dve.scalar_tensor_tensor(out=x[:, d, c0:c0 + n], in0=ps[:, 4 + j % 4, 0:n], scalar=0.5,
                                             in1=x[:, d, c0:c0 + n], op0=ALU.mult, op1=ALU.add
                                             ).then_inc(s["res"], 1)

        def split_input(s):
            for k in range(KT):
                dve.wait_ge(s["hi"], s.base["hi"] + k + 1)
                dve.tensor_tensor(hl[:, k, :], mixin[:, k % 3, :], hh[:, k, :].bitcast(F32), ALU.subtract
                                  ).then_inc(s["h"], 1)

        def add_proj(name, s):
            split_input(s)
            with dve.Fori(0, 2) as i:
                for w in range(4):
                    for c, (c0, n) in enumerate(CHUNKS):
                        j = w * NC + c
                        if c < NC - 1:
                            dve.wait_ge(s["part"], s.base["part"] + i * 8 + (2 * w + c + 1))
                        else:
                            dve.wait_ge(unit_done, i * 4 + (SLOTS + COL[name] + w + 1))
                        xt = x[:, bass.ds(i * 4 + w, 1), c0:c0 + n]
                        dve.tensor_tensor(xt, ps[:, j % 4:j % 4 + 1, 0:n], xt, ALU.add).then_inc(s["free"], 1)

        dve.sem_inc(S["n1"]["prod"], 2)
        dve.sem_inc(S["n1"]["res"], 4)
        dve.sem_inc(S["n1"]["free"], 4)
        dve.sem_inc(S["n1"]["hid"], 1)
        L = S["load"]
        dve.wait_ge(L["vecs_t"], L.base["vecs_t"] + 1)
        dve.tensor_copy(vecs[:], ps[:, 0, 0:60]).then_inc(L["vecs"], 1)
        dve.tensor_copy(taps[:], ps[:, 1, 0:CT * CONVW].rearrange("p (k t) -> p k t", t=CONVW)
                        ).then_inc(L["vecs"], 1)
        for t in range(QT + 1):
            n = P if t < QT else TSAMP
            for h in range(2):
                j = 2 * t + h
                dve.wait_ge(L["xt"], L.base["xt"] + j + 1)
                dve.tensor_copy(x[:, 4 * h:4 * h + 4, t * P:t * P + n],
                                ps[:, 2 + j % 4, :].rearrange("p (k c) -> p k c", c=P)[:, :, 0:n]
                                ).then_inc(L["xin_free"], 1)
        C = S["conv"]
        dve.wait_ge(C["cct"], 1)
        for k in range(CT):
            dve.tensor_copy(Us[:, k, :, 0:PAD], ps[:, 6 + k // 2, (k % 2) * 240:(k % 2) * 240 + 240]
                            .rearrange("p (b t) -> p b t", t=PAD)).then_inc(C["us"], 1)
        barrier(dve, 1)
        norm(S["n1"], CHUNKS, x, sq, rs, tb, G_FFN1, hh, hl)
        ffn("ffn1", S["n1"])
        barrier(dve, 2)
        dve.memset(U[:, :, 0:PAD], 0.0).then_inc(C["us"], 1)
        norm(S["nm"], CHUNKS, x, sq3, rs3, tb3, G_MIX, h3h, h3l)
        dve.wait_ge(C["us"], CT + 1)
        with dve.Fori(0, CT) as i:
            dve.wait_ge(S["nm"]["free"], i * (2 * NC) + (S["nm"].base["free"] + 4 + 2 * NC))
            k = bass.ds(i, 1)
            dve.tensor_tensor(U[:, k, PAD:PAD + SEQ], U[:, k, PAD:PAD + SEQ], ya[:, k, 0:SEQ], ALU.mult
                              ).then_inc(C["glu"], 1)
            dve.tensor_tensor(Us[:, k, :, PAD:PAD + TS], Us[:, k, :, PAD:PAD + TS],
                              ya[:, k, SEQ:T].rearrange("p o (b t) -> p o b t", t=TS), ALU.mult
                              ).then_inc(C["glu"], 1)
            dve.wait_ge(C["glu"], i * 2 + 2)
            for t in range(CONVW):
                up = U[:, bass.ds(i, 1), t:t + SEQ].rearrange("p o t -> p (o t)")
                us = Us[:, bass.ds(i, 1), :, t:t + TS].rearrange("p o b t -> p (o b) t")
                yp = ya[:, bass.ds(i, 1), 0:SEQ].rearrange("p o t -> p (o t)")
                ys = ya[:, bass.ds(i, 1), SEQ:T].rearrange("p o (b t) -> p (o b) t", t=TS)
                w = taps[:, bass.ds(i, 1), t:t + 1].rearrange("p o t -> p (o t)")
                for q, (src, dst) in enumerate(((up, yp), (us, ys))):
                    if t == 0:
                        dve.tensor_scalar(dst, src, w, vecs[:, bass.ds(i + V_CB, 1)], ALU.mult, ALU.add
                                          ).then_inc(C["tap"], 1)
                    else:
                        dve.wait_ge(C["tap"], i * (2 * CONVW) + (2 * t - 1 + q))
                        dve.scalar_tensor_tensor(out=dst, in0=src, scalar=w, in1=dst, op0=ALU.mult, op1=ALU.add
                                                 ).then_inc(C["tap"], 1)
        barrier(dve, 3)
        M, C = S["mem"], S["conv"]
        for k in range(CT):
            dve.tensor_copy(cct[:, k].rearrange("p a (b t) -> p (a b) t", t=PAD), Us[:, k, :, TS:PAD + TS]
                            ).then_inc(C["ug"], 1)
        for t in range(2):
            for h in range(2):
                dve.wait_ge(M["xt"], M.base["xt"] + 2 * t + h + 1)
                dve.tensor_copy(memT[:, 4 * h:4 * h + 4, t * P:(t + 1) * P],
                                ps[:, 2 * t + h, :].rearrange("p (k c) -> p k c", c=P)).then_inc(M["ev"], 1)
        dve.wait_ge(M["ev"], M.base["ev"] + 4)
        norm(M, [(0, NMEM)], memT, msq, mrs, mtb, G_MEM, mh, ml)
        for c, (c0, n) in enumerate(CHUNKS):
            dve.wait_ge(C["mean"], c + 1)
            dve.tensor_scalar(mu[:, c, 0:n], ps[:, LNB[c], 0:n], 1.0 / WA, None, ALU.mult).then_inc(C["mu"], 1)
            dve.wait_ge(C["mu"], c + 1)
            for k in range(CT):
                dve.tensor_tensor(ya[:, k, c0:c0 + n], ya[:, k, c0:c0 + n], mu[:, c, 0:n], ALU.subtract
                                  ).then_inc(C["xc"], 1)
        dve.wait_ge(C["xc"], CT * NC)
        for c, (c0, n) in enumerate(CHUNKS):
            dve.wait_ge(C["summed"], c + 1)
            dve.tensor_scalar(mrs[:, c, 0:n], ps[:, LNB[c], 0:n], 1.0 / WA, EPS, ALU.mult, ALU.add
                              ).then_inc(C["var"], 1)
        for c, (c0, n) in enumerate(CHUNKS):
            dve.wait_ge(C["std"], c + 1)
            dve.reciprocal(mrs[:, c, 0:n], mrs[:, c, 0:n]).then_inc(C["rstd"], 1)
            dve.wait_ge(C["rstd"], c + 1)
            for k in range(CT):
                dve.scalar_tensor_tensor(out=ya[:, k, c0:c0 + n], in0=ya[:, k, c0:c0 + n],
                                         scalar=vecs[:, V_LG + k:V_LG + k + 1], in1=mrs[:, c, 0:n], op0=ALU.mult,
                                         op1=ALU.mult).then_inc(C["ln"], 1)
        barrier(dve, 4)
        A = S["pa"]
        dve.sem_inc(A["s_free"], WN)
        dve.sem_inc(A["o_free"], 2)
        for p in range(2):
            dve.sem_inc(A[f"ost{p}"], 16)
        with dve.Fori(0, H // 4) as i:
            def mask(n):
                p, h, t = wsteps[n]
                w = P * (t + 1)
                if n % WP == 0:
                    dve.wait_ge(A[f"in{p}"], i * 64 + 64)
                dve.wait_ge(A["s_full"], i * WN + (WN + n + 1))
                b = 2 * (n % 2)
                dve.sem_inc(met, 1)
                dve.tensor_tensor_reduce(out=Sb[:, n % 3, 0:w], in0=ps[:, b:b + 2, :].rearrange("p b n -> p (b n)")
                                         [:, 0:w], in1=pb[:, p, h, SEQ - w:SEQ], scale=1.0, scalar=-3.0e38,
                                         op0=ALU.add, op1=ALU.max, accum_out=stat[:, n % 4, 0:1]
                                         ).then_inc(A["s_free"], 1)
                dve.wait_ge(A["s_free"], i * WN + (WN + n + 1))
                dve.tensor_scalar(stat[:, n % 4, 1:2], stat[:, n % 4, 0:1], -0.125, None, ALU.mult
                                  ).then_inc(A["m"], 1)

            def normalise(n):
                p, h, t = wsteps[n]
                w = P * (t + 1)
                dve.wait_ge(A["e"], i * WN + (n + 1))
                dve.reciprocal(stat[:, n % 4, 3:4], stat[:, n % 4, 2:3]).then_inc(A["r"], 1)
                dve.wait_ge(A["r"], i * WN + (n + 1))
                dve.tensor_scalar(Sb[:, n % 3, 0:w], Sb[:, n % 3, 0:w], stat[:, n % 4, 3:4], None, ALU.mult
                                  ).then_inc(A["p"], 1)

            def output(n):
                p, h, t = wsteps[n]
                if n % WP == 0:
                    dve.wait_ge(A[f"ost{p}"], i * 16 + 16)
                dve.wait_ge(A["o_full"], i * WN + (n + 1))
                dve.tensor_copy(oT[64 * h:64 * h + 64, p, t * P:(t + 1) * P], ps[64 * h:64 * h + 64, 6 + n % 2, 0:P]
                                ).then_inc(A["o_free"], 1)

            mask(0)
            mask(1)
            normalise(0)
            for n in range(WN):
                if n + 2 < WN:
                    mask(n + 2)
                if n + 1 < WN:
                    normalise(n + 1)
                if n >= 1:
                    output(n - 1)
            output(WN - 1)
        barrier(dve, 5)
        B = S["sa"]
        dve.sem_inc(B["t_freed"], 1)
        dve.sem_inc(B["s_free"], 1)
        dve.sem_inc(B["o_free"], 1)
        dve.memset(Qc[:], 0.0).then_inc(B["qz"], 1)
        dve.wait_ge(B["qz"], 1)
        dve.wait_ge(B["bias"], 16)
        with dve.Fori(0, NB // 2) as i:
            dve.wait_ge(B["qk_in"], i * 32 + 32)
            dve.wait_ge(B["s_full"], i * 2 + 2)
            for b in range(2):
                for k in range(CT):
                    for hf in range(2):
                        h = 2 * k + hf
                        dve.tensor_copy(Qc[64 * hf:64 * hf + 64, b, k, h * TS:(h + 1) * TS],
                                        Qin[64 * hf:64 * hf + 64, k, b * TS:(b + 1) * TS]).then_inc(B["q"], 1)
            for b, c in [(b, c) for b in range(2) for c in range(3)]:
                j = 3 * b + c
                w = 4 * (OG if c < 2 else P)
                for k in range(1, CT, 2):
                    dve.wait_ge(B["t_full"], i * 24 + (j * CT + k + 1))
                    dve.wait_ge(B["s_part"], i * 6 + (j + 1))
                    dve.tensor_copy(Kc[:, k, 0:w], ps[:, 1, 0:w]).then_inc(B["t_freed"], 1)
            dve.wait_ge(B["s_full"], i * 2 + 4)
            dve.sem_inc(met, 1)
            off = 0
            for c, w in enumerate((4 * OG, 4 * OG, 512, TS)):
                ttr = dve.tensor_tensor_reduce(out=Ss[:, off:off + w], in0=ps[:, 2 + c, 0:w], in1=sbias[:, off:off + w],
                                               scale=1.0, scalar=-3.0e38, op0=ALU.add, op1=ALU.max,
                                               accum_out=sstat[:, c:c + 1])
                off += w
            ttr.then_inc(B["s_free"], 1)
            dve.wait_ge(B["s_free"], i + 2)
            dve.tensor_reduce(sstat[:, 4:5], sstat[:, 0:4], AX.X, ALU.max).then_inc(B["mx"], 1)
            dve.wait_ge(B["mx"], i + 1)
            dve.tensor_scalar(sstat[:, 5:6], sstat[:, 4:5], -0.125, None, ALU.mult).then_inc(B["m"], 1)
            dve.wait_ge(B["e"], i + 1)
            dve.reciprocal(sstat[:, 7:8], sstat[:, 6:7]).then_inc(B["r"], 1)
            dve.wait_ge(B["r"], i + 1)
            dve.tensor_scalar(Ss[:], Ss[:], sstat[:, 7:8], None, ALU.mult).then_inc(B["p"], 1)
            dve.wait_ge(B["pt_full"], i * 4 + 2)
            dve.tensor_copy(PTs[0:OG, 4:8, :], ps[0:OG, 1, :].rearrange("p (k c) -> p k c", c=P)
                            ).then_inc(B["pt_d"], 1)
            dve.wait_ge(B["pt_full"], i * 4 + 4)
            dve.tensor_copy(PTs[0:TS, 12, :], ps[0:TS, 1, 0:P]).then_inc(B["pt_d"], 1)
            dve.wait_ge(B["v_used"], i * 2 + 4)
            for hf in range(2):
                src = ps[64 * hf:64 * hf + 64, 6, 0:P].rearrange("p (b k c) -> p k b c", b=2, k=CT)
                dve.tensor_copy(oS[64 * hf:64 * hf + 64, :, bass.ds(i * 2, 2), :], src[:, :, :, hf * TS:(hf + 1) * TS]
                                ).then_inc(B["o_free"], 1)
        barrier(dve, 6)
        add_proj("w_out", S["so"])
        barrier(dve, 7)
        norm(S["nx"], CHUNKS, x, sq, rs, tb, G_X, hh, hl)
        barrier(dve, 8)
        X = S["xa"]
        dve.sem_inc(X["o_free"], 2)
        for p in range(2):
            dve.sem_inc(X[f"ost{p}"], 16)
        with dve.Fori(0, HX // 2) as i:
            def xmax(n):
                dve.wait_ge(X["s_full"], i * XN + (n + 1))
                dve.tensor_reduce(xstat[:, n % 4, 0:1], ps[:, n % 2, 0:NMEM], AX.X, ALU.max).then_inc(X["mx"], 1)
                dve.wait_ge(X["mx"], i * XN + (n + 1))
                dve.tensor_scalar(xstat[:, n % 4, 1:2], xstat[:, n % 4, 0:1], -(HDX ** -0.5), None, ALU.mult
                                  ).then_inc(X["m"], 1)

            def xnorm(n):
                dve.wait_ge(X["e"], i * XN + (n + 3))
                dve.reciprocal(xstat[:, n % 4, 3:4], xstat[:, n % 4, 2:3]).then_inc(X["r"], 1)
                dve.wait_ge(X["r"], i * XN + (n + 1))
                dve.tensor_scalar(Xb[:, n % 3, :], Xb[:, n % 3, :], xstat[:, n % 4, 3:4], None, ALU.mult
                                  ).then_inc(X["p"], 1)

            def xout(n):
                p, t = xsteps[n]
                if t == 0:
                    dve.wait_ge(X[f"ost{p}"], i * 16 + 16)
                dve.wait_ge(X["o_full"], i * XN + (XN + n + 1))
                dve.tensor_copy(xo[:, p, :, t * P:(t + 1) * P], ps[:, 4 + n % 2, 0:2 * P]
                                .rearrange("p (k c) -> p k c", c=P)).then_inc(X["o_free"], 1)

            xmax(0)
            xmax(1)
            xnorm(0)
            for n in range(XN):
                if n + 2 < XN:
                    xmax(n + 2)
                if n + 1 < XN:
                    xnorm(n + 1)
                if n >= 1:
                    xout(n - 1)
            xout(XN - 1)
        Y = S["xs"]
        dve.sem_inc(Y["t_freed"], 1)
        dve.sem_inc(Y["oe"], 1)
        dve.memset(cqc[:], 0.0).then_inc(Y["qz"], 1)
        dve.wait_ge(Y["qz"], 1)
        dve.wait_ge(Y["q_in"], 16)
        with dve.Fori(0, 2) as i:
            dve.wait_ge(Y["s_full"], i * 4 + 2)
            for h in range(HX):
                dve.tensor_copy(cqc[:, :, 2 * h:2 * h + 2, h * TS:(h + 1) * TS],
                                cq[:, 2 * h:2 * h + 2, bass.ds(i * 32, 32)].rearrange("p k (b t) -> p b k t", b=4)
                                ).then_inc(Y["qc"], 1)
            for b in range(4):
                for m in (1, 3):
                    dve.wait_ge(Y["t_full"], i * 16 + (b * 4 + m + 1))
                    dve.wait_ge(Y["s_full"], i * 4 + (b + 2))
                    dve.tensor_copy(cKT[:, 2 * m:2 * m + 2, :], ps[:, 1, :].rearrange("p (k c) -> p k c", k=2)
                                    ).then_inc(Y["t_freed"], 1)
            dve.wait_ge(Y["s_full"], i * 4 + 6)
            dve.tensor_reduce(cstat[:, 0:1], ps[:, 2, 0:NMEM], AX.X, ALU.max).then_inc(Y["mx"], 1)
            dve.wait_ge(Y["mx"], i + 1)
            dve.tensor_scalar(cstat[:, 1:2], cstat[:, 0:1], -(HDX ** -0.5), None, ALU.mult).then_inc(Y["m"], 1)
            dve.wait_ge(Y["e"], i + 2)
            dve.reciprocal(cstat[:, 3:4], cstat[:, 2:3]).then_inc(Y["r"], 1)
            dve.wait_ge(Y["r"], i + 1)
            dve.tensor_scalar(cS[:], cS[:], cstat[:, 3:4], None, ALU.mult).then_inc(Y["p"], 1)
            dve.wait_ge(Y["o_full"], i + 2)
            dve.tensor_copy(co[:, :, bass.ds(i * 4, 4), :], ps[:, 4, 0:KT * 32]
                            .rearrange("p (k b t) -> p k b t", b=4, t=TS)).then_inc(Y["oe"], 1)
        barrier(dve, 9)
        add_proj("w_co", S["sc"])
        barrier(dve, 10)
        norm(S["n2"], CHUNKS, x, sq, rs, tb, G_FFN2, hh, hl)
        ffn("ffn2", S["n2"])
        barrier(dve, 11)
        F = S["fin"]
        squares(F, CHUNKS, x, sq)
        inverse_rms(F, CHUNKS, rs)
        for c, (c0, n) in enumerate(CHUNKS):
            dve.wait_ge(F["rstd"], F.base["rstd"] + c + 1)
            for k in range(KT):
                dve.scalar_tensor_tensor(out=x[:, k, c0:c0 + n], in0=x[:, k, c0:c0 + n],
                                         scalar=vecs[:, G_FIN + k:G_FIN + k + 1], in1=rs[:, c, 0:n], op0=ALU.mult,
                                         op1=ALU.mult).then_inc(F["h"], 1)

    ctx.close()


_INS = ["x_prompt", "x_sample", "mem_prompt", "cache_win_k", "cache_win_v", "cache_conv", "cache_mem_k",
        "cache_mem_v", "ffn1_norm", "ffn1_gate", "ffn1_up", "ffn1_down", "mix_norm", "w_in", "conv_w", "conv_b",
        "conv_ln_g", "conv_ln_b", "w_out", "xattn_norm", "mem_norm", "w_cq", "w_ck", "w_cv", "w_co", "ffn2_norm",
        "ffn2_gate", "ffn2_up", "ffn2_down", "final_norm"]
_OUTS = [("y_prompt", (1, SEQ, D)), ("y_sample", (NB, TS, D)),
         ("new_win_k_prompt", (1, 1, SEQ, H, HD)), ("new_win_v_prompt", (1, 1, SEQ, H, HD)),
         ("new_conv_prompt", (1, 1, PAD, WA)),
         ("new_mem_k_prompt", (1, 1, NMEM, HX, HDX)), ("new_mem_v_prompt", (1, 1, NMEM, HX, HDX)),
         ("new_win_k_sample", (1, NB, TS, H, HD)), ("new_win_v_sample", (1, NB, TS, H, HD)),
         ("new_conv_sample", (1, NB, PAD, WA))]


def kernel(**inputs):
    import concourse.bacc as _bacc
    from concourse.bass_utils import run_bass_kernel_spmd as _run

    nc = _bacc.Bacc("TRN2", target_bir_lowering=False, num_devices=1)
    given = {n: np.ascontiguousarray(inputs[n]) for n in _INS}
    given["prompt_bias"] = prompt_bias()
    given["sample_bias"] = sample_bias()
    arrays, ins = {}, {}
    for name, a in given.items():
        arrays[f"in_{name}"] = a
        ins[name] = nc.dram_tensor(f"in_{name}", a.shape, mybir.dt.from_np(a.dtype), kind="ExternalInput").ap()
    outs = {name: nc.dram_tensor(f"out_{name}", shape, F32, kind="ExternalOutput").ap() for name, shape in _OUTS}
    decoder_layer(nc, ins, outs)
    r = _run(nc, [arrays], core_ids=[0])
    return tuple(r.results[0][f"out_{name}"] for name, _ in _OUTS)
```

```python
from collections import defaultdict
from contextlib import ExitStack

import concourse.bass as bass
import numpy as np
from concourse import mybir

F32 = mybir.dt.float32
F32R = mybir.dt.float32r
ALU = mybir.AluOpType
ACT = mybir.ActivationFunctionType
AX = mybir.AxisListType

P = 128
D = 1024
KT = D // P
SEQ, NB, TS = 1024, 8, 8
TSAMP = NB * TS
T = SEQ + TSAMP
CHUNKS = [(0, 384), (384, 384), (768, T - 768)]
NC = len(CHUNKS)
DFF = 2816
FG = DFF // (2 * P)
H, HD = 8, 64
WA = H * HD
CT = WA // P
CONVW = 31
PAD = CONVW - 1
NMEM, HX, HDX = 256, 4, 256
EPS = 1e-6
WBUF = 2048
OLD = WBUF - 512
OG, ORS = OLD // 16, 8
RR = 4
NKEY = OG * ORS + 512 + TS
NEG = -1.0e30
QT = SEQ // P
SLOTS = 4
SQ = 4
LNB = (4, 6, 7)


def log_multiplicity(d):
    c = ((d <= 128).astype(np.float64) + ((d <= 512) & (d % 4 == 0)) + ((d <= 2048) & (d % 16 == 0))) * (d >= 0)
    return np.where(c > 0, np.log(np.maximum(c, 1.0)), NEG)


def prompt_bias():
    d = np.arange(P)[:, None] + (SEQ - P) - np.arange(SEQ)[None, :]
    slopes = 2.0 ** -(np.arange(H) + 1.0)
    b = 8.0 * (log_multiplicity(d)[None] - slopes[:, None, None] * d[None])
    return np.where(d[None] < 0, NEG, np.maximum(b, NEG)).astype(np.float32)


def sample_bias():
    old = np.arange(OG)[None, :] * 16 + np.arange(ORS)[:, None]
    recent = OLD + np.arange(P)[None, :] * RR + np.arange(RR)[:, None]
    pos = np.concatenate([old.ravel(), recent.ravel(), WBUF + np.arange(TS)])
    d = WBUF + np.arange(TS)[:, None] - pos[None, :]
    slopes = 2.0 ** -(np.arange(H) + 1.0)
    b = 8.0 * (log_multiplicity(d)[None] - slopes[:, None, None] * d[None])
    return np.where(d[None] < 0, NEG, np.maximum(b, NEG)).reshape(H * TS, NKEY).astype(np.float32)


def decoder_layer(nc, I, O):
    ctx = ExitStack()

    def sem(name):
        return ctx.enter_context(nc.semaphore(name))

    def alloc(stack, name, shape, dt=F32):
        return stack.enter_context(nc.sbuf_tensor(name, shape, dt))

    z = nc.dram_tensor("z_scratch", (20 * P, T), F32).ap()
    zx = nc.dram_tensor("zx_scratch", (KT * P, T), F32).ap()
    mix = nc.dram_tensor("mix_scratch", (KT * P, T), F32).ap()
    mixx = nc.dram_tensor("mixx_scratch", (KT * P, T), F32).ap()
    mkT = nc.dram_tensor("mkT_scratch", (KT * P, NMEM), F32).ap()

    x = alloc(ctx, "x", [P, KT, T])
    raw = alloc(ctx, "raw", [P, 2, KT, P])
    wh = alloc(ctx, "wh", [P, SLOTS, KT, P], F32R)
    wl = alloc(ctx, "wl", [P, SLOTS, KT, P], F32R)
    ident = alloc(ctx, "ident", [P, P])
    ones = alloc(ctx, "ones", [P, P])
    vecs = alloc(ctx, "vecs", [P, 60])
    taps = alloc(ctx, "taps", [P, CT, CONVW])
    G_FFN1, G_MIX, G_X, G_MEM, G_FFN2, G_FIN = (8 * j for j in range(6))
    V_CB, V_LG, V_LB = 48, 52, 56

    early = ExitStack()
    Us = alloc(early, "Us", [P, CT, NB, PAD + TS])
    with ExitStack() as g:
        hh = alloc(g, "hh", [P, KT, T], F32R)
        hl = alloc(g, "hl", [P, KT, T], F32R)
        sq = alloc(g, "sq", [P, 4, 384])
        tb = alloc(g, "tb", [P, 3, 384])
        rs = alloc(g, "rs", [P, NC, 384])
        with ExitStack() as f:
            bh = alloc(f, "bh", [P, 2, KT, P], F32R)
            bl = alloc(f, "bl", [P, 2, KT, P], F32R)
            hidh = alloc(f, "hidh", [P, 2, T], F32R)
            hidl = alloc(f, "hidl", [P, 2, T], F32R)
            sg = alloc(f, "sg", [P, 2, 384])
            ht = alloc(f, "ht", [P, 2, 384])
        with ExitStack() as f:
            xin = alloc(f, "xin", [P, 3, D])
            small = alloc(f, "small", [60, P])
            taps_in = alloc(f, "taps_in", [CONVW, WA])
            cc_in = alloc(f, "cc_in", [4 * PAD, 2, WA])
        with ExitStack() as f:
            stage = alloc(f, "stage", [P, 2, T])
        with ExitStack() as f:
            mixin = alloc(f, "mixin", [P, NC, KT, 384])
        with ExitStack() as f:
            ytok = alloc(f, "ytok", [P, 2, D])
    with ExitStack() as e:
        U = alloc(e, "U", [P, CT, T])
        ya = alloc(e, "ya", [P, CT, T])
        with ExitStack() as g:
            h3h = alloc(g, "h3h", [P, KT, T], F32R)
            h3l = alloc(g, "h3l", [P, KT, T], F32R)
            sq3 = alloc(g, "sq3", [P, 4, 384])
            tb3 = alloc(g, "tb3", [P, 3, 384])
            rs3 = alloc(g, "rs3", [P, NC, 384])
            stage3 = alloc(g, "stage3", [P, 2, T])
        with ExitStack() as g:
            min_ = alloc(g, "min_", [P, 2, D])
            memT = alloc(g, "memT", [P, KT, NMEM])
            mh = alloc(g, "mh", [P, KT, NMEM], F32R)
            ml = alloc(g, "ml", [P, KT, NMEM], F32R)
            msq = alloc(g, "msq", [P, 4, 384])
            mtb = alloc(g, "mtb", [P, 3, 384])
            mrs = alloc(g, "mrs", [P, NC, 384])
            kvT = alloc(g, "kvT", [P, KT, NMEM])
            kvtok = alloc(g, "kvtok", [P, 2, D])
            cct = alloc(g, "cct", [P, CT, 2, 4 * PAD])
            ucs = alloc(g, "ucs", [4 * PAD, 3, WA])
            mu = alloc(g, "mu", [P, NC, 384])
    early.close()
    ahead = ExitStack()
    sbias = alloc(ahead, "sbias", [H * TS, NKEY])
    Qall = alloc(ahead, "Qall", [P, CT, TSAMP])
    Kall = alloc(ahead, "Kall", [P, CT, TSAMP])
    Ko = [alloc(ahead, "Ko0", [OG, ORS, WA])]
    Kr = [alloc(ahead, "Kr0", [P, RR, WA])]
    with ExitStack() as g:
        qT = alloc(g, "qT", [P, 2, SEQ])
        kTp = alloc(g, "kTp", [P, 2, SEQ])
        vT = alloc(g, "vT", [P, 2, SEQ])
        pb = alloc(g, "pb", [P, 2, 2, SEQ])
        Sb = alloc(g, "Sb", [P, 3, SEQ])
        PT = alloc(g, "PT", [P, 2, QT, P])
        vtok = alloc(g, "vtok", [P, 2, QT, P])
        ktok = alloc(g, "ktok", [P, 2, QT, P])
        oT = alloc(g, "oT", [P, 2, SEQ])
        stat = alloc(g, "stat", [P, 4, 4])
        ks = alloc(g, "ks", [P, 2, CT, TSAMP])
        kvs = alloc(g, "kvs", [TSAMP, 2, WA])
    with ExitStack() as g:
        Ko.append(alloc(g, "Ko1", [OG, ORS, WA]))
        Kr.append(alloc(g, "Kr1", [P, RR, WA]))
        Vo = alloc(g, "Vo", [OG, 2, ORS, WA])
        Vr = alloc(g, "Vr", [P, 2, RR, WA])
        Vn = alloc(g, "Vn", [TS, 2, WA])
        Kc = alloc(g, "Kc", [P, 4, 512])
        Qc = alloc(g, "Qc", [P, 2, CT, H * TS])
        Ss = alloc(g, "Ss", [H * TS, NKEY])
        PTs = alloc(g, "PTs", [P, 13, H * TS])
        OV = alloc(g, "OV", [H * TS, WA])
        sstat = alloc(g, "sstat", [H * TS, 8])
        oS = alloc(g, "oS", [P, CT, NB, TS])
    ahead.close()
    with ExitStack() as g:
        xq = alloc(g, "xq", [P, 2, 2, SEQ])
        xk = alloc(g, "xk", [P, 2, 2, NMEM])
        xv = alloc(g, "xv", [P, 2, 2, HDX])
        Xb = alloc(g, "Xb", [P, 3, NMEM])
        XT = alloc(g, "XT", [P, 2, 2, P])
        xo = alloc(g, "xo", [P, 2, 2, SEQ])
        xstat = alloc(g, "xstat", [P, 4, 4])
        cq = alloc(g, "cq", [P, KT, TSAMP])
        cqc = alloc(g, "cqc", [P, 4, KT, HX * TS])
        cK = alloc(g, "cK", [P, 2, 2, D])
        cV = alloc(g, "cV", [P, 4, 2, D])
        cKT = alloc(g, "cKT", [P, 2, KT, NMEM])
        cS = alloc(g, "cS", [P, NMEM])
        cPT = alloc(g, "cPT", [P, 2, P])
        cstat = alloc(g, "cstat", [P, 4])
        cO = alloc(g, "cO", [P, D])
        co = alloc(g, "co", [P, KT, NB, TS])

    ps = ctx.enter_context(nc.psum_tensor("ps", [P, 8, 512], F32))

    setup_done = sem("setup_done")
    raw_full = [sem("raw_full0"), sem("raw_full1")]
    w_hi = sem("w_hi")
    w_split = sem("w_split")
    unit_done = sem("unit_done")
    row_done = sem("row_done")
    met = sem("met")
    phase_end = sem("phase_end")

    OUT = O
    W = {n: I[n].rearrange("o (k p) n -> p (o k) n", p=P) for n in
         ("ffn1_gate", "ffn1_up", "ffn2_gate", "ffn2_up", "w_in", "w_out", "w_cq", "w_ck", "w_cv", "w_co")}
    DOWN = {n: I[n].rearrange("o f n -> (o f) n") for n in ("ffn1_down", "ffn2_down")}

    plan = [("ffn1", 6 * FG), ("w_in", 20), ("w_ck", 8), ("w_cv", 8), ("w_out", 8), ("w_cq", 8), ("w_co", 8),
            ("ffn2", 6 * FG)]
    UNIT, COL, ROW = {}, {}, {}
    u = c = r = 0
    for n, k in plan:
        UNIT[n], COL[n], ROW[n] = u, c, r
        u += k
        c += 4 * FG if n.startswith("ffn") else k
        r += 2 * FG if n.startswith("ffn") else 0

    class Sems:
        def __init__(self, tag, shared=None, base=None):
            self.tag, self.made, self.base = tag, {} if shared is None else shared, defaultdict(int, base or {})

        def __getitem__(self, n):
            if n not in self.made:
                self.made[n] = sem(f"{self.tag}_{n}")
            return self.made[n]

    S = {n: Sems(n) for n in ("mk", "conv", "pa", "sa", "xa", "xs")}

    def of_norm(nc_, split=True):
        return {"sq": KT * nc_, "summed": KT * nc_, "var": nc_, "std": nc_, "rstd": nc_,
                "t": KT * nc_ * split, "hi": KT * nc_ * split, "h": KT * nc_}

    def of_proj(n, stored):
        return {"part": 2 * n, "free": 3 * n} | {f"st{w}": 8 * stored for w in range(2)}

    of_split = {"hi": NC * KT, "h": NC * KT, "in0": 16, "in1": 16, "in2": 16}
    of_ffn = {"gate": 4 * FG, "up": 4 * FG, "prod": 6 * FG, "res": NC * KT * FG, "sg": 6 * FG, "hhi": 6 * FG,
              "hid": 6 * FG, "down": (NC * KT - 1) * FG}
    shared, base = {}, defaultdict(int)
    for n, adds in (("load", {"in0": 48, "in1": 48, "in2": 48, "xt": 2 * (QT + 1)}), ("n1", of_norm(NC) | of_ffn),
                    ("nm", of_norm(NC) | of_proj(20, 12)), ("mem", of_norm(1)), ("so", of_split | of_proj(8, 0)),
                    ("nx", of_norm(NC) | of_proj(8, 8)), ("sc", of_split | of_proj(8, 0)),
                    ("n2", of_norm(NC) | of_ffn), ("fin", of_norm(NC, False))):
        S[n] = Sems("g", shared, base)
        for name, v in adds.items():
            base[name] += v
    block = ctx.enter_context(nc.Block())
    x_tok = I["x_prompt"].rearrange("b t d -> (b t) d")
    xs_tok = I["x_sample"].rearrange("b t d -> (b t) d")
    mem_tok = I["mem_prompt"].rearrange("b (t p) d -> p (b t) d", p=P)
    rows = [("ffn1_norm", G_FFN1, 8), ("mix_norm", G_MIX, 8), ("xattn_norm", G_X, 8), ("mem_norm", G_MEM, 8),
            ("ffn2_norm", G_FFN2, 8), ("final_norm", G_FIN, 8), ("conv_b", V_CB, 4), ("conv_ln_g", V_LG, 4),
            ("conv_ln_b", V_LB, 4)]
    cache_conv = I["cache_conv"].rearrange("o (a b) t c -> (b t) (o a) c", b=4)
    new_conv_s = OUT["new_conv_sample"].rearrange("o (a b) t c -> (b t) (o a) c", b=4)
    new_conv_p = OUT["new_conv_prompt"].rearrange("o b t c -> (o b t) c")
    win_p = {n: OUT[f"new_win_{n}_prompt"].rearrange("o b (t p) h e -> p (o b t) (h e)", p=P) for n in "kv"}
    win_s = {n: OUT[f"new_win_{n}_sample"].rearrange("o b t h e -> (o b t) (h e)") for n in "kv"}
    mem_o = {n: OUT[f"new_mem_{n}_prompt"].rearrange("o b (t p) h e -> p (o b t) (h e)", p=P) for n in "kv"}
    win_c = {n: I[f"cache_win_{n}"].rearrange("o b w h e -> (o b) w (h e)") for n in "kv"}
    mem_c = {n: I[f"cache_mem_{n}"].rearrange("o b (p j) h e -> (o b) p j (h e)", j=2) for n in "kv"}

    wsteps = [(p, h, t) for p in range(2) for h in range(2) for t in range(QT)]
    WN, WP = len(wsteps), len(wsteps) // 2
    xsteps = [(p, t) for p in range(2) for t in range(QT)]
    XN = len(xsteps)

    KG = 3 * CT
    SJ = SQ * (KG + 2)

    def key_job(q, g):
        return q * KG + 2 * max(q - 1, 0) + g

    def prob_job(q):
        return key_job(q + 1, KG) if q + 1 < SQ else SJ - 2

    def block_of(blk):
        return (OG, blk * OG) if blk < ORS else (P if blk < 12 else TS, ORS * OG + (blk - ORS) * P)

    def turns(n):
        p, h, t = wsteps[n]
        own = [("p", c) for c in range(1 + (t >= 4))]
        early = {WP - 2: [("v", 0), ("v", 1)], WP - 1: [("k", 0), ("k", 1)]}
        return early.get(n, []) + own

    WT = 4 + sum(len(turns(n)) for n in range(WN))

    def norm_order(nc_):
        seq = [("sq", 0, k) for k in range(KT)]
        if nc_ > 1:
            seq += [("sq", 1, 0), ("sq", 1, 1), ("var", 0, 0), ("sq", 1, 2), ("sq", 1, 3), ("inv", 0, 0)]
            seq += [("sq", 1, k) for k in range(4, 6)]
        else:
            seq += [("var", 0, 0), ("inv", 0, 0)]
        rest = [("sq", 1, 6), ("sq", 1, 7)] + [("sq", 2, k) for k in range(KT)] if nc_ > 1 else []
        for c in range(nc_):
            for k in range(KT):
                seq.append(("tile", c, k))
                seq += rest[:2]
                rest = rest[2:]
                if c + 1 < nc_ and k == (5, 1)[c > 0]:
                    seq.append(("var", c + 1, 0))
                if c + 1 < nc_ and k == (7, 3)[c > 0]:
                    seq.append(("inv", c + 1, 0))
        return seq

    def barrier(eng, n):
        eng.drain().then_inc(phase_end, 1)
        eng.wait_ge(phase_end, 3 * n)

    @block.sync
    def _(sp):
        def load_unit(parity, split_needed, src, dst=None):
            sp.wait_ge(w_split, split_needed)
            sp.dma_start(raw[:, parity] if dst is None else dst, src).then_inc(raw_full[parity], 16)

        def ffn_loads(name):
            u0 = UNIT[name]
            gate, up, down = W[f"{name}_gate"], W[f"{name}_up"], DOWN[f"{name}_down"]
            with sp.Fori(0, FG) as i:
                for j in range(6):
                    if j < 4:
                        src = (gate, up)[j % 2][:, :, bass.ds(i * (2 * P) + (j // 2) * P, P)]
                        dst = None
                    else:
                        src = down[bass.ds(i * (2 * P) + (j - 4) * P, P), :]
                        dst = raw[:, j % 2].rearrange("p k n -> p (k n)")
                    load_unit(j % 2, i * 6 + (u0 + j + 1), src, dst)

        def first_loads(name):
            for j in range(SLOTS):
                load_unit(j % 2, UNIT[name] + j + 1, W[name][:, :, j * P:(j + 1) * P])

        def col_loads(name, first=0):
            u0, n = UNIT[name] + first, dict(plan)[name] - first
            with sp.Fori(0, n // 4) as i:
                for j in range(4):
                    load_unit(j % 2, i * 4 + (u0 + j + 1), W[name][:, :, bass.ds(i * (4 * P) + (first + j) * P, P)])

        def in_loads():
            u0 = UNIT["w_in"]
            with sp.Fori(0, CT // 2) as i:
                for j in range(4):
                    load_unit(j % 2, i * 4 + (u0 + j + 1),
                              W["w_in"][:, :, bass.ds(i * (2 * P) + (3 * CT + j // 2 + CT * (j % 2)) * P, P)])
            with sp.Fori(0, 3 * CT // 4) as i:
                for j in range(4):
                    load_unit(j % 2, i * 4 + (u0 + 2 * CT + j + 1), W["w_in"][:, :, bass.ds(i * (4 * P) + j * P, P)])

        def load_mix(s, src):
            for c, (c0, n) in enumerate(CHUNKS):
                sp.dma_start(mixin[:, c, :, 0:n], src[:, c0:c0 + n].rearrange("(k p) t -> p k t", p=P)
                             ).then_inc(s[f"in{c}"], 16)

        L = S["load"]
        for name, c0, n in rows:
            v = I[name]
            v = v.rearrange("(k p) -> k p", p=P) if name == "final_norm" else v.rearrange("o (k p) -> (o k) p", p=P)
            sp.dma_start(small[c0:c0 + n, :], v).then_inc(L["small"], 16)
        sp.dma_start(taps_in[:], I["conv_w"].rearrange("o t c -> (o t) c")).then_inc(L["small"], 16)
        for t in range(QT + 1):
            if t >= 3:
                sp.wait_ge(L["xin_free"], L.base["xin_free"] + 2 * (t - 2))
            n = P if t < QT else TSAMP
            src = x_tok[t * P:t * P + n, :] if t < QT else xs_tok
            sp.dma_start(xin[0:n, t % 3, :], src).then_inc(L[f"in{t % 3}"], 16)
        sp.dma_start(cc_in[:], cache_conv).then_inc(S["conv"]["cc_in"], 16)
        ffn_loads("ffn1")
        in_loads()
        first_loads("w_ck")
        sp.wait_ge(phase_end, 3 * 3)
        sp.dma_start(min_[:], mem_tok).then_inc(S["mem"]["in"], 16)
        col_loads("w_ck", SLOTS)
        col_loads("w_cv")
        A = S["pa"]
        sp.wait_ge(phase_end, 3 * 4)
        for a in range(2):
            sp.dma_start(ks[:, a], z[(1 + a) * CT * P:(2 + a) * CT * P, SEQ:T].rearrange("(k p) t -> p k t", p=P)
                         ).then_inc(A["tok_in"], 16)
        with sp.Fori(0, H // 4) as i:
            for p in range(2):
                sp.wait_ge(A["s_full"], i * WN + WP * (p + 1))
                for dst, r0 in ((vT, 2 * CT), (kTp, CT), (qT, 0)):
                    sp.dma_start(dst[:, p], z[bass.ds(i * (2 * P) + (r0 + p) * P, P), 0:SEQ]).then_inc(A[f"in{p}"], 16)
                sp.wait_ge(A["s_free"], i * WN + WP * (p + 1))
                sp.dma_start(pb[:, p], I["prompt_bias"][bass.ds(i * 4 + 2 * p, 2), :, :].rearrange("h p n -> p h n")
                             ).then_inc(A[f"in{p}"], 16)
        first_loads("w_out")
        B = S["sa"]
        sp.dma_start(sbias[:], I["sample_bias"]).then_inc(B["bias"], 16)
        for dst, r0 in ((Qall, 0), (Kall, CT)):
            sp.dma_start(dst[:], z[r0 * P:(r0 + CT) * P, SEQ:T].rearrange("(k p) t -> p k t", p=P)
                         ).then_inc(B["qk_in"], 16)

        def rows_of(n, b):
            c = win_c[n][bass.ds(b, 1), :, :].rearrange("b w e -> (b w) e")
            old = c[0:OLD, :].rearrange("(g s) e -> g s e", s=16)[:, 0:ORS, :]
            return old, c[OLD:WBUF, :].rearrange("(p r) e -> p r e", r=RR)

        def load_keys(b, slot):
            old, recent = rows_of("k", b)
            sp.dma_start(Ko[slot][:], old).then_inc(B[f"k{slot}"], 16)
            sp.dma_start(Kr[slot][:], recent).then_inc(B[f"k{slot}"], 16)

        def load_values(b, slot, row):
            old, recent = rows_of("v", b)
            sp.wait_ge(B["v_used"], b + 1)
            sp.dma_start(Vo[:, slot], old).then_inc(B[f"v{slot}"], 16)
            sp.dma_start(Vr[:, slot], recent).then_inc(B[f"v{slot}"], 16)
            sp.dma_start(Vn[:, slot], win_s["v"][bass.ds(row, TS), :]).then_inc(B[f"v{slot}"], 16)

        load_keys(0, 0)
        sp.wait_ge(phase_end, 3 * 5)
        with sp.Fori(0, NB // 2 - 1) as i:
            for q in range(2):
                sp.wait_ge(B["s_full"], i * 2 + (q + 2))
                load_keys(i * 2 + (q + 1), (q + 1) % 2)
                load_values(i * 2 + q, q, i * (2 * TS) + q * TS)
        sp.wait_ge(B["s_full"], NB)
        load_keys(NB - 1, 1)
        for b in (NB - 2, NB - 1):
            load_values(b, b % 2, b * TS)
        M = S["so"]
        sp.wait_ge(phase_end, 3 * 6)
        load_mix(M, mix)
        col_loads("w_out", SLOTS)
        col_loads("w_cq")
        X = S["xa"]
        sp.wait_ge(phase_end, 3 * 8)
        with sp.Fori(0, HX // 2) as i:
            for p in range(2):
                sp.wait_ge(X["o_full"], i * XN + QT * (p + 1))
                sp.dma_start(xq[:, p], zx[bass.ds(i * (2 * HDX) + p * HDX, HDX), 0:SEQ]
                             .rearrange("(k p) t -> p k t", p=P)).then_inc(X[f"in{p}"], 16)
                sp.dma_start(xk[:, p], mkT[bass.ds(i * (2 * HDX) + p * HDX, HDX), :]
                             .rearrange("(k p) t -> p k t", p=P)).then_inc(X[f"in{p}"], 16)
                sp.dma_start(xv[:, p], mem_o["v"][:, :, bass.ds(i * (2 * HDX) + p * HDX, HDX)]
                             ).then_inc(X[f"in{p}"], 16)
        first_loads("w_co")
        Y = S["xs"]
        sp.dma_start(cq[:], zx[:, SEQ:T].rearrange("(k p) t -> p k t", p=P)).then_inc(Y["q_in"], 16)
        with sp.Fori(0, 2) as i:
            for b in range(4):
                sp.wait_ge(Y["t_full"], i * 16 + (4 * b + 4))
                sp.dma_start(cK[:, b % 2], mem_c["k"][bass.ds(i * 4 + b, 1)].rearrange("b p j e -> p (b j) e")
                             ).then_inc(Y[f"k{b % 2}"], 16)
            sp.wait_ge(Y["o_full"], i + 1)
            sp.dma_start(cV[:].rearrange("p b j e -> p b (j e)"),
                         mem_c["v"][bass.ds(i * 4, 4)].rearrange("b p j e -> p b (j e)")).then_inc(Y["v"], 16)
        M = S["sc"]
        sp.wait_ge(phase_end, 3 * 9)
        load_mix(M, mixx)
        col_loads("w_co", SLOTS)
        ffn_loads("ffn2")
        F = S["fin"]
        yp = OUT["y_prompt"].rearrange("b t d -> (b t) d")
        for t in range(QT + 1):
            n = P if t < QT else TSAMP
            sp.wait_ge(F["tok"], F.base["tok"] + 2 * (t + 1))
            dst = yp[t * P:t * P + n, :] if t < QT else OUT["y_sample"].rearrange("b t d -> (b t) d")
            sp.dma_start(dst, ytok[0:n, t % 2, :]).then_inc(F[f"out{t % 2}"], 16)
        sp.wait_ge(F["out0"], F.base["out0"] + 16 * ((QT + 2) // 2))
        sp.wait_ge(F["out1"], F.base["out1"] + 16 * ((QT + 1) // 2))

    @block.gpsimd
    def _(pool):
        pool.memset(ident[:], 0.0).then_inc(setup_done, 1)
        pool.memset(ones[:], 1.0).then_inc(setup_done, 1)
        pool.wait_ge(setup_done, 1)
        pool.affine_select(out=ident[:], in_=ident[:], compare_op=ALU.not_equal, fill=1.0, base=0,
                           pattern=[[-1, P]], channel_multiplier=1).then_inc(setup_done, 1)
        pool.sem_inc(w_split, 2)

        def split(parity, full, m, hi, lo, slot_sem, slot_need, hi_here=True):
            pool.wait_ge(raw_full[parity], full)
            pool.wait_ge(slot_sem, slot_need)
            pool.sem_inc(met, 1)
            if hi_here:
                pool.tensor_copy(hi, raw[:, parity]).then_inc(w_hi, 1)
            pool.wait_ge(w_hi, m + 1)
            pool.tensor_tensor(lo, raw[:, parity], hi.bitcast(F32), ALU.subtract).then_inc(w_split, 1)

        def ffn_split(name, phase):
            u0, c0, r0 = UNIT[name], COL[name], ROW[name]
            with pool.Fori(0, FG) as i:
                for j in range(6):
                    full = i * 48 + 16 * ((u0 + j) // 2 + 1)
                    if j < 4:
                        split(j % 2, full, i * 6 + (u0 + j), wh[:, j], wl[:, j], unit_done, i * 4 + (c0 + j + 1))
                    else:
                        pool.wait_ge(phase_end, 3 * phase)
                        split(j % 2, full, i * 6 + (u0 + j), bh[:, j - 4], bl[:, j - 4], row_done,
                              i * 2 + (r0 + j - 4 + 1))

        def col_split(name, n, first=0, hi_here=True):
            u0, c0 = UNIT[name] + first, COL[name] + first
            with pool.Fori(0, n // 4) as i:
                for j in range(4):
                    split(j % 2, i * 32 + 16 * ((u0 + j) // 2 + 1), i * 4 + (u0 + j), wh[:, j], wl[:, j],
                          unit_done, i * 4 + (c0 + j + 1), hi_here)

        for name, n in plan:
            if name.startswith("ffn"):
                ffn_split(name, {"ffn1": 1, "ffn2": 10}[name])
            elif name == "w_ck":
                col_split(name, SLOTS)
                col_split(name, n - SLOTS, SLOTS, hi_here=False)
            else:
                col_split(name, n, hi_here=name != "w_cv")

    @block.tensor
    def _(pe):
        pe.sem_inc(unit_done, SLOTS)
        pe.sem_inc(row_done, 2)
        pe.wait_ge(setup_done, 3)

        def three(out, w_hi_, w_lo_, a_hi, a_lo, first, last):
            pe.matmul(out, w_hi_, a_hi, start=first, stop=False)
            pe.matmul(out, w_lo_, a_hi, start=False, stop=False)
            return pe.matmul(out, w_hi_, a_lo, start=False, stop=last)

        def norm(s, chunks, sqt):
            for c, (c0, n) in enumerate(chunks):
                for k in range(KT):
                    pe.wait_ge(s["sq"], s.base["sq"] + c * KT + k + 1)
                    pe.matmul(ps[:, 5 + c, 0:n], ones[:], sqt[:, k % 4, 0:n], start=(k == 0),
                              stop=(k == KT - 1)).then_inc(s["summed"], 1)

        def ffn(name, s):
            u0, c0_, r0 = UNIT[name], COL[name], ROW[name]
            with pe.Fori(0, FG) as i:
                for f in range(2):
                    for c, (c0, n) in enumerate(CHUNKS):
                        j = NC * f + c
                        if f == 0:
                            pe.wait_ge(s["h"], s.base["h"] + KT * (c + 1))
                        pe.wait_ge(s["prod"], s.base["prod"] + i * 6 + (j + 1))
                        for gu in range(2):
                            if c == 0:
                                pe.wait_ge(w_split, i * 6 + (u0 + 2 * f + gu + 3))
                            out = ps[:, 2 * (j % 2) + gu, 0:n]
                            w = 2 * f + gu
                            for k in range(KT):
                                mm = three(out, wh[:, w, k], wl[:, w, k], hh[:, k, c0:c0 + n], hl[:, k, c0:c0 + n],
                                           k == 0, k == KT - 1)
                            if c < NC - 1:
                                mm.then_inc(s[("gate", "up")[gu]], 1)
                            else:
                                mm.then_inc(unit_done, 1)
                pe.wait_ge(w_split, i * 6 + (u0 + 8))
                for c, (c0, n) in enumerate(CHUNKS):
                    pe.wait_ge(s["hid"], s.base["hid"] + i * 6 + (NC + c + 2))
                    for d in range(KT):
                        j = c * KT + d
                        pe.wait_ge(s["res"], s.base["res"] + i * (NC * KT) + (j + 1))
                        out = ps[:, 4 + j % 4, 0:n]
                        for f in range(2):
                            mm = three(out, bh[:, f, d], bl[:, f, d], hidh[:, f, c0:c0 + n], hidl[:, f, c0:c0 + n],
                                       f == 0, f == 1)
                        if j < NC * KT - 1:
                            mm.then_inc(s["down"], 1)
                        else:
                            mm.then_inc(row_done, 2)

        def proj(name, s, nunits, chunks, ah, al, h_need):
            u0 = UNIT[name]
            nc_ = len(chunks)
            with pe.Fori(0, nunits // 4) as i:
                for w in range(4):
                    pe.wait_ge(w_split, i * 4 + (u0 + w + 3))
                    for c, (c0, n) in enumerate(chunks):
                        j = w * nc_ + c
                        if w == 0:
                            pe.wait_ge(s["h"], s.base["h"] + h_need(c))
                        pe.wait_ge(s["free"], s.base["free"] + i * (4 * nc_) + (j + 1))
                        out = ps[:, j % 4, 0:n]
                        for k in range(KT):
                            mm = three(out, wh[:, w, k], wl[:, w, k], ah[:, k, c0:c0 + n], al[:, k, c0:c0 + n],
                                       k == 0, k == KT - 1)
                        mm.then_inc(s["part"] if c < nc_ - 1 else unit_done, 1)

        L = S["load"]
        pe.wait_ge(L["small"], L.base["small"] + 16 * 10)
        pe.transpose(ps[:, 0, 0:60], small[:], ident[0:60, 0:60])
        for k in range(CT):
            mm = pe.transpose(ps[:, 1, k * CONVW:(k + 1) * CONVW], taps_in[:, k * P:(k + 1) * P],
                              ident[0:CONVW, 0:CONVW])
        mm.then_inc(L["vecs_t"], 1)
        for t in range(QT + 1):
            n = P if t < QT else TSAMP
            pe.wait_ge(L[f"in{t % 3}"], L.base[f"in{t % 3}"] + 16 * (t // 3 + 1))
            for h in range(2):
                j = 2 * t + h
                if j >= 4:
                    pe.wait_ge(L["xin_free"], L.base["xin_free"] + j - 3)
                for k in range(4):
                    kk = 4 * h + k
                    mm = pe.transpose(ps[:, 2 + j % 4, k * P:k * P + n], xin[0:n, t % 3, kk * P:(kk + 1) * P],
                                      ident[0:n, 0:n])
                mm.then_inc(L["xt"], 1)
        C = S["conv"]
        pe.wait_ge(C["cc_in"], 16)
        for k in range(CT):
            for a in range(2):
                mm = pe.transpose(ps[:, 6 + k // 2, ((k % 2) * 2 + a) * 120:((k % 2) * 2 + a) * 120 + 120],
                                  cc_in[:, a, k * P:(k + 1) * P], ident[0:120, 0:120])
        mm.then_inc(C["cct"], 1)
        barrier(pe, 1)
        norm(S["n1"], CHUNKS, sq)
        ffn("ffn1", S["n1"])
        barrier(pe, 2)
        norm(S["nm"], CHUNKS, sq3)
        proj("w_in", S["nm"], 20, CHUNKS, h3h, h3l, lambda c: KT * (c + 1))
        barrier(pe, 3)
        M, C = S["mem"], S["conv"]
        pe.wait_ge(M["in"], M.base["in"] + 16)
        for t in range(2):
            for h in range(2):
                for k in range(4):
                    kk = 4 * h + k
                    mm = pe.transpose(ps[:, 2 * t + h, k * P:(k + 1) * P], min_[:, t, kk * P:(kk + 1) * P], ident[:])
                mm.then_inc(M["xt"], 1)
        for k in range(CT):
            pe.wait_ge(C["ug"], k + 1)
            if k >= 1:
                pe.wait_ge(C["ucs"], 2 * k)
            pe.transpose(ps[0:PAD, 4, 0:P], U[:, k, SEQ:SEQ + PAD], ident[:])
            for a in range(2):
                mm = pe.transpose(ps[0:120, 4, (a + 1) * P:(a + 2) * P], cct[:, k, a, :], ident[:])
            mm.then_inc(C["ut"], 1)
        norm(M, [(0, NMEM)], msq)
        pe.wait_ge(C["ucs"], 2 * CT)
        for c, (c0, n) in enumerate(CHUNKS):
            for k in range(CT):
                mm = pe.matmul(ps[:, LNB[c], 0:n], ones[:], ya[:, k, c0:c0 + n], start=(k == 0), stop=(k == CT - 1))
            mm.then_inc(C["mean"], 1)
        for name, n in (("w_ck", "mk"), ("w_cv", "mv")):
            s = S["mk"]
            u0 = UNIT[name]
            with pe.Fori(0, 2) as i:
                for w in range(4):
                    pe.wait_ge(w_split, i * 4 + (u0 + w + 3))
                    pe.wait_ge(M["h"], M.base["h"] + KT)
                    pe.wait_ge(s[n + "_free"], s.base[n + "_free"] + i * 4 + (w + 1))
                    for k in range(KT):
                        mm = three(ps[:, w, 0:NMEM], wh[:, w, k], wl[:, w, k], mh[:, k], ml[:, k], k == 0, k == KT - 1)
                    mm.then_inc(unit_done, 1)
            for t in range(2):
                for h in range(2):
                    j = 2 * t + h
                    pe.wait_ge(s[n + "_free"], s.base[n + "_free"] + 12)
                    for k in range(4):
                        kk = 4 * h + k
                        mm = pe.transpose(ps[:, j, k * P:(k + 1) * P], kvT[:, kk, t * P:(t + 1) * P], ident[:])
                    mm.then_inc(s[n + "_t"], 1)
            if n == "mk":
                for c, (c0, w) in enumerate(CHUNKS):
                    for k in range(CT):
                        pe.wait_ge(C["sq"], c * CT + k + 1)
                        mm = pe.matmul(ps[:, LNB[c], 0:w], ones[:], U[:, k, c0:c0 + w], start=(k == 0),
                                       stop=(k == CT - 1))
                    mm.then_inc(C["summed"], 1)
            pe.wait_ge(s[n + "_tok"], s.base[n + "_tok"] + 4)
        barrier(pe, 4)
        A = S["pa"]
        pe.sem_inc(A["s_full"], WN)
        pe.wait_ge(A["tok_in"], 32)
        for a in range(2):
            for k in range(CT):
                mm = pe.transpose(ps[0:TSAMP, 6 + a, k * P:(k + 1) * P], ks[:, a, k, :], ident[:])
            mm.then_inc(A["tok_t"], 1)
        pe.wait_ge(A["tok_e"], 2)
        with pe.Fori(0, H // 4) as i:
            tf = [0]
            upto = {}

            def tbank():
                b = 4 + tf[0] % 2
                pe.wait_ge(A["t_free"], i * WT + (tf[0] + 1))
                tf[0] += 1
                return b

            def tokens(src, p, half):
                b = tbank()
                for k in range(4):
                    mm = pe.transpose(ps[:, b, k * P:(k + 1) * P], src[:, p, (4 * half + k) * P:(4 * half + k + 1) * P],
                                      ident[:])
                mm.then_inc(A["t_full"], 1)

            def scores(n):
                p, h, t = wsteps[n]
                if n % WP == 0:
                    pe.wait_ge(A[f"in{p}"], i * 64 + 64)
                pe.wait_ge(A["s_free"], i * WN + (WN + n - 1))
                for c in range(1 + (t >= 4)):
                    w = min(512, P * (t + 1) - 512 * c)
                    mm = pe.matmul(ps[:, 2 * (n % 2) + c, 0:w], qT[64 * h:64 * h + 64, p, t * P:(t + 1) * P],
                                   kTp[64 * h:64 * h + 64, p, 512 * c:512 * c + w], start=True, stop=True)
                mm.then_inc(A["s_full"], 1)

            def turn(n):
                p, h, t = wsteps[n]
                for kind, c in turns(n):
                    if kind != "p":
                        tokens(vT if kind == "v" else kTp, 1, c)
                        continue
                    if c == 0:
                        pe.wait_ge(A["p"], i * WN + (n + 1))
                    b = tbank()
                    for k in range(4 * c, min(4 * c + 4, t + 1)):
                        mm = pe.transpose(ps[:, b, (k % 4) * P:(k % 4 + 1) * P], Sb[:, n % 3, k * P:(k + 1) * P],
                                          ident[:])
                    mm.then_inc(A["t_full"], 1)
                upto[n] = tf[0]

            def values(n):
                p, h, t = wsteps[n]
                pe.wait_ge(A["t_free"], i * WT + (upto[n] + 2))
                pe.wait_ge(A["o_free"], i * WN + (n + 1))
                for k in range(t + 1):
                    mm = pe.matmul(ps[64 * h:64 * h + 64, 6 + n % 2, 0:P], vtok[:, p, k, 64 * h:64 * h + 64],
                                   PT[:, n % 2, k, :], start=(k == 0), stop=(k == t))
                mm.then_inc(A["o_full"], 1)

            scores(0)
            scores(1)
            for src in (vT, kTp):
                for half in range(2):
                    tokens(src, 0, half)
            for n in range(WN):
                if n + 2 < WN:
                    scores(n + 2)
                turn(n)
                if n >= 1:
                    values(n - 1)
            values(WN - 1)
        barrier(pe, 5)
        B = S["sa"]
        pe.sem_inc(B["s_full"], 2)
        pe.sem_inc(B["v_used"], 2)
        with pe.Fori(0, NB // SQ) as i:
            def bank_of(j):
                pe.wait_ge(B[("t_freea", "t_freed")[j % 2]], i * (SJ // 2) + (j // 2 + 1))
                return j % 2

            def evacuated(j):
                pe.wait_ge(B[("t_freea", "t_freed")[j % 2]], i * (SJ // 2) + (j // 2 + 2))

            def key_group(q, g):
                c, k = divmod(g, CT)
                if g == 0:
                    pe.wait_ge(B[f"k{q % 2}"], i * (16 * SQ) + 32 * (q // 2 + 1))
                bank = bank_of(key_job(q, g))
                for r in range(4):
                    if c < 2:
                        src, w = Ko[q % 2][:, 4 * c + r, k * P:(k + 1) * P], OG
                    else:
                        src, w = Kr[q % 2][:, r, k * P:(k + 1) * P], P
                    mm = pe.transpose(ps[:, bank, r * w:(r + 1) * w], src, ident[0:w, 0:w])
                mm.then_inc(B["t_full"], 1)

            def score_group(q, g):
                c, k = divmod(g, CT)
                if q % 2 == 0 and g == 0:
                    pe.wait_ge(B["q"], i * (2 * H) + H * (q // 2 + 1))
                evacuated(key_job(q, g))
                if g == 0:
                    pe.wait_ge(B["s_free"], i * SQ + (q + 1))
                w = 4 * (OG if c < 2 else P)
                mm = pe.matmul(ps[0:64, 2 + c, 0:w], Qc[:, q % 2, k, :], Kc[:, g % 4, 0:w], start=(k == 0),
                               stop=(k == CT - 1))
                if g == KG - 1:
                    for k in range(CT):
                        mm = pe.matmul(ps[0:64, 5, 0:TS], Qc[:, q % 2, k, :],
                                       Kall[:, k, bass.ds(i * (SQ * TS) + q * TS, TS)], start=(k == 0),
                                       stop=(k == CT - 1))
                    mm.then_inc(B["s_full"], 1)

            def probabilities(q, part):
                j = prob_job(q) + part
                if part == 0:
                    pe.wait_ge(B["p"], i * SQ + (q + 1))
                bank = bank_of(j)
                pe.sem_inc(met, 1)
                for blk in (range(8), range(8, 13))[part]:
                    w, off = block_of(blk)
                    mm = pe.transpose(ps[0:w, bank, (blk % 8) * 64:(blk % 8) * 64 + 64], Ss[:, off:off + w],
                                      ident[0:64, 0:64])
                mm.then_inc(B["t_full"], 1)

            def values(q):
                evacuated(prob_job(q))
                evacuated(prob_job(q) + 1)
                pe.wait_ge(B[f"v{q % 2}"], i * (24 * SQ) + 48 * (q // 2 + 1))
                for blk in range(13):
                    w, _ = block_of(blk)
                    v = Vo[:, q % 2, blk, :] if blk < ORS else Vr[:, q % 2, blk - ORS, :] if blk < 12 else Vn[:, q % 2, :]
                    mm = pe.matmul(ps[0:64, 6, :], PTs[0:w, blk, :], v, start=(blk == 0), stop=(blk == 12))
                mm.then_inc(B["v_used"], 1)

            def turn_output(q):
                pe.wait_ge(B["ov"], i * SQ + (q + 1))
                pe.wait_ge(B["o_free"], i * (2 * SQ) + (2 * q + 1))
                pe.sem_inc(met, 1)
                for k in range(CT):
                    mm = pe.transpose(ps[:, 7, k * 64:(k + 1) * 64], OV[:, k * P:(k + 1) * P], ident[0:64, 0:64])
                mm.then_inc(B["ot"], 1)

            for q in range(SQ):
                for g in range(KG):
                    key_group(q, g)
                    if g >= 2:
                        score_group(q, g - 2)
                    if g == 1 and q >= 2:
                        values(q - 2)
                    if g == 6 and q >= 2:
                        turn_output(q - 2)
                if q >= 1:
                    probabilities(q - 1, 0)
                score_group(q, KG - 2)
                if q >= 1:
                    probabilities(q - 1, 1)
                score_group(q, KG - 1)
            values(SQ - 2)
            probabilities(SQ - 1, 0)
            probabilities(SQ - 1, 1)
            turn_output(SQ - 2)
            values(SQ - 1)
            turn_output(SQ - 1)
        barrier(pe, 6)
        proj("w_out", S["so"], 8, CHUNKS, hh, hl, lambda c: KT * (c + 1))
        barrier(pe, 7)
        norm(S["nx"], CHUNKS, sq)
        proj("w_cq", S["nx"], 8, CHUNKS, hh, hl, lambda c: KT * (c + 1))
        barrier(pe, 8)
        X = S["xa"]
        pe.sem_inc(X["o_full"], XN)
        with pe.Fori(0, HX // 2) as i:
            def xscores(n):
                p, t = xsteps[n]
                if t == 0:
                    pe.wait_ge(X[f"in{p}"], i * 48 + 48)
                pe.wait_ge(X["e"], i * XN + (n + 1))
                for k in range(2):
                    mm = pe.matmul(ps[:, n % 2, 0:NMEM], xq[:, p, k, t * P:(t + 1) * P], xk[:, p, k, :],
                                   start=(k == 0), stop=(k == 1))
                mm.then_inc(X["s_full"], 1)

            def xturn(n):
                pe.wait_ge(X["p"], i * XN + (n + 1))
                pe.wait_ge(X["t_free"], i * XN + (n + 1))
                for k in range(2):
                    mm = pe.transpose(ps[:, 2 + n % 2, k * P:(k + 1) * P], Xb[:, n % 3, k * P:(k + 1) * P], ident[:])
                mm.then_inc(X["t_full"], 1)

            def xvalues(n):
                p, t = xsteps[n]
                pe.wait_ge(X["t_free"], i * XN + (n + 3))
                pe.wait_ge(X["o_free"], i * XN + (n + 1))
                for d in range(2):
                    for k in range(2):
                        mm = pe.matmul(ps[:, 4 + n % 2, d * P:(d + 1) * P], xv[:, p, k, d * P:(d + 1) * P],
                                       XT[:, n % 2, k, :], start=(k == 0), stop=(k == 1))
                mm.then_inc(X["o_full"], 1)

            xscores(0)
            xscores(1)
            for n in range(XN):
                if n + 2 < XN:
                    xscores(n + 2)
                xturn(n)
                if n >= 1:
                    xvalues(n - 1)
            xvalues(XN - 1)
        Y = S["xs"]
        pe.sem_inc(Y["s_full"], 2)
        pe.sem_inc(Y["t_full"], 8)
        pe.sem_inc(Y["o_full"], 1)
        with pe.Fori(0, 2) as i:
            def turn_keys(b):
                pe.wait_ge(Y[f"k{b % 2}"], i * 32 + 16 * (b // 2 + 1))
                for m in range(4):
                    pe.wait_ge(Y[("t_freea", "t_freed")[m % 2]], i * 8 + (b * 2 + m // 2 + 1))
                    for k in range(2):
                        for j in range(2):
                            mm = pe.transpose(ps[:, m % 2, k * 256 + j * P:k * 256 + (j + 1) * P],
                                              cK[:, b % 2, j, (2 * m + k) * P:(2 * m + k + 1) * P], ident[:])
                    mm.then_inc(Y["t_full"], 1)

            turn_keys(0)
            for b in range(4):
                if b < 3:
                    turn_keys(b + 1)
                pe.wait_ge(Y["t_freea"], i * 8 + (b * 2 + 3))
                pe.wait_ge(Y["t_freed"], i * 8 + (b * 2 + 3))
                if b == 0:
                    pe.wait_ge(Y["qc"], i * 4 + 4)
                    pe.wait_ge(Y["e"], i + 1)
                for k in range(KT):
                    mm = pe.matmul(ps[32 * b:32 * b + 32, 2, 0:NMEM], cqc[:, b, k, :], cKT[:, b % 2, k, :],
                                   start=(k == 0), stop=(k == KT - 1))
                mm.then_inc(Y["s_full"], 1)
            pe.wait_ge(Y["p"], i + 1)
            for j in range(2):
                mm = pe.transpose(ps[:, 3, j * P:(j + 1) * P], cS[:, j * P:(j + 1) * P], ident[:])
            mm.then_inc(Y["pt_full"], 1)
            pe.wait_ge(Y["pt"], i + 1)
            pe.wait_ge(Y["v"], i * 16 + 16)
            for b in range(4):
                for half in range(2):
                    for j in range(2):
                        mm = pe.matmul(ps[32 * b:32 * b + 32, 4 + half, :], cPT[:, j, 32 * b:32 * b + 32],
                                       cV[:, b, j, 512 * half:512 * half + 512], start=(j == 0), stop=(j == 1))
            mm.then_inc(Y["o_full"], 1)
            pe.wait_ge(Y["ov"], i * 2 + 2)
            pe.wait_ge(Y["oe"], i * HX + 1)
            for k in range(KT):
                mm = pe.transpose(ps[:, 6 + k // 4, (k % 4) * P:(k % 4 + 1) * P], cO[:, k * P:(k + 1) * P], ident[:])
            mm.then_inc(Y["ot"], 1)
        barrier(pe, 9)
        proj("w_co", S["sc"], 8, CHUNKS, hh, hl, lambda c: KT * (c + 1))
        barrier(pe, 10)
        norm(S["n2"], CHUNKS, sq)
        ffn("ffn2", S["n2"])
        barrier(pe, 11)
        F = S["fin"]
        norm(F, CHUNKS, sq)
        for t in range(QT + 1):
            n = P if t < QT else TSAMP
            pe.wait_ge(F["h"], F.base["h"] + KT * ([c for c, (c0, w) in enumerate(CHUNKS) if t * P < c0 + w][0] + 1))
            for h in range(2):
                j = 2 * t + h
                if j >= 4:
                    pe.wait_ge(F["tok"], F.base["tok"] + j - 3)
                for k in range(4):
                    mm = pe.transpose(ps[0:n, j % 4, k * P:(k + 1) * P], x[:, 4 * h + k, t * P:t * P + n], ident[:])
                mm.then_inc(F["yt"], 1)

    @block.scalar
    def _(act):
        def norm(s, chunks, src, sqt, rst, tbt, hit, split=True):
            for what, c, m in norm_order(len(chunks)):
                c0, n = chunks[c]
                if what == "sq":
                    j = c * KT + m
                    if j >= 4:
                        act.wait_ge(s["summed"], s.base["summed"] + j - 3)
                    act.activation(sqt[:, j % 4, 0:n], src[:, m, c0:c0 + n], ACT.Square).then_inc(s["sq"], 1)
                elif what == "var":
                    act.wait_ge(s["var"], s.base["var"] + c + 1)
                    act.activation(rst[:, c, 0:n], rst[:, c, 0:n], ACT.Sqrt).then_inc(s["std"], 1)
                elif what == "tile" and split:
                    j = c * KT + m
                    act.wait_ge(s["t"], s.base["t"] + j + 1)
                    act.copy(hit[:, m, c0:c0 + n], tbt[:, j % 3, 0:n]).then_inc(s["hi"], 1)

        def ffn(name, s):
            c0_ = COL[name]
            with act.Fori(0, FG) as i:
                def silu(j):
                    f, c = divmod(j, NC)
                    n = CHUNKS[c][1]
                    if c < NC - 1:
                        act.wait_ge(s["gate"], s.base["gate"] + i * 4 + (2 * f + c + 1))
                    else:
                        act.wait_ge(unit_done, i * 4 + (SLOTS + c0_ + 2 * f + 1))
                    act.wait_ge(s["prod"], s.base["prod"] + i * 6 + (j + 1))
                    act.activation(sg[:, j % 2, 0:n], ps[:, 2 * (j % 2), 0:n], ACT.Silu).then_inc(s["sg"], 1)

                def hi(j):
                    f, c = divmod(j, NC)
                    c0, n = CHUNKS[c]
                    act.wait_ge(s["prod"], s.base["prod"] + i * 6 + (j + 3))
                    act.copy(hidh[:, f, c0:c0 + n], ht[:, j % 2, 0:n]).then_inc(s["hhi"], 1)

                for j in range(2 * NC):
                    silu(j)
                    if j >= 1:
                        hi(j - 1)
                hi(2 * NC - 1)

        def store_proj(name, s, stg, nunits, first, dst):
            with act.Fori(0, nunits // 4) as i:
                for w in range(4):
                    act.wait_ge(s[f"st{w % 2}"], s.base[f"st{w % 2}"] + i * 32 + 16 * (w // 2 + 1))
                    for c, (c0, n) in enumerate(CHUNKS):
                        j = w * NC + c
                        if c < NC - 1:
                            act.wait_ge(s["part"], s.base["part"] + i * 8 + (2 * (first + w) + c + 1))
                        else:
                            act.wait_ge(unit_done, i * 4 + (SLOTS + COL[name] + first + w + 1))
                        act.copy(stg[:, w % 2, c0:c0 + n], ps[:, j % 4, 0:n]).then_inc(s["free"], 1)
                    act.wait_ge(s["free"], s.base["free"] + i * 12 + (4 + NC * (first + w + 1)))
                    act.dma_start(dst[bass.ds(i * (4 * P) + w * P, P), :], stg[:, w % 2, :]
                                  ).then_inc(s[f"st{w % 2}"], 16)
            for w in range(2):
                act.wait_ge(s[f"st{w}"], s.base[f"st{w}"] + 8 * nunits + 16)

        def gate_units(s):
            C = S["conv"]
            with act.Fori(0, CT // 2) as i:
                for w in range(4):
                    k = bass.ds(i * 2 + w // 2, 1)
                    for c, (c0, n) in enumerate(CHUNKS):
                        bank = (w * NC + c) % 4
                        if c < NC - 1:
                            act.wait_ge(s["part"], s.base["part"] + i * 8 + (2 * w + c + 1))
                        else:
                            act.wait_ge(unit_done, i * 4 + (SLOTS + COL["w_in"] + w + 1))
                        if w % 2:
                            act.activation(ya[:, k, c0:c0 + n], ps[:, bank:bank + 1, 0:n], ACT.Sigmoid
                                           ).then_inc(s["free"], 1)
                            continue
                        np_ = min(n, SEQ - c0)
                        cp = act.copy(U[:, k, PAD + c0:PAD + c0 + np_], ps[:, bank:bank + 1, 0:np_])
                        if np_ < n:
                            cp = act.copy(Us[:, k, :, PAD:PAD + TS],
                                          ps[:, bank:bank + 1, np_:n].rearrange("p o (b t) -> p o b t", t=TS))
                        cp.then_inc(s["free"], 1)

        def split_input(s):
            for c, (c0, n) in enumerate(CHUNKS):
                act.wait_ge(s[f"in{c}"], s.base[f"in{c}"] + 16)
                for k in range(KT):
                    act.copy(hh[:, k, c0:c0 + n], mixin[:, c, k, 0:n]).then_inc(s["hi"], 1)

        for w in range(2):
            act.sem_inc(S["nm"][f"st{w}"], 16)
        barrier(act, 1)
        norm(S["n1"], CHUNKS, x, sq, rs, tb, hh)
        ffn("ffn1", S["n1"])
        barrier(act, 2)
        norm(S["nm"], CHUNKS, x, sq3, rs3, tb3, h3h)
        gate_units(S["nm"])
        store_proj("w_in", S["nm"], stage3, 3 * CT, 2 * CT, z)
        barrier(act, 3)
        M, C, s = S["mem"], S["conv"], S["mk"]
        act.sem_inc(s["mk_free"], 4)
        act.sem_inc(s["mv_free"], 4)
        for k in range(CT):
            act.wait_ge(C["ut"], k + 1)
            act.copy(ucs[0:PAD, 0, k * P:(k + 1) * P], ps[0:PAD, 4, 0:P]).then_inc(C["ucs"], 1)
            act.copy(ucs[:, 1:3, k * P:(k + 1) * P], ps[0:4 * PAD, 4, P:3 * P].rearrange("p (a c) -> p a c", a=2)
                     ).then_inc(C["ucs"], 1)
        act.wait_ge(C["ucs"], 2 * CT)
        act.dma_start(new_conv_p, ucs[0:PAD, 0, :]).then_inc(C["ucst"], 16)
        act.dma_start(new_conv_s, ucs[:, 1:3, :]).then_inc(C["ucst"], 16)
        act.wait_ge(M["ev"], M.base["ev"] + 4)
        norm(M, [(0, NMEM)], memT, msq, mrs, mtb, mh)
        for c, (c0, n) in enumerate(CHUNKS):
            for k in range(CT):
                act.wait_ge(C["xc"], c * CT + k + 1)
                act.activation(U[:, k, c0:c0 + n], ya[:, k, c0:c0 + n], ACT.Square).then_inc(C["sq"], 1)
        for name, n in (("w_ck", "mk"), ("w_cv", "mv")):
            if n == "mv":
                act.wait_ge(s["mkst"], s.base["mkst"] + 16)
            for half in range(2):
                for w in range(4):
                    act.wait_ge(unit_done, SLOTS + COL[name] + 4 * half + w + 1)
                    act.copy(kvT[:, 4 * half + w, :], ps[:, w, 0:NMEM]).then_inc(s[n + "_free"], 1)
                    if (n, half) != ("mv", 1):
                        u = UNIT[name] + 4 * half + w + SLOTS
                        act.wait_ge(raw_full[u % 2], 16 * (u // 2 + 1))
                        act.wait_ge(w_hi, u)
                        act.copy(wh[:, w], raw[:, u % 2]).then_inc(w_hi, 1)
                if (n, half) == ("mv", 0):
                    for k in range(CT):
                        act.wait_ge(C["ln"], CT * (NC - 1) + k + 1)
                        act.activation(ya[:, k, :], ya[:, k, :], ACT.Silu, bias=vecs[:, V_LB + k:V_LB + k + 1]
                                       ).then_inc(C["ob"], 1)
                    act.wait_ge(C["ob"], CT)
                    act.dma_start(mix[CT * P:KT * P, :].rearrange("(k p) t -> p k t", p=P), ya[:]).then_inc(C["obst"], 16)
            if n == "mk":
                act.wait_ge(s["mk_free"], s.base["mk_free"] + 12)
                act.dma_start(mkT.rearrange("(k p) t -> p k t", p=P), kvT[:]).then_inc(s["mkst"], 16)
            for t in range(2):
                for h in range(2):
                    j = 2 * t + h
                    act.wait_ge(s[n + "_t"], s.base[n + "_t"] + j + 1)
                    if n == "mv" and j == 0:
                        act.wait_ge(s["kvst"], s.base["kvst"] + 16)
                    act.copy(kvtok[:, t, 512 * h:512 * h + 512], ps[:, j, :]).then_inc(s[n + "_tok"], 1)
            act.wait_ge(s[n + "_tok"], s.base[n + "_tok"] + 4)
            act.dma_start(mem_o[n[1]], kvtok[:]).then_inc(s["kvst"], 16)
            if n == "mk":
                for c, (c0, w) in enumerate(CHUNKS):
                    act.wait_ge(C["var"], c + 1)
                    act.activation(mrs[:, c, 0:w], mrs[:, c, 0:w], ACT.Sqrt).then_inc(C["std"], 1)
        act.wait_ge(C["obst"], 16)
        act.wait_ge(C["ucst"], 32)
        act.wait_ge(s["kvst"], s.base["kvst"] + 32)
        act.wait_ge(s["mkst"], s.base["mkst"] + 16)
        barrier(act, 4)
        A = S["pa"]
        act.sem_inc(A["t_free"], 2)
        act.sem_inc(A["kst"], 32)
        for a in range(2):
            act.wait_ge(A["tok_t"], a + 1)
            act.copy(kvs[:, a, :], ps[0:TSAMP, 6 + a, :]).then_inc(A["tok_e"], 1)
        act.wait_ge(A["tok_e"], 2)
        act.dma_start(win_s["k"], kvs[:, 0, :]).then_inc(A["tokst"], 16)
        act.dma_start(win_s["v"], kvs[:, 1, :]).then_inc(A["tokst"], 16)
        with act.Fori(0, H // 4) as i:
            tf = [0]

            def evac(dst):
                act.wait_ge(A["t_full"], i * WT + (tf[0] + 1))
                nb = dst.shape[1]
                act.copy(dst, ps[:, 4 + tf[0] % 2, 0:nb * P].rearrange("p (k c) -> p k c", c=P)
                         ).then_inc(A["t_free"], 1)
                tf[0] += 1

            def tokens(kind, p, half):
                if kind == "v" and half == 0:
                    act.wait_ge(A["kst"], i * 64 + (32 + 32 * p))
                dst = vtok if kind == "v" else ktok
                evac(dst[:, p, 4 * half:4 * half + 4, :])
                if half == 1:
                    act.wait_ge(A["t_free"], i * WT + (tf[0] + 2))
                    act.dma_start(win_p[kind][:, :, bass.ds(i * (2 * P) + p * P, P)], dst[:, p]).then_inc(A["kst"], 16)

            def exp(n):
                p, h, t = wsteps[n]
                act.wait_ge(A["m"], i * WN + (n + 1))
                w = P * (t + 1)
                act.activation(Sb[:, n % 3, 0:w], Sb[:, n % 3, 0:w], ACT.Exp, bias=stat[:, n % 4, 1:2], scale=0.125,
                               accum_out=stat[:, n % 4, 2:3]).then_inc(A["e"], 1)

            def store(p):
                act.wait_ge(A["o_free"], i * WN + (2 + WP * (p + 1)))
                act.dma_start(mix[bass.ds(i * (2 * P) + p * P, P), 0:SEQ], oT[:, p]).then_inc(A[f"ost{p}"], 16)

            exp(0)
            exp(1)
            for kind in "vk":
                for half in range(2):
                    tokens(kind, 0, half)
            for n in range(WN):
                p, h, t = wsteps[n]
                for kind, c in turns(n):
                    if kind != "p":
                        tokens(kind, 1, c)
                        continue
                    if n >= 2 and c == 0:
                        act.wait_ge(A["o_full"], i * WN + (n - 1))
                    evac(PT[:, n % 2, 4 * c:min(4 * c + 4, t + 1), :])
                if n + 2 < WN:
                    exp(n + 2)
                if n == WP + 3:
                    store(0)
            store(1)
        act.wait_ge(A["kst"], 32 * (H // 2) + 32)
        for p in range(2):
            act.wait_ge(A[f"ost{p}"], 16 * (H // 4) + 16)
        act.wait_ge(A["tokst"], 32)
        barrier(act, 5)
        B = S["sa"]
        act.sem_inc(B["t_freea"], 1)
        with act.Fori(0, NB // SQ) as i:
            def key_evac(q, g):
                j = key_job(q, g)
                w = 4 * (OG if g < 2 * CT else P)
                act.wait_ge(B["t_full"], i * SJ + (j + 1))
                act.copy(Kc[:, g % 4, 0:w], ps[:, 0, 0:w]).then_inc(B["t_freea"], 1)

            def exp(q):
                act.wait_ge(B["m"], i * SQ + (q + 1))
                act.activation(Ss[:], Ss[:], ACT.Exp, bias=sstat[:, 5:6], scale=0.125, accum_out=sstat[:, 6:7]
                               ).then_inc(B["e"], 1)

            def prob_evac(q):
                act.wait_ge(B["t_full"], i * SJ + (prob_job(q) + 1))
                act.copy(PTs[0:OG, 0:8, :], ps[0:OG, 0, :].rearrange("p (k c) -> p k c", c=64)
                         ).then_inc(B["t_freea"], 1)

            def value_evac(q):
                act.wait_ge(B["v_used"], i * SQ + (q + 3))
                act.copy(OV[:], ps[0:64, 6, :]).then_inc(B["ov"], 1)

            for q in range(SQ):
                for g in range(0, KG, 2):
                    key_evac(q, g)
                    if g == 0 and q >= 1:
                        exp(q - 1)
                    if g == 0 and q >= 2:
                        value_evac(q - 2)
                if q >= 1:
                    prob_evac(q - 1)
            exp(SQ - 1)
            value_evac(SQ - 2)
            prob_evac(SQ - 1)
            value_evac(SQ - 1)
        act.wait_ge(B["o_free"], 1 + 2 * NB)
        act.dma_start(mix[0:CT * P, SEQ:T].rearrange("(k p) t -> p k t", p=P),
                      oS[:].rearrange("p k b t -> p k (b t)")).then_inc(B["ost"], 16)
        act.wait_ge(B["ost"], 16)
        barrier(act, 6)
        split_input(S["so"])
        barrier(act, 7)
        norm(S["nx"], CHUNKS, x, sq, rs, tb, hh)
        store_proj("w_cq", S["nx"], stage, KT, 0, zx)
        barrier(act, 8)
        X = S["xa"]
        act.sem_inc(X["t_free"], 2)
        act.sem_inc(X["e"], 2)
        with act.Fori(0, HX // 2) as i:
            def xexp(n):
                act.wait_ge(X["m"], i * XN + (n + 1))
                act.activation(Xb[:, n % 3, :], ps[:, n % 2, 0:NMEM], ACT.Exp, bias=xstat[:, n % 4, 1:2],
                               scale=HDX ** -0.5, accum_out=xstat[:, n % 4, 2:3]).then_inc(X["e"], 1)

            def xstore(p):
                act.wait_ge(X["o_free"], i * XN + (2 + QT * (p + 1)))
                act.dma_start(mixx[bass.ds(i * (2 * HDX) + p * HDX, HDX), 0:SEQ].rearrange("(k p) t -> p k t", p=P),
                              xo[:, p]).then_inc(X[f"ost{p}"], 16)

            xexp(0)
            xexp(1)
            for n in range(XN):
                act.wait_ge(X["t_full"], i * XN + (n + 1))
                if n >= 2:
                    act.wait_ge(X["o_full"], i * XN + (XN + n - 1))
                act.copy(XT[:, n % 2], ps[:, 2 + n % 2, 0:2 * P].rearrange("p (k c) -> p k c", c=P)
                         ).then_inc(X["t_free"], 1)
                if n + 2 < XN:
                    xexp(n + 2)
                if n == QT + 3:
                    xstore(0)
            xstore(1)
        Y = S["xs"]
        act.sem_inc(Y["t_freea"], 1)
        act.sem_inc(Y["e"], 1)
        with act.Fori(0, 2) as i:
            for b in range(4):
                for m in (0, 2):
                    act.wait_ge(Y["t_full"], i * 16 + (b * 4 + m + 9))
                    act.copy(cKT[:, b % 2, 2 * m:2 * m + 2, :], ps[:, 0, :].rearrange("p (k c) -> p k c", k=2)
                             ).then_inc(Y["t_freea"], 1)
            act.wait_ge(Y["m"], i + 1)
            act.activation(cS[:], ps[:, 2, 0:NMEM], ACT.Exp, bias=cstat[:, 1:2], scale=HDX ** -0.5,
                           accum_out=cstat[:, 2:3]).then_inc(Y["e"], 1)
            act.wait_ge(Y["pt_full"], i + 1)
            act.copy(cPT[:], ps[:, 3, 0:2 * P].rearrange("p (k c) -> p k c", c=P)).then_inc(Y["pt"], 1)
            act.wait_ge(Y["o_full"], i + 2)
            act.copy(cO[:, 0:512], ps[:, 4, :]).then_inc(Y["ov"], 1)
        act.wait_ge(Y["oe"], 2 * HX + 1)
        act.dma_start(mixx[:, SEQ:T].rearrange("(k p) t -> p k t", p=P), co[:].rearrange("p k b t -> p k (b t)")
                      ).then_inc(Y["ost"], 16)
        for p in range(2):
            act.wait_ge(X[f"ost{p}"], 16 * (HX // 2) + 16)
        act.wait_ge(Y["ost"], 16)
        barrier(act, 9)
        split_input(S["sc"])
        barrier(act, 10)
        norm(S["n2"], CHUNKS, x, sq, rs, tb, hh)
        ffn("ffn2", S["n2"])
        barrier(act, 11)
        F = S["fin"]
        norm(F, CHUNKS, x, sq, rs, tb, hh, split=False)
        for t in range(QT + 1):
            n = P if t < QT else TSAMP
            for h in range(2):
                act.wait_ge(F["yt"], F.base["yt"] + 2 * t + h + 1)
                if t >= 2:
                    act.wait_ge(F[f"out{t % 2}"], F.base[f"out{t % 2}"] + 16 * (t // 2))
                act.copy(ytok[0:n, t % 2, 512 * h:512 * h + 512], ps[0:n, (2 * t + h) % 4, :]).then_inc(F["tok"], 1)

    @block.vector
    def _(dve):
        def norm(s, chunks, src, sqt, rst, tbt, gain, hit, lot, split=True):
            def lo(j):
                c, k = divmod(j, KT)
                c0, n = chunks[c]
                dve.wait_ge(s["hi"], s.base["hi"] + j + 1)
                dve.tensor_tensor(lot[:, k, c0:c0 + n], tbt[:, j % 3, 0:n], hit[:, k, c0:c0 + n].bitcast(F32),
                                  ALU.subtract).then_inc(s["h"], 1)

            for what, c, m in norm_order(len(chunks)):
                c0, n = chunks[c]
                if what == "var":
                    dve.wait_ge(s["summed"], s.base["summed"] + KT * (c + 1))
                    dve.tensor_scalar(rst[:, c, 0:n], ps[:, 5 + c, 0:n], 1.0 / D, EPS, ALU.mult, ALU.add
                                      ).then_inc(s["var"], 1)
                elif what == "inv":
                    dve.wait_ge(s["std"], s.base["std"] + c + 1)
                    dve.reciprocal(rst[:, c, 0:n], rst[:, c, 0:n]).then_inc(s["rstd"], 1)
                elif what == "tile":
                    j = c * KT + m
                    dve.wait_ge(s["rstd"], s.base["rstd"] + c + 1)
                    if split and j >= 3:
                        dve.wait_ge(s["h"], s.base["h"] + j - 2)
                    out, done = (tbt[:, j % 3, 0:n], "t") if split else (src[:, m, c0:c0 + n], "h")
                    dve.scalar_tensor_tensor(out=out, in0=src[:, m, c0:c0 + n],
                                             scalar=vecs[:, gain + m:gain + m + 1], in1=rst[:, c, 0:n], op0=ALU.mult,
                                             op1=ALU.mult).then_inc(s[done], 1)
                    if split and j >= 1:
                        lo(j - 1)
            if split:
                lo(KT * len(chunks) - 1)

        def ffn(name, s):
            c0_, r0_ = COL[name], ROW[name]
            with dve.Fori(0, FG) as i:
                def lo(j):
                    f, c = divmod(j, NC)
                    c0, n = CHUNKS[c]
                    dve.wait_ge(s["hhi"], s.base["hhi"] + i * 6 + (j + 1))
                    dve.tensor_tensor(hidl[:, f, c0:c0 + n], ht[:, j % 2, 0:n], hidh[:, f, c0:c0 + n].bitcast(F32),
                                      ALU.subtract).then_inc(s["hid"], 1)

                for j in range(2 * NC):
                    f, c = divmod(j, NC)
                    n = CHUNKS[c][1]
                    if c < NC - 1:
                        dve.wait_ge(s["up"], s.base["up"] + i * 4 + (2 * f + c + 1))
                    else:
                        dve.wait_ge(unit_done, i * 4 + (SLOTS + c0_ + 2 * f + 2))
                    dve.wait_ge(s["sg"], s.base["sg"] + i * 6 + (j + 1))
                    dve.wait_ge(s["hid"], s.base["hid"] + i * 6 + max(j, 1))
                    dve.tensor_tensor(ht[:, j % 2, 0:n], ps[:, 2 * (j % 2) + 1, 0:n], sg[:, j % 2, 0:n], ALU.mult
                                      ).then_inc(s["prod"], 1)
                    if j >= 1:
                        lo(j - 1)
                lo(2 * NC - 1)
                for j in range(NC * KT):
                    c, d = divmod(j, KT)
                    c0, n = CHUNKS[c]
                    if j < NC * KT - 1:
                        dve.wait_ge(s["down"], s.base["down"] + i * (NC * KT - 1) + (j + 1))
                    else:
                        dve.wait_ge(row_done, i * 2 + (2 + r0_ + 2))
                    dve.scalar_tensor_tensor(out=x[:, d, c0:c0 + n], in0=ps[:, 4 + j % 4, 0:n], scalar=0.5,
                                             in1=x[:, d, c0:c0 + n], op0=ALU.mult, op1=ALU.add
                                             ).then_inc(s["res"], 1)

        def split_input(s):
            for c, (c0, n) in enumerate(CHUNKS):
                for k in range(KT):
                    dve.wait_ge(s["hi"], s.base["hi"] + c * KT + k + 1)
                    dve.tensor_tensor(hl[:, k, c0:c0 + n], mixin[:, c, k, 0:n], hh[:, k, c0:c0 + n].bitcast(F32),
                                      ALU.subtract).then_inc(s["h"], 1)

        def add_proj(name, s):
            split_input(s)
            with dve.Fori(0, 2) as i:
                for w in range(4):
                    for c, (c0, n) in enumerate(CHUNKS):
                        j = w * NC + c
                        if c < NC - 1:
                            dve.wait_ge(s["part"], s.base["part"] + i * 8 + (2 * w + c + 1))
                        else:
                            dve.wait_ge(unit_done, i * 4 + (SLOTS + COL[name] + w + 1))
                        xt = x[:, bass.ds(i * 4 + w, 1), c0:c0 + n]
                        dve.tensor_tensor(xt, ps[:, j % 4:j % 4 + 1, 0:n], xt, ALU.add).then_inc(s["free"], 1)

        dve.sem_inc(S["n1"]["prod"], 2)
        dve.sem_inc(S["n1"]["res"], 4)
        dve.sem_inc(S["n1"]["free"], 4)
        dve.sem_inc(S["n1"]["hid"], 1)
        L = S["load"]
        dve.wait_ge(L["vecs_t"], L.base["vecs_t"] + 1)
        dve.tensor_copy(vecs[:], ps[:, 0, 0:60]).then_inc(L["vecs"], 1)
        dve.tensor_copy(taps[:], ps[:, 1, 0:CT * CONVW].rearrange("p (k t) -> p k t", t=CONVW)
                        ).then_inc(L["vecs"], 1)
        for t in range(QT + 1):
            n = P if t < QT else TSAMP
            for h in range(2):
                j = 2 * t + h
                dve.wait_ge(L["xt"], L.base["xt"] + j + 1)
                dve.tensor_copy(x[:, 4 * h:4 * h + 4, t * P:t * P + n],
                                ps[:, 2 + j % 4, :].rearrange("p (k c) -> p k c", c=P)[:, :, 0:n]
                                ).then_inc(L["xin_free"], 1)
        C = S["conv"]
        dve.wait_ge(C["cct"], 1)
        for k in range(CT):
            dve.tensor_copy(Us[:, k, :, 0:PAD], ps[:, 6 + k // 2, (k % 2) * 240:(k % 2) * 240 + 240]
                            .rearrange("p (b t) -> p b t", t=PAD)).then_inc(C["us"], 1)
        barrier(dve, 1)
        norm(S["n1"], CHUNKS, x, sq, rs, tb, G_FFN1, hh, hl)
        ffn("ffn1", S["n1"])
        barrier(dve, 2)
        dve.memset(U[:, :, 0:PAD], 0.0).then_inc(C["us"], 1)
        norm(S["nm"], CHUNKS, x, sq3, rs3, tb3, G_MIX, h3h, h3l)
        dve.wait_ge(C["us"], CT + 1)
        with dve.Fori(0, CT) as i:
            dve.wait_ge(S["nm"]["free"], i * (2 * NC) + (S["nm"].base["free"] + 4 + 2 * NC))
            k = bass.ds(i, 1)
            dve.tensor_tensor(U[:, k, PAD:PAD + SEQ], U[:, k, PAD:PAD + SEQ], ya[:, k, 0:SEQ], ALU.mult
                              ).then_inc(C["glu"], 1)
            dve.tensor_tensor(Us[:, k, :, PAD:PAD + TS], Us[:, k, :, PAD:PAD + TS],
                              ya[:, k, SEQ:T].rearrange("p o (b t) -> p o b t", t=TS), ALU.mult
                              ).then_inc(C["glu"], 1)
            dve.wait_ge(C["glu"], i * 2 + 2)
            for t in range(CONVW):
                up = U[:, bass.ds(i, 1), t:t + SEQ].rearrange("p o t -> p (o t)")
                us = Us[:, bass.ds(i, 1), :, t:t + TS].rearrange("p o b t -> p (o b) t")
                yp = ya[:, bass.ds(i, 1), 0:SEQ].rearrange("p o t -> p (o t)")
                ys = ya[:, bass.ds(i, 1), SEQ:T].rearrange("p o (b t) -> p (o b) t", t=TS)
                w = taps[:, bass.ds(i, 1), t:t + 1].rearrange("p o t -> p (o t)")
                for q, (src, dst) in enumerate(((up, yp), (us, ys))):
                    if t == 0:
                        dve.tensor_scalar(dst, src, w, vecs[:, bass.ds(i + V_CB, 1)], ALU.mult, ALU.add
                                          ).then_inc(C["tap"], 1)
                    else:
                        dve.wait_ge(C["tap"], i * (2 * CONVW) + (2 * t - 1 + q))
                        dve.scalar_tensor_tensor(out=dst, in0=src, scalar=w, in1=dst, op0=ALU.mult, op1=ALU.add
                                                 ).then_inc(C["tap"], 1)
        barrier(dve, 3)
        M, C = S["mem"], S["conv"]
        for k in range(CT):
            dve.tensor_copy(cct[:, k].rearrange("p a (b t) -> p (a b) t", t=PAD), Us[:, k, :, TS:PAD + TS]
                            ).then_inc(C["ug"], 1)
        for t in range(2):
            for h in range(2):
                dve.wait_ge(M["xt"], M.base["xt"] + 2 * t + h + 1)
                dve.tensor_copy(memT[:, 4 * h:4 * h + 4, t * P:(t + 1) * P],
                                ps[:, 2 * t + h, :].rearrange("p (k c) -> p k c", c=P)).then_inc(M["ev"], 1)
        dve.wait_ge(M["ev"], M.base["ev"] + 4)
        norm(M, [(0, NMEM)], memT, msq, mrs, mtb, G_MEM, mh, ml)
        for c, (c0, n) in enumerate(CHUNKS):
            dve.wait_ge(C["mean"], c + 1)
            dve.tensor_scalar(mu[:, c, 0:n], ps[:, LNB[c], 0:n], 1.0 / WA, None, ALU.mult).then_inc(C["mu"], 1)
            dve.wait_ge(C["mu"], c + 1)
            for k in range(CT):
                dve.tensor_tensor(ya[:, k, c0:c0 + n], ya[:, k, c0:c0 + n], mu[:, c, 0:n], ALU.subtract
                                  ).then_inc(C["xc"], 1)
        dve.wait_ge(C["xc"], CT * NC)
        for c, (c0, n) in enumerate(CHUNKS):
            dve.wait_ge(C["summed"], c + 1)
            dve.tensor_scalar(mrs[:, c, 0:n], ps[:, LNB[c], 0:n], 1.0 / WA, EPS, ALU.mult, ALU.add
                              ).then_inc(C["var"], 1)
        for c, (c0, n) in enumerate(CHUNKS):
            dve.wait_ge(C["std"], c + 1)
            dve.reciprocal(mrs[:, c, 0:n], mrs[:, c, 0:n]).then_inc(C["rstd"], 1)
            dve.wait_ge(C["rstd"], c + 1)
            for k in range(CT):
                dve.scalar_tensor_tensor(out=ya[:, k, c0:c0 + n], in0=ya[:, k, c0:c0 + n],
                                         scalar=vecs[:, V_LG + k:V_LG + k + 1], in1=mrs[:, c, 0:n], op0=ALU.mult,
                                         op1=ALU.mult).then_inc(C["ln"], 1)
        barrier(dve, 4)
        A = S["pa"]
        dve.sem_inc(A["s_free"], WN)
        dve.sem_inc(A["o_free"], 2)
        for p in range(2):
            dve.sem_inc(A[f"ost{p}"], 16)
        with dve.Fori(0, H // 4) as i:
            def mask(n):
                p, h, t = wsteps[n]
                w = P * (t + 1)
                if n % WP == 0:
                    dve.wait_ge(A[f"in{p}"], i * 64 + 64)
                dve.wait_ge(A["s_full"], i * WN + (WN + n + 1))
                b = 2 * (n % 2)
                dve.sem_inc(met, 1)
                dve.tensor_tensor_reduce(out=Sb[:, n % 3, 0:w], in0=ps[:, b:b + 2, :].rearrange("p b n -> p (b n)")
                                         [:, 0:w], in1=pb[:, p, h, SEQ - w:SEQ], scale=1.0, scalar=-3.0e38,
                                         op0=ALU.add, op1=ALU.max, accum_out=stat[:, n % 4, 0:1]
                                         ).then_inc(A["s_free"], 1)
                dve.wait_ge(A["s_free"], i * WN + (WN + n + 1))
                dve.tensor_scalar(stat[:, n % 4, 1:2], stat[:, n % 4, 0:1], -0.125, None, ALU.mult
                                  ).then_inc(A["m"], 1)

            def normalise(n):
                p, h, t = wsteps[n]
                w = P * (t + 1)
                dve.wait_ge(A["e"], i * WN + (n + 1))
                dve.reciprocal(stat[:, n % 4, 3:4], stat[:, n % 4, 2:3]).then_inc(A["r"], 1)
                dve.wait_ge(A["r"], i * WN + (n + 1))
                dve.tensor_scalar(Sb[:, n % 3, 0:w], Sb[:, n % 3, 0:w], stat[:, n % 4, 3:4], None, ALU.mult
                                  ).then_inc(A["p"], 1)

            def output(n):
                p, h, t = wsteps[n]
                if n % WP == 0:
                    dve.wait_ge(A[f"ost{p}"], i * 16 + 16)
                dve.wait_ge(A["o_full"], i * WN + (n + 1))
                dve.tensor_copy(oT[64 * h:64 * h + 64, p, t * P:(t + 1) * P], ps[64 * h:64 * h + 64, 6 + n % 2, 0:P]
                                ).then_inc(A["o_free"], 1)

            mask(0)
            mask(1)
            normalise(0)
            for n in range(WN):
                if n + 2 < WN:
                    mask(n + 2)
                if n + 1 < WN:
                    normalise(n + 1)
                if n >= 1:
                    output(n - 1)
            output(WN - 1)
        barrier(dve, 5)
        B = S["sa"]
        dve.sem_inc(B["t_freed"], 1)
        dve.sem_inc(B["o_free"], 1)
        dve.sem_inc(B["s_free"], 1)
        dve.memset(Qc[:], 0.0).then_inc(B["qz"], 1)
        dve.wait_ge(B["qz"], 1)
        dve.wait_ge(B["bias"], 16)
        dve.wait_ge(B["qk_in"], 32)
        with dve.Fori(0, NB // SQ) as i:
            def queries(q):
                dve.wait_ge(B["s_full"], i * SQ + (q + 2))
                for h in range(H):
                    rows_ = slice(64 * (h % 2), 64 * (h % 2) + 64)
                    dve.tensor_copy(Qc[rows_, :, h // 2, h * TS:(h + 1) * TS],
                                    Qall[rows_, h // 2, bass.ds(i * (SQ * TS) + q * TS, 2 * TS)]
                                    .rearrange("p (q t) -> p q t", t=TS)).then_inc(B["q"], 1)

            def key_evac(q, g):
                j = key_job(q, g)
                w = 4 * (OG if g < 2 * CT else P)
                dve.wait_ge(B["t_full"], i * SJ + (j + 1))
                dve.tensor_copy(Kc[:, g % 4, 0:w], ps[:, 1, 0:w]).then_inc(B["t_freed"], 1)

            def mask(q):
                dve.wait_ge(B["s_full"], i * SQ + (q + 3))
                dve.sem_inc(met, 1)
                off = 0
                for n, w in enumerate((4 * OG, 4 * OG, 4 * P, TS)):
                    ttr = dve.tensor_tensor_reduce(out=Ss[:, off:off + w], in0=ps[0:64, 2 + n, 0:w],
                                                   in1=sbias[:, off:off + w], scale=1.0, scalar=-3.0e38, op0=ALU.add,
                                                   op1=ALU.max, accum_out=sstat[:, n:n + 1])
                    off += w
                ttr.then_inc(B["s_free"], 1)
                dve.wait_ge(B["s_free"], i * SQ + (q + 2))
                dve.tensor_reduce(sstat[:, 4:5], sstat[:, 0:4], AX.X, ALU.max).then_inc(B["mx"], 1)
                dve.wait_ge(B["mx"], i * SQ + (q + 1))
                dve.tensor_scalar(sstat[:, 5:6], sstat[:, 4:5], -0.125, None, ALU.mult).then_inc(B["m"], 1)

            def normalise(q):
                dve.wait_ge(B["e"], i * SQ + (q + 1))
                dve.reciprocal(sstat[:, 7:8], sstat[:, 6:7]).then_inc(B["r"], 1)
                dve.wait_ge(B["r"], i * SQ + (q + 1))
                dve.tensor_scalar(Ss[:], Ss[:], sstat[:, 7:8], None, ALU.mult).then_inc(B["p"], 1)

            def output(q):
                dve.wait_ge(B["ot"], i * SQ + (q + 1))
                for hf in range(2):
                    rows_ = slice(64 * hf, 64 * hf + 64)
                    src = ps[rows_, 7, 0:CT * 80].rearrange("p (k c) -> p k c", c=80)[:, :, hf * TS:(hf + 1) * TS]
                    dve.tensor_copy(oS[rows_, :, bass.ds(i * SQ + q, 1), :].rearrange("p k o t -> p k (o t)"), src
                                    ).then_inc(B["o_free"], 1)

            def prob_evac(q):
                dve.wait_ge(B["t_full"], i * SJ + (prob_job(q) + 2))
                dve.tensor_copy(PTs[:, 8:12, :], ps[:, 1, 0:256].rearrange("p (k c) -> p k c", c=64))
                dve.tensor_copy(PTs[0:TS, 12, :], ps[0:TS, 1, 256:320]).then_inc(B["t_freed"], 1)

            queries(0)
            for q in range(SQ):
                for g in range(1, KG, 2):
                    key_evac(q, g)
                    if g == 1 and q >= 1:
                        mask(q - 1)
                        if q == 2:
                            queries(2)
                        normalise(q - 1)
                    if g == 7 and q >= 2:
                        output(q - 2)
                if q >= 1:
                    prob_evac(q - 1)
            mask(SQ - 1)
            normalise(SQ - 1)
            prob_evac(SQ - 1)
            output(SQ - 2)
            output(SQ - 1)
        barrier(dve, 6)
        add_proj("w_out", S["so"])
        barrier(dve, 7)
        norm(S["nx"], CHUNKS, x, sq, rs, tb, G_X, hh, hl)
        barrier(dve, 8)
        X = S["xa"]
        dve.sem_inc(X["o_free"], 2)
        for p in range(2):
            dve.sem_inc(X[f"ost{p}"], 16)
        with dve.Fori(0, HX // 2) as i:
            def xmax(n):
                dve.wait_ge(X["s_full"], i * XN + (n + 1))
                dve.tensor_reduce(xstat[:, n % 4, 0:1], ps[:, n % 2, 0:NMEM], AX.X, ALU.max).then_inc(X["mx"], 1)
                dve.wait_ge(X["mx"], i * XN + (n + 1))
                dve.tensor_scalar(xstat[:, n % 4, 1:2], xstat[:, n % 4, 0:1], -(HDX ** -0.5), None, ALU.mult
                                  ).then_inc(X["m"], 1)

            def xnorm(n):
                dve.wait_ge(X["e"], i * XN + (n + 3))
                dve.reciprocal(xstat[:, n % 4, 3:4], xstat[:, n % 4, 2:3]).then_inc(X["r"], 1)
                dve.wait_ge(X["r"], i * XN + (n + 1))
                dve.tensor_scalar(Xb[:, n % 3, :], Xb[:, n % 3, :], xstat[:, n % 4, 3:4], None, ALU.mult
                                  ).then_inc(X["p"], 1)

            def xout(n):
                p, t = xsteps[n]
                if t == 0:
                    dve.wait_ge(X[f"ost{p}"], i * 16 + 16)
                dve.wait_ge(X["o_full"], i * XN + (XN + n + 1))
                dve.tensor_copy(xo[:, p, :, t * P:(t + 1) * P], ps[:, 4 + n % 2, 0:2 * P]
                                .rearrange("p (k c) -> p k c", c=P)).then_inc(X["o_free"], 1)

            xmax(0)
            xmax(1)
            xnorm(0)
            for n in range(XN):
                if n + 2 < XN:
                    xmax(n + 2)
                if n + 1 < XN:
                    xnorm(n + 1)
                if n >= 1:
                    xout(n - 1)
            xout(XN - 1)
        Y = S["xs"]
        dve.sem_inc(Y["t_freed"], 1)
        dve.sem_inc(Y["oe"], 1)
        dve.memset(cqc[:], 0.0).then_inc(Y["qz"], 1)
        dve.wait_ge(Y["qz"], 1)
        dve.wait_ge(Y["q_in"], 16)
        with dve.Fori(0, 2) as i:
            dve.wait_ge(Y["s_full"], i * 4 + 2)
            for h in range(HX):
                dve.tensor_copy(cqc[:, :, 2 * h:2 * h + 2, h * TS:(h + 1) * TS],
                                cq[:, 2 * h:2 * h + 2, bass.ds(i * 32, 32)].rearrange("p k (b t) -> p b k t", b=4)
                                ).then_inc(Y["qc"], 1)
            for b in range(4):
                for m in (1, 3):
                    dve.wait_ge(Y["t_full"], i * 16 + (b * 4 + m + 9))
                    dve.tensor_copy(cKT[:, b % 2, 2 * m:2 * m + 2, :], ps[:, 1, :].rearrange("p (k c) -> p k c", k=2)
                                    ).then_inc(Y["t_freed"], 1)
            dve.wait_ge(Y["s_full"], i * 4 + 6)
            dve.tensor_reduce(cstat[:, 0:1], ps[:, 2, 0:NMEM], AX.X, ALU.max).then_inc(Y["mx"], 1)
            dve.wait_ge(Y["mx"], i + 1)
            dve.tensor_scalar(cstat[:, 1:2], cstat[:, 0:1], -(HDX ** -0.5), None, ALU.mult).then_inc(Y["m"], 1)
            dve.wait_ge(Y["e"], i + 2)
            dve.reciprocal(cstat[:, 3:4], cstat[:, 2:3]).then_inc(Y["r"], 1)
            dve.wait_ge(Y["r"], i + 1)
            dve.tensor_scalar(cS[:], cS[:], cstat[:, 3:4], None, ALU.mult).then_inc(Y["p"], 1)
            dve.wait_ge(Y["o_full"], i + 2)
            dve.tensor_copy(cO[:, 512:D], ps[:, 5, :]).then_inc(Y["ov"], 1)
            dve.wait_ge(Y["ot"], i + 1)
            for h in range(HX):
                src = ps[:, 6 + h // 2, (h % 2) * 2 * P:(h % 2 + 1) * 2 * P].rearrange("p (k b c) -> p k b c", k=2, b=4)
                dve.tensor_copy(co[:, 2 * h:2 * h + 2, bass.ds(i * 4, 4), :], src[:, :, :, h * TS:(h + 1) * TS]
                                ).then_inc(Y["oe"], 1)
        barrier(dve, 9)
        add_proj("w_co", S["sc"])
        barrier(dve, 10)
        norm(S["n2"], CHUNKS, x, sq, rs, tb, G_FFN2, hh, hl)
        ffn("ffn2", S["n2"])
        barrier(dve, 11)
        F = S["fin"]
        norm(F, CHUNKS, x, sq, rs, tb, G_FIN, hh, hl, split=False)

    ctx.close()


_INS = ["x_prompt", "x_sample", "mem_prompt", "cache_win_k", "cache_win_v", "cache_conv", "cache_mem_k",
        "cache_mem_v", "ffn1_norm", "ffn1_gate", "ffn1_up", "ffn1_down", "mix_norm", "w_in", "conv_w", "conv_b",
        "conv_ln_g", "conv_ln_b", "w_out", "xattn_norm", "mem_norm", "w_cq", "w_ck", "w_cv", "w_co", "ffn2_norm",
        "ffn2_gate", "ffn2_up", "ffn2_down", "final_norm"]
_OUTS = [("y_prompt", (1, SEQ, D)), ("y_sample", (NB, TS, D)),
         ("new_win_k_prompt", (1, 1, SEQ, H, HD)), ("new_win_v_prompt", (1, 1, SEQ, H, HD)),
         ("new_conv_prompt", (1, 1, PAD, WA)),
         ("new_mem_k_prompt", (1, 1, NMEM, HX, HDX)), ("new_mem_v_prompt", (1, 1, NMEM, HX, HDX)),
         ("new_win_k_sample", (1, NB, TS, H, HD)), ("new_win_v_sample", (1, NB, TS, H, HD)),
         ("new_conv_sample", (1, NB, PAD, WA))]


def kernel(**inputs):
    import concourse.bacc as _bacc
    from concourse.bass_utils import run_bass_kernel_spmd as _run

    nc = _bacc.Bacc("TRN2", target_bir_lowering=False, num_devices=1)
    given = {n: np.ascontiguousarray(inputs[n]) for n in _INS}
    given["prompt_bias"] = prompt_bias()
    given["sample_bias"] = sample_bias()
    arrays, ins = {}, {}
    for name, a in given.items():
        arrays[f"in_{name}"] = a
        ins[name] = nc.dram_tensor(f"in_{name}", a.shape, mybir.dt.from_np(a.dtype), kind="ExternalInput").ap()
    outs = {name: nc.dram_tensor(f"out_{name}", shape, F32, kind="ExternalOutput").ap() for name, shape in _OUTS}
    decoder_layer(nc, ins, outs)
    r = _run(nc, [arrays], core_ids=[0])
    return tuple(r.results[0][f"out_{name}"] for name, _ in _OUTS)
```
